# Optimizing a Trainium2 kernel written in Bass

```python
import jax, jax.numpy as jnp
from jax import lax
import numpy as np

D_MODEL = 1024
BATCH = 1
SEQ = 256
DEPTH = 2

GRID_W = 64
CTX_LEN = 256

ATTN_HEAD_DIM = 64
ATTN_HEADS = 8
ATTN_KV_HEADS = 2
ATTN_Q_PER_KV = ATTN_HEADS // ATTN_KV_HEADS
ATTN_WIDTH = ATTN_HEADS * ATTN_HEAD_DIM
ATTN_KV_WIDTH = ATTN_KV_HEADS * ATTN_HEAD_DIM
Q_BLOCK = 128
ROPE_THETA = 10000.0
ROPE_AXIS_DIM = ATTN_HEAD_DIM // 2

GLA_HEADS = 4
GLA_DK = 64
GLA_DV = 128
GLA_K_WIDTH = GLA_HEADS * GLA_DK
GLA_V_WIDTH = GLA_HEADS * GLA_DV
GLA_GATE_RANK = 16
GLA_GATE_TEMP = 16.0
GLA_CHUNK = 64

SGU_GROUPS = 4
SGU_CHUNK = 128
SGU_WIDTH = 512
SGU_GROUP_DIM = SGU_WIDTH // SGU_GROUPS

DEEPNORM_ALPHA = (2 * DEPTH) ** 0.25
DEEPNORM_BETA = (8 * DEPTH) ** -0.25
EPS = 1e-6

SPLIT_SIZES = (
    ATTN_WIDTH, ATTN_KV_WIDTH, ATTN_KV_WIDTH, ATTN_WIDTH,
    GLA_K_WIDTH, GLA_K_WIDTH, GLA_V_WIDTH, GLA_GATE_RANK, GLA_GATE_RANK,
    GLA_V_WIDTH,
    SGU_WIDTH, SGU_WIDTH, SGU_WIDTH,
    D_MODEL, D_MODEL, D_MODEL,
)
PROJ_WIDTH = sum(SPLIT_SIZES)


def _split_points():
    pts, acc = [], 0
    for s in SPLIT_SIZES[:-1]:
        acc += s
        pts.append(acc)
    return pts

def layer_norm(x, g, b):
    xf = x.astype(jnp.float32)
    mu = jnp.mean(xf, axis=-1, keepdims=True)
    var = jnp.mean(jnp.square(xf - mu), axis=-1, keepdims=True)
    return ((xf - mu) * lax.rsqrt(var + EPS) * g + b).astype(x.dtype)

def rms_norm(x, g):
    xf = x.astype(jnp.float32)
    y = xf * lax.rsqrt(jnp.mean(jnp.square(xf), axis=-1, keepdims=True) + EPS)
    return (y * g).astype(x.dtype)

def axial_rope_angles(rows):
    row = jnp.repeat(jnp.arange(rows, dtype=jnp.float32), GRID_W)
    col = jnp.tile(jnp.arange(GRID_W, dtype=jnp.float32), rows)
    freqs = ROPE_THETA ** (-jnp.arange(0, ROPE_AXIS_DIM, 2, dtype=jnp.float32) / ROPE_AXIS_DIM)
    return row[:, None] * freqs, col[:, None] * freqs

def rope_1d(x, ang):
    m = ang.shape[-1]
    cos = jnp.cos(ang)[None, :, None, :]
    sin = jnp.sin(ang)[None, :, None, :]
    x1, x2 = x[..., :m], x[..., m:]
    return jnp.concatenate([x1 * cos - x2 * sin, x1 * sin + x2 * cos], axis=-1)

def apply_axial_rope(x, ang_r, ang_c):
    xf = x.astype(jnp.float32)
    out = jnp.concatenate([rope_1d(xf[..., :ROPE_AXIS_DIM], ang_r),
                           rope_1d(xf[..., ROPE_AXIS_DIM:], ang_c)], axis=-1)
    return out.astype(x.dtype)

def gqa_project(pq, pk, pv, q_norm, k_norm):
    B, N, _ = pq.shape
    q = rms_norm(pq.reshape(B, N, ATTN_HEADS, ATTN_HEAD_DIM), q_norm)
    k = rms_norm(pk.reshape(B, N, ATTN_KV_HEADS, ATTN_HEAD_DIM), k_norm)
    v = pv.reshape(B, N, ATTN_KV_HEADS, ATTN_HEAD_DIM)
    return q, k, v

def attend(q, k, v):
    s = jnp.einsum('btgrd,blgd->bgrtl', q, k, preferred_element_type=jnp.float32) * (ATTN_HEAD_DIM ** -0.5)
    p = jax.nn.softmax(s, axis=-1)
    return jnp.einsum('bgrtl,blgd->btgrd', p.astype(v.dtype), v)

def blocked_attention(q, k, v):
    B, N = q.shape[:2]
    nb = N // Q_BLOCK
    qb = q.reshape(B, nb, Q_BLOCK, ATTN_KV_HEADS, ATTN_Q_PER_KV, ATTN_HEAD_DIM)
    qb = jnp.moveaxis(qb, 1, 0)
    ob = lax.map(lambda qi: attend(qi, k, v), qb)
    return jnp.moveaxis(ob, 0, 1).reshape(B, N, ATTN_WIDTH)

def gla_scan(q, k, v, g, s0):
    B, H, N, dk = q.shape
    dv = v.shape[-1]
    nc = N // GLA_CHUNK
    mask = jnp.tril(jnp.ones((GLA_CHUNK, GLA_CHUNK), dtype=bool))

    def chunks(t):
        return jnp.moveaxis(t.reshape(B, H, nc, GLA_CHUNK, t.shape[-1]), 2, 0)

    def step(s, inp):
        qc, kc, vc, gc = inp
        b = jnp.cumsum(gc, axis=2)
        b_last = b[:, :, -1:, :]
        inter = jnp.einsum('bhtd,bhde->bhte', qc * jnp.exp(b), s)
        rel = jnp.where(mask[:, :, None], b[:, :, :, None, :] - b[:, :, None, :, :], -jnp.inf)
        att = jnp.einsum('bhtd,bhsd,bhtsd->bhts', qc, kc, jnp.exp(rel))
        o = inter + jnp.einsum('bhts,bhse->bhte', att, vc)
        s_new = jnp.exp(b_last[:, :, 0, :])[..., None] * s + \
            jnp.einsum('bhsd,bhse->bhde', kc * jnp.exp(b_last - b), vc)
        return s_new, o

    s_fin, o = lax.scan(step, s0, (chunks(q), chunks(k), chunks(v), chunks(g)))
    return jnp.moveaxis(o, 0, 2).reshape(B, H, N, dv), s_fin

def gla_heads(pq, pk, pv, paf, pab, a2_f, ab_f, a2_b, ab_b):
    B, N, _ = pq.shape

    def heads(t, d):
        return t.reshape(B, N, GLA_HEADS, d).transpose(0, 2, 1, 3).astype(jnp.float32)

    def log_decay(pa, a2, ab):
        z = (pa @ a2 + ab).astype(jnp.float32)
        return heads(jax.nn.log_sigmoid(z) / GLA_GATE_TEMP, GLA_DK)

    q = heads(pq, GLA_DK) * (GLA_DK ** -0.5)
    k = heads(pk, GLA_DK)
    v = heads(pv, GLA_DV)
    return q, k, v, log_decay(paf, a2_f, ab_f), log_decay(pab, a2_b, ab_b)

def gla_finish(o, o_norm, dtype):
    B, H, N, dv = o.shape
    o = rms_norm(o.transpose(0, 2, 1, 3), o_norm)
    return o.reshape(B, N, H * dv).astype(dtype)

def sgu(pu, pv, ln_g, ln_b, w_s, b_s):
    B, N, _ = pu.shape
    nch = N // SGU_CHUNK
    vn = layer_norm(pv, ln_g, ln_b).reshape(B, nch, SGU_CHUNK, SGU_GROUPS, SGU_GROUP_DIM)
    mixed = jnp.einsum('gts,bnsgc->bntgc', w_s, vn) + b_s.T[None, None, :, :, None]
    return pu * mixed.reshape(B, N, SGU_WIDTH)

def trunk_layer(x, ctx, c, c_ctx, p, ang_r, ang_c, need_ctx):
    B = x.shape[0]
    shift, scale, gate = jnp.split(jax.nn.silu(c) @ p['w_ada'] + p['b_ada'], 3, axis=-1)
    shift_c, scale_c, gate_c = jnp.split(jax.nn.silu(c_ctx) @ p['w_ada'] + p['b_ada'], 3, axis=-1)
    h = x * (1.0 + scale[:, None, :]) + shift[:, None, :]
    hc = ctx * (1.0 + scale_c) + shift_c

    pts = _split_points()
    (a_q, a_k, a_v, a_g, g_q, g_k, g_v, g_af, g_ab, g_g,
     s_u, s_v, s_g, m_a, m_g, m_s) = jnp.split(h @ p['w_in'], pts, axis=-1)
    (ca_q, ca_k, ca_v, ca_g, cg_q, cg_k, cg_v, cg_af, cg_ab, cg_g,
     cs_u, cs_v, cs_g, cm_a, cm_g, cm_s) = jnp.split(hc @ p['w_in'], pts, axis=-1)

    ql, kl, vl = gqa_project(a_q, a_k, a_v, p['q_norm'], p['k_norm'])
    ql = apply_axial_rope(ql, ang_r, ang_c)
    kl = apply_axial_rope(kl, ang_r, ang_c)
    qc, kc, vc = gqa_project(ca_q, ca_k, ca_v, p['q_norm'], p['k_norm'])
    k_all = jnp.concatenate([kc, kl], axis=1)
    v_all = jnp.concatenate([vc, vl], axis=1)
    y_attn = blocked_attention(ql, k_all, v_all) * jax.nn.silu(a_g)

    qlg, klg, vlg, gfl, gbl = gla_heads(g_q, g_k, g_v, g_af, g_ab, p['a2_f'], p['ab_f'], p['a2_b'], p['ab_b'])
    qcg, kcg, vcg, gfc, gbc = gla_heads(cg_q, cg_k, cg_v, cg_af, cg_ab, p['a2_f'], p['ab_f'], p['a2_b'], p['ab_b'])
    zeros = jnp.zeros((B, GLA_HEADS, GLA_DK, GLA_DV), jnp.float32)
    flip = lambda t: jnp.flip(t, axis=2)
    oc_f, s_f = gla_scan(qcg, kcg, vcg, gfc, zeros)
    oc_b, s_b = gla_scan(flip(qcg), flip(kcg), flip(vcg), flip(gbc), zeros)
    ol_f, _ = gla_scan(qlg, klg, vlg, gfl, s_f)
    ol_b, _ = gla_scan(flip(qlg), flip(klg), flip(vlg), flip(gbl), s_b)
    y_gla = gla_finish(ol_f + flip(ol_b), p['gla_o_norm'], x.dtype) * jax.nn.silu(g_g)

    y_sgu = sgu(s_u, s_v, p['sgu_ln_g'], p['sgu_ln_b'], p['sgu_w'], p['sgu_b']) * jax.nn.silu(s_g)

    def merge(ya, yg, ys, ga, gg, gs):
        m = (jax.nn.sigmoid(ga) * (ya @ p['w_br_attn'])
             + jax.nn.sigmoid(gg) * (yg @ p['w_br_gla'])
             + jax.nn.sigmoid(gs) * (ys @ p['w_br_sgu']))
        return m @ p['w_out']

    out = merge(y_attn, y_gla, y_sgu, m_a, m_g, m_s)
    x_new = layer_norm(DEEPNORM_ALPHA * x + gate[:, None, :] * out, p['post_g'], p['post_b'])

    if not need_ctx:
        return x_new, ctx

    L = ctx.shape[1]
    yc_attn = attend(qc.reshape(B, L, ATTN_KV_HEADS, ATTN_Q_PER_KV, ATTN_HEAD_DIM), kc, vc)
    yc_attn = yc_attn.reshape(B, L, ATTN_WIDTH) * jax.nn.silu(ca_g)
    yc_gla = gla_finish(oc_f + flip(oc_b), p['gla_o_norm'], ctx.dtype) * jax.nn.silu(cg_g)
    yc_sgu = sgu(cs_u, cs_v, p['sgu_ln_g'], p['sgu_ln_b'], p['sgu_w'], p['sgu_b']) * jax.nn.silu(cs_g)
    out_c = merge(yc_attn, yc_gla, yc_sgu, cm_a, cm_g, cm_s)
    ctx_new = layer_norm(DEEPNORM_ALPHA * ctx + gate_c * out_c, p['post_g'], p['post_b'])
    return x_new, ctx_new

def first_inputs(seed: int = 0) -> dict:
    key = jax.random.key(seed)
    ks = iter(jax.random.split(key, 32))

    def nrm(shape, s):
        return jax.random.normal(next(ks), shape, jnp.float32) * s

    L, D = DEPTH, D_MODEL
    return {
        "x": nrm((BATCH, SEQ, D), 1.0),
        "c": nrm((BATCH, D), 1.0),
        "ctx": nrm((BATCH, CTX_LEN, D), 1.0),
        "c_ctx": nrm((D,), 1.0),
        "w_ada": nrm((L, D, 3 * D), 0.5 * D ** -0.5),
        "b_ada": nrm((L, 3 * D), 0.02),
        "w_in": nrm((L, D, PROJ_WIDTH), D ** -0.5),
        "attn_q_norm": 1.0 + nrm((L, ATTN_HEAD_DIM), 0.02),
        "attn_k_norm": 1.0 + nrm((L, ATTN_HEAD_DIM), 0.02),
        "gla_a2_f": nrm((L, GLA_GATE_RANK, GLA_K_WIDTH), GLA_GATE_RANK ** -0.5),
        "gla_ab_f": nrm((L, GLA_K_WIDTH), 0.1),
        "gla_a2_b": nrm((L, GLA_GATE_RANK, GLA_K_WIDTH), GLA_GATE_RANK ** -0.5),
        "gla_ab_b": nrm((L, GLA_K_WIDTH), 0.1),
        "gla_o_norm": 1.0 + nrm((L, GLA_DV), 0.02),
        "sgu_ln_g": 1.0 + nrm((L, SGU_WIDTH), 0.02),
        "sgu_ln_b": nrm((L, SGU_WIDTH), 0.02),
        "sgu_w": nrm((L, SGU_GROUPS, SGU_CHUNK, SGU_CHUNK), SGU_CHUNK ** -0.5),
        "sgu_b": 1.0 + nrm((L, SGU_GROUPS, SGU_CHUNK), 0.02),
        "w_br_attn": nrm((L, ATTN_WIDTH, D), ATTN_WIDTH ** -0.5 * DEEPNORM_BETA),
        "w_br_gla": nrm((L, GLA_V_WIDTH, D), GLA_V_WIDTH ** -0.5 * DEEPNORM_BETA),
        "w_br_sgu": nrm((L, SGU_WIDTH, D), SGU_WIDTH ** -0.5 * DEEPNORM_BETA),
        "w_out": nrm((L, D, D), D ** -0.5 * DEEPNORM_BETA),
        "post_ln_g": 1.0 + nrm((L, D), 0.02),
        "post_ln_b": nrm((L, D), 0.02),
    }

def first_block(x, c, ctx, c_ctx, w_ada, b_ada, w_in, attn_q_norm, attn_k_norm,
              gla_a2_f, gla_ab_f, gla_a2_b, gla_ab_b, gla_o_norm,
              sgu_ln_g, sgu_ln_b, sgu_w, sgu_b,
              w_br_attn, w_br_gla, w_br_sgu, w_out, post_ln_g, post_ln_b):
    n_lat = x.shape[1]
    rows = n_lat // GRID_W
    ang_r, ang_c = axial_rope_angles(rows)
    for i in range(DEPTH):
        p = {
            'w_ada': w_ada[i], 'b_ada': b_ada[i], 'w_in': w_in[i],
            'q_norm': attn_q_norm[i], 'k_norm': attn_k_norm[i],
            'a2_f': gla_a2_f[i], 'ab_f': gla_ab_f[i], 'a2_b': gla_a2_b[i], 'ab_b': gla_ab_b[i],
            'gla_o_norm': gla_o_norm[i],
            'sgu_ln_g': sgu_ln_g[i], 'sgu_ln_b': sgu_ln_b[i], 'sgu_w': sgu_w[i], 'sgu_b': sgu_b[i],
            'w_br_attn': w_br_attn[i], 'w_br_gla': w_br_gla[i], 'w_br_sgu': w_br_sgu[i],
            'w_out': w_out[i], 'post_g': post_ln_g[i], 'post_b': post_ln_b[i],
        }
        x, ctx = trunk_layer(x, ctx, c, c_ctx, p, ang_r, ang_c, need_ctx=(i < DEPTH - 1))
    return x


DN_HEADS = 4
DN_DK = 128
DN_DV = 128
DN_QK = DN_HEADS * DN_DK
DN_V = DN_HEADS * DN_DV
DN_CONV = 5
CHUNK = 64
N_DIR = 2
CF_WIDTH = 512
CF_CONV = 31
N_BRANCH = 2

SIZES = (2 * DN_QK + DN_V,
         DN_V,
         N_DIR * DN_HEADS,
         N_DIR * DN_HEADS,
         CF_WIDTH,
         CF_WIDTH,
         CF_WIDTH,
         N_BRANCH * D_MODEL)
D_IN = sum(SIZES)


def rms_norm_2(x, w):
    xf = x.astype(jnp.float32)
    y = xf * lax.rsqrt(jnp.mean(xf * xf, axis=-1, keepdims=True) + EPS)
    return (y * w.astype(jnp.float32)).astype(x.dtype)

def layer_norm_2(x, w, b):
    xf = x.astype(jnp.float32)
    mu = jnp.mean(xf, axis=-1, keepdims=True)
    xc = xf - mu
    y = xc * lax.rsqrt(jnp.mean(xc * xc, axis=-1, keepdims=True) + EPS)
    return (y * w.astype(jnp.float32) + b.astype(jnp.float32)).astype(x.dtype)

def l2_normalize(t):
    return t * lax.rsqrt(jnp.sum(t * t, axis=-1, keepdims=True) + EPS)

def depthwise_conv_centred(u, w):
    k = w.shape[0]
    return lax.conv_general_dilated(
        u, w[:, None, :].astype(u.dtype), window_strides=(1,),
        padding=[(k // 2, k // 2)], dimension_numbers=('NWC', 'WIO', 'NWC'),
        feature_group_count=u.shape[-1])

def gated_delta_chunked(q, k, v, g, beta):
    bsz, seq, nh, dk = q.shape
    dv = v.shape[-1]
    n = seq // CHUNK
    q = q.reshape(bsz, n, CHUNK, nh, dk).transpose(0, 3, 1, 2, 4) * (dk ** -0.5)
    k = k.reshape(bsz, n, CHUNK, nh, dk).transpose(0, 3, 1, 2, 4)
    v = v.reshape(bsz, n, CHUNK, nh, dv).transpose(0, 3, 1, 2, 4)
    g = jnp.cumsum(g.reshape(bsz, n, CHUNK, nh).transpose(0, 3, 1, 2), axis=-1)
    beta = beta.reshape(bsz, n, CHUNK, nh).transpose(0, 3, 1, 2)

    incl = jnp.tril(jnp.ones((CHUNK, CHUNK), dtype=bool))
    strict = jnp.tril(jnp.ones((CHUNK, CHUNK), dtype=bool), k=-1)
    diff = g[..., :, None] - g[..., None, :]
    decay = jnp.where(incl, jnp.exp(jnp.where(incl, diff, 0.0)), 0.0)

    k_beta = k * beta[..., None]
    lmat = jnp.where(strict, jnp.einsum('bhncd,bhnsd->bhncs', k_beta, k) * decay, 0.0)
    eye = jnp.eye(CHUNK, dtype=jnp.float32)
    rhs = jnp.concatenate([v * beta[..., None], k_beta * jnp.exp(g)[..., None]], axis=-1)
    sol = lax.linalg.triangular_solve(eye + lmat, rhs, left_side=True, lower=True,
                                      unit_diagonal=True)
    value, k_cum = sol[..., :dv], sol[..., dv:]

    attn = jnp.einsum('bhncd,bhnsd->bhncs', q, k) * decay
    q_dec = q * jnp.exp(g)[..., None]
    g_last = g[..., -1]
    k_dec = k * jnp.exp(g_last[..., None] - g)[..., None]

    xs = (jnp.moveaxis(value, 2, 0), jnp.moveaxis(k_cum, 2, 0), jnp.moveaxis(attn, 2, 0),
          jnp.moveaxis(q_dec, 2, 0), jnp.moveaxis(k_dec, 2, 0),
          jnp.moveaxis(jnp.exp(g_last), 2, 0))

    def step(state, inp):
        val_n, kc_n, a_n, qd_n, kd_n, dl_n = inp
        v_new = val_n - jnp.einsum('bhcd,bhde->bhce', kc_n, state)
        o_n = jnp.einsum('bhcd,bhde->bhce', qd_n, state) + jnp.einsum('bhcs,bhse->bhce', a_n, v_new)
        state = state * dl_n[..., None, None] + jnp.einsum('bhcd,bhce->bhde', kd_n, v_new)
        return state, o_n

    s0 = jnp.zeros((bsz, nh, dk, dv), dtype=jnp.float32)
    _, o = lax.scan(step, s0, xs)
    return o.transpose(1, 0, 3, 2, 4).reshape(bsz, seq, nh, dv)

def hybrid_mixer(h, w_in, qkv_conv_w, a_log, dt_bias, dn_norm_w, w_dn_out,
                 cf_conv_w, cf_conv_b, cf_ln_w, cf_ln_b, w_cf_out, gate_b, w_out):
    bsz, seq, _ = h.shape
    pts = []
    acc = 0
    for s in SIZES[:-1]:
        acc += s
        pts.append(acc)
    proj = h @ w_in
    qkv, z_a, a_lg, b_lg, cf_val, cf_glu, z_b, gate_lg = jnp.split(proj, pts, axis=-1)

    qkv = jax.nn.silu(depthwise_conv_centred(qkv, qkv_conv_w))
    q = qkv[..., :DN_QK].astype(jnp.float32).reshape(bsz, seq, DN_HEADS, DN_DK)
    k = qkv[..., DN_QK:2 * DN_QK].astype(jnp.float32).reshape(bsz, seq, DN_HEADS, DN_DK)
    v = qkv[..., 2 * DN_QK:].astype(jnp.float32).reshape(bsz, seq, DN_HEADS, DN_DV)
    q = l2_normalize(q)
    k = l2_normalize(k)
    a_lg = a_lg.astype(jnp.float32).reshape(bsz, seq, N_DIR, DN_HEADS)
    g = -jnp.exp(a_log.astype(jnp.float32)) * jax.nn.softplus(a_lg + dt_bias.astype(jnp.float32))
    beta = jax.nn.sigmoid(b_lg.astype(jnp.float32).reshape(bsz, seq, N_DIR, DN_HEADS))
    o_fwd = gated_delta_chunked(q, k, v, g[:, :, 0], beta[:, :, 0])
    flip = lambda t: jnp.flip(t, axis=1)
    o_bwd = flip(gated_delta_chunked(flip(q), flip(k), flip(v), flip(g[:, :, 1]), flip(beta[:, :, 1])))
    o = o_fwd + o_bwd
    o = o * lax.rsqrt(jnp.mean(o * o, axis=-1, keepdims=True) + EPS) * dn_norm_w.astype(jnp.float32)
    o = o * jax.nn.silu(z_a.astype(jnp.float32).reshape(bsz, seq, DN_HEADS, DN_DV))
    y_a = o.reshape(bsz, seq, DN_V).astype(h.dtype) @ w_dn_out

    u = cf_val * jax.nn.sigmoid(cf_glu)
    u = depthwise_conv_centred(u, cf_conv_w) + cf_conv_b
    u = jax.nn.silu(layer_norm_2(u, cf_ln_w, cf_ln_b))
    y_b = (u * jax.nn.silu(z_b)) @ w_cf_out

    gate = jax.nn.sigmoid(gate_lg + gate_b).reshape(bsz, seq, N_BRANCH, D_MODEL)
    y = gate[:, :, 0] * y_a + gate[:, :, 1] * y_b
    return y @ w_out

def second_inputs(seed: int = 0) -> dict:
    key = jax.random.key(seed)
    ks = jax.random.split(key, 17)
    nrm = jax.random.normal
    x = nrm(ks[0], (BATCH, SEQ, D_MODEL), jnp.float32)
    norm_w = 1.0 + 0.05 * nrm(ks[1], (DEPTH, D_MODEL), jnp.float32)
    w_in = nrm(ks[2], (DEPTH, D_MODEL, D_IN), jnp.float32) * D_MODEL ** -0.5
    qkv_conv_w = nrm(ks[3], (DEPTH, DN_CONV, 2 * DN_QK + DN_V), jnp.float32) * DN_CONV ** -0.5
    a_log = jnp.log(jax.random.uniform(ks[4], (DEPTH, N_DIR, DN_HEADS), jnp.float32, 1.0, 16.0))
    dt = jnp.exp(jax.random.uniform(ks[5], (DEPTH, N_DIR, DN_HEADS), jnp.float32,
                                    float(np.log(1e-3)), float(np.log(1e-1))))
    dt_bias = dt + jnp.log(-jnp.expm1(-dt))
    dn_norm_w = 1.0 + 0.05 * nrm(ks[6], (DEPTH, DN_DV), jnp.float32)
    w_dn_out = nrm(ks[7], (DEPTH, DN_V, D_MODEL), jnp.float32) * DN_V ** -0.5
    cf_conv_w = nrm(ks[8], (DEPTH, CF_CONV, CF_WIDTH), jnp.float32) * CF_CONV ** -0.5
    cf_conv_b = 0.02 * nrm(ks[9], (DEPTH, CF_WIDTH), jnp.float32)
    cf_ln_w = 1.0 + 0.05 * nrm(ks[10], (DEPTH, CF_WIDTH), jnp.float32)
    cf_ln_b = 0.02 * nrm(ks[11], (DEPTH, CF_WIDTH), jnp.float32)
    w_cf_out = nrm(ks[12], (DEPTH, CF_WIDTH, D_MODEL), jnp.float32) * CF_WIDTH ** -0.5
    gate_b = 0.02 * nrm(ks[13], (DEPTH, N_BRANCH * D_MODEL), jnp.float32)
    w_out = nrm(ks[14], (DEPTH, D_MODEL, D_MODEL), jnp.float32) * D_MODEL ** -0.5
    final_norm_w = 1.0 + 0.05 * nrm(ks[15], (D_MODEL,), jnp.float32)
    return {'x': x, 'norm_w': norm_w, 'w_in': w_in, 'qkv_conv_w': qkv_conv_w,
            'a_log': a_log, 'dt_bias': dt_bias, 'dn_norm_w': dn_norm_w, 'w_dn_out': w_dn_out,
            'cf_conv_w': cf_conv_w, 'cf_conv_b': cf_conv_b, 'cf_ln_w': cf_ln_w, 'cf_ln_b': cf_ln_b,
            'w_cf_out': w_cf_out, 'gate_b': gate_b, 'w_out': w_out, 'final_norm_w': final_norm_w}

def second_block(x, norm_w, w_in, qkv_conv_w, a_log, dt_bias, dn_norm_w, w_dn_out,
              cf_conv_w, cf_conv_b, cf_ln_w, cf_ln_b, w_cf_out, gate_b, w_out, final_norm_w):
    for l in range(DEPTH):
        h = rms_norm_2(x, norm_w[l])
        x = x + hybrid_mixer(h, w_in[l], qkv_conv_w[l], a_log[l], dt_bias[l], dn_norm_w[l],
                             w_dn_out[l], cf_conv_w[l], cf_conv_b[l], cf_ln_w[l], cf_ln_b[l],
                             w_cf_out[l], gate_b[l], w_out[l])
    return rms_norm_2(x, final_norm_w)


def setup_inputs(seed=0):
    out = dict(first_inputs(seed))
    for name, value in second_inputs(seed + 1).items():
        if name != "x":
            out[name + "_2"] = value
    return out


def reference(
    x, c, ctx, c_ctx, w_ada, b_ada, w_in, attn_q_norm, attn_k_norm, gla_a2_f, gla_ab_f,
    gla_a2_b, gla_ab_b, gla_o_norm, sgu_ln_g, sgu_ln_b, sgu_w, sgu_b, w_br_attn, w_br_gla,
    w_br_sgu, w_out, post_ln_g, post_ln_b, norm_w_2, w_in_2, qkv_conv_w_2, a_log_2, dt_bias_2,
    dn_norm_w_2, w_dn_out_2, cf_conv_w_2, cf_conv_b_2, cf_ln_w_2, cf_ln_b_2, w_cf_out_2,
    gate_b_2, w_out_2, final_norm_w_2,
):
    x = first_block(
        x, c, ctx, c_ctx, w_ada, b_ada, w_in, attn_q_norm, attn_k_norm, gla_a2_f, gla_ab_f,
        gla_a2_b, gla_ab_b, gla_o_norm, sgu_ln_g, sgu_ln_b, sgu_w, sgu_b, w_br_attn, w_br_gla,
        w_br_sgu, w_out, post_ln_g, post_ln_b,
    )
    return second_block(
        x, norm_w_2, w_in_2, qkv_conv_w_2, a_log_2, dt_bias_2, dn_norm_w_2, w_dn_out_2,
        cf_conv_w_2, cf_conv_b_2, cf_ln_w_2, cf_ln_b_2, w_cf_out_2, gate_b_2, w_out_2,
        final_norm_w_2,
    )


_drawn_inputs = setup_inputs


def setup_inputs(seed=0):
    import zlib

    import numpy as np

    out = dict(_drawn_inputs(seed))
    spreads = {}
    factors = {'ctx': 8.0,
     'c_ctx': 8.0,
     'b_ada': 8.0,
     'attn_q_norm': 8.0,
     'attn_k_norm': 8.0,
     'gla_a2_f': 8.0,
     'gla_ab_f': 8.0,
     'gla_a2_b': 8.0,
     'gla_ab_b': 8.0,
     'gla_o_norm': 64.0,
     'sgu_ln_g': 22.149,
     'sgu_ln_b': 45.73,
     'sgu_b': 42.216,
     'w_br_attn': 7.467,
     'cf_conv_b_2': 5.345,
     'cf_ln_w_2': 3.674,
     'cf_ln_b_2': 8.0,
     'gate_b_2': 8.0,
     'dn_norm_w_2': 3.077}
    for name, (base, spread) in spreads.items():
        noise = np.random.default_rng([zlib.crc32(name.encode()), seed]).standard_normal(out[name].shape)
        drawn = base * np.exp(spread * noise) if base else spread * noise
        out[name] = __import__('jax').numpy.asarray(drawn.astype(out[name].dtype))
    for name, factor in factors.items():
        out[name] = (out[name] * factor).astype(out[name].dtype)
    return out
```

```python
from contextlib import ExitStack

import numpy as np

import concourse.bass as bass
from concourse import mybir

F = mybir.dt.float32
U32 = mybir.dt.uint32
ALU = mybir.AluOpType
ACT = mybir.ActivationFunctionType
AX = mybir.AxisListType.X

D = 1024
ALPHA = 4.0 ** 0.25
EPS = 1e-6
MS = (1, 2, 4, 8, 16, 32)
HEADS = (0, 4, 1, 5, 2, 6, 3, 7)

UNIT = 2048
NU = 7

C_ID, C_MASK, C_TWO, C_COS, C_SIN, C_SCAN, C_O128, C_O512, C_ONE, C_INC, C_COL = (
    0, 128, 1664, 1792, 1920, 2048, 2560, 2688, 2816, 2944, 3200)
C_W = 3208

PA_BADA, PA_AB, PA_ON, PA_PM, PA_SW, PA_W = 0, 16, 20, 24, 536, 1048
RA_QK, RA_LG, RA_LB, RA_W = 0, 640, 1152, 1664
PB_NW, PB_CW, PB_FW, PB_FB, PB_LW, PB_LB, PB_GB, PB_DN, PB_AL, PB_DT, PB_W = (
    0, 8, 68, 192, 196, 200, 204, 220, 221, 222, 224)


def plan_a(l):
    out = [(f"a{l}ada{j}", 4096) for j in range(6)]
    out += [(f"a{l}{n}", w) for n, w in (("qa", 4096), ("kv", 8 * 288), ("gqk", 4096), ("gv", 4096), ("ag", 4096),
                                         ("gg", 4096), ("sv", 4096), ("su", 4096), ("sg", 4096))]
    for j in range(2):
        for b in "ags":
            out += [(f"a{l}m{b}{j}", 4096), (f"a{l}b{b}{j}", 2048)]
    return out + [(f"a{l}o{j}", 4096) for j in range(2)]


def plan_b(l):
    out = [(f"b{l}{n}", w) for n, w in (("q0", 4096), ("q1", 4096), ("q2", 4096), ("ab", 800), ("za", 4096),
                                        ("cv", 4096), ("cg", 4096), ("zb", 4096))]
    for j in range(2):
        for b in range(2):
            out += [(f"b{l}m{b}{j}", 4096), (f"b{l}b{b}{j}", 2048)]
    return out + [(f"b{l}o{j}", 4096) for j in range(2)]


PLAN = plan_a(0) + plan_a(1) + plan_b(0) + plan_b(1)


class Engine:

    def __init__(self, sem, chained):
        self.sem, self.chained, self.n, self.seen, self.todo = sem, chained, 0, {}, []

    def put(self, fn, waits, inc=True):
        flat = []

        def add(w):
            if w is None:
                return
            if isinstance(w, list):
                for x in w:
                    add(x)
            else:
                flat.append(w)

        add(list(waits))
        if self.chained and self.n:
            flat.append((self.sem, self.n))
        need = {}
        for sem, v in flat:
            if self.seen.get(id(sem), 0) < v and need.get(id(sem), (sem, 0))[1] < v:
                need[id(sem)] = (sem, v)
        for sem, v in need.values():
            self.seen[id(sem)] = v
        if inc:
            self.n += 1
        self.todo.append((list(need.values()), fn, inc))
        return (self.sem, self.n)

    def run(self, eng):
        for need, fn, inc in self.todo:
            for sem, v in need:
                eng.wait_ge(sem, v)
            ins = fn(eng)
            if inc:
                ins.then_inc(self.sem, 1)


class Bank:
    def __init__(self, t):
        self.t, self.free = t, []


class Pool:

    def __init__(self, banks):
        self.banks, self.i = banks, 0

    def take(self):
        b = self.banks[self.i % len(self.banks)]
        self.i += 1
        return b


def weave(*parts):
    live = [[g, n, 0.0] for g, n in parts]
    while live:
        for it in list(live):
            it[2] += it[1]
            while it[2] >= 1:
                it[2] -= 1
                try:
                    next(it[0])
                except StopIteration:
                    live.remove(it)
                    break


def drain(g):
    for _ in g:
        pass


def build_program(nc, wf, consts, cT, xin, xinT, pa, ra, rpost, pb, rfin, out):
    with ExitStack() as ctx:
        arena = ctx.enter_context(nc.sbuf_tensor("arena", [128, 53200], F))
        top = [0]

        def al(n):
            o = top[0]
            top[0] += n
            assert top[0] <= 53200, top[0]
            return arena[:, o:o + n]

        def sem(name):
            return ctx.enter_context(nc.semaphore(name))

        PS = [Bank(ctx.enter_context(nc.psum_tensor(f"ps{i}", [128, 512], F))[:, :]) for i in range(8)]

        V = Engine(sem("s_v"), True)
        A = Engine(sem("s_a"), True)
        G = Engine(sem("s_g"), True)
        P = Engine(sem("s_p"), False)
        S = Engine(sem("s_sp"), False)
        dman = [0]

        def mm(o, l, r, start, stop, *w, inc=False):
            return P.put(lambda e: e.matmul(o, l, r, start=start, stop=stop, skip_group_check=True), w, inc)

        def tr(o, i, idn, *w, inc=False):
            return P.put(lambda e: e.transpose(o, i, idn), w, inc)

        def tt(E, o, a, b, op, *w):
            return E.put(lambda e: e.tensor_tensor(o, a, b, op), w)

        def ts(E, o, a, s1, s2, op0, op1, *w):
            if s2 is None:
                return E.put(lambda e: e.tensor_scalar(o, a, s1, None, op0), w)
            return E.put(lambda e: e.tensor_scalar(o, a, s1, s2, op0, op1), w)

        def stt(E, o, a, s, b, op0, op1, *w):
            return E.put(lambda e: e.scalar_tensor_tensor(out=o, in0=a, scalar=s, in1=b, op0=op0, op1=op1), w)

        def act(o, i, f, *w, bias=None, scale=None, acc=None):
            kw = {}
            if bias is not None:
                kw["bias"] = bias
            if scale is not None:
                kw["scale"] = scale
            if acc is not None:
                kw["accum_out"] = acc
            return A.put(lambda e: e.activation(o, i, f, **kw), w)

        def cp(E, o, i, *w):
            return E.put(lambda e: e.tensor_copy(o, i), w)

        def ms(E, o, v, *w):
            return E.put(lambda e: e.memset(o, v), w)

        def pred(o, mask, data, *w):
            return V.put(lambda e: e.copy_predicated(o, mask, data), w)

        def dma(o, i, *w, s=None):
            if s is None:
                s = sem(f"s_d{dman[0]}")
                dman[0] += 1

            def go(e):
                e.dma_start(o, i).then_inc(s, 16)

            S.put(go, w, inc=False)
            return (s, 16)

        def r3(ap, n):
            return ap.rearrange("p (a b) -> p a b", a=n)

        ring = al(NU * UNIT)
        usem = [sem(f"s_u{i}") for i in range(NU)]
        ucount = [0] * NU
        ufree = [[] for _ in range(NU)]
        ubusy = [False] * NU
        st = {"next": 0, "at": 0, "off": 0}
        loaded = {}

        def fill():
            while st["next"] < len(PLAN):
                name, w = PLAN[st["next"]]
                k = -(-w // UNIT)
                at = st["at"] if st["at"] + k <= NU else 0
                if any(ubusy[at:at + k]):
                    return
                for u in range(at, at + k):
                    ubusy[u] = True
                off = st["off"]
                dst, src = ring[:, at * UNIT:at * UNIT + w], wf[off:off + 128 * w].rearrange("(p n) -> p n", p=128)
                waits = [t for u in range(at, at + k) for t in ufree[u]]
                dma(dst, src, waits, s=usem[at])
                ucount[at] += 16
                loaded[name] = (dst, (usem[at], ucount[at]), at, k)
                st["next"] += 1
                st["at"] = (at + k) % NU
                st["off"] += 128 * w

        def use(name):
            fill()
            return loaded[name][0], loaded[name][1]

        def release(name, tok):
            _, _, at, k = loaded[name]
            for u in range(at, at + k):
                ubusy[u] = False
                ufree[u] = [tok]
            fill()

        cst = al(C_W)
        k_cst = dma(cst, consts)
        ident = cst[:, C_ID:C_ID + 128]

        def mask(m, swapped):
            o = C_MASK + (2 * MS.index(m) + swapped) * 128
            return cst[:, o:o + 128].bitcast(U32)

        two = cst[:, C_TWO:C_TWO + 128]
        o128 = cst[:, C_O128:C_O128 + 128]
        o512 = cst[:, C_O512:C_O512 + 128]
        ones = cst[:, C_ONE:C_ONE + 128]
        eps = cst[:, C_COL:C_COL + 1]
        one = cst[:, C_COL + 1:C_COL + 2]
        zero = cst[:, C_COL + 2:C_COL + 3]
        mhalf = cst[:, C_COL + 3:C_COL + 4]
        for E in (V, A, G, P):
            E.todo.append(([k_cst], None, False))
            E.seen[id(k_cst[0])] = 16

        X = al(2048)
        base = top[0]

        def rows_of(w, n):
            return w.rearrange("p (k n) -> p k n", k=n)

        def feat(bank, w, n, c0, cols, hT, t0, t1, nk, waits, m=128, o=0, start=True, stop=True):
            tok = None
            for k in range(nk):
                tok = mm(bank.t[0:m, o:o + t1 - t0], w[:, k, c0:c0 + m], hT[:, k, t0:t1],
                         start and k == 0, stop and k == nk - 1, waits if k == 0 else None, inc=(k == nk - 1))
            return tok

        def token(bank, w, c0, c1, hT, t0, waits, nk=8):
            tok = None
            for k in range(nk):
                tok = mm(bank.t[:, 0:c1 - c0], hT[:, k, t0:t0 + 128], w[:, k, c0:c1],
                         k == 0, k == nk - 1, waits if k == 0 else None, inc=(k == nk - 1))
            return tok

        def rstd_small(o, i, *w):
            n = i.shape[1]
            a = ts(G, o, i, eps, None, ALU.add, None, *w)
            return tt(G, o, o, mhalf.to_broadcast([128, n]), ALU.pow, a)

        def rstd_big(o, i, *w):
            act(o, i, ACT.Ln, *w, bias=eps)
            return act(o, o, ACT.Exp, scale=-0.5)

        def layer_a(l, k_x):
            top[0] = base
            t_lo = 0
            T = 512
            hT = r3(al(4096), 8)
            qkv_gv = al(5120)
            QKV = r3(qkv_gv[:, 0:3072], 4)
            GV = r3(qkv_gv[:, 3072:5120], 4)
            mT = r3(qkv_gv[:, 0:4096], 8)
            AG, GG, SG = (r3(al(2048), 4) for _ in range(3))
            GQ, GK = (r3(al(1024), 2) for _ in range(2))
            par = al(PA_SW)
            row = al(640)
            gate = al(1024)
            scol = al(32)
            cc = al(16)
            TH = al(512)
            TH2 = al(512)
            s0 = top[0]
            l0 = 0 if l == 0 else 256
            tiles = range(4) if l == 0 else range(2, 4)

            k_par = dma(par, pa[l][:, 0:PA_SW], k_x)
            k_row = dma(row, ra[l][0:640].partition_broadcast(128), k_x)
            k_c = dma(cc, cT, k_x)
            PM = par[:, PA_PM:PA_PM + 512]
            DP, AP, GP = Pool(PS[0:3]), Pool(PS[3:5]), Pool(PS[5:8])

            top[0] = s0
            cs = al(16)
            ada = al(2048)
            bg = al(1024)
            k_bg = dma(bg[0:2, :], ra[l][RA_W:RA_W + 1024].partition_broadcast(2), k_x)
            act(cs, cc, ACT.Tanh, k_c, k_x, scale=0.5)
            k = stt(V, cs, cs, 1.0, cc, ALU.add, ALU.mult, (A.sem, A.n), k_c)
            k_cs = ts(V, cs, cs, 0.5, None, ALU.mult, None, k)
            cs3 = r3(cs, 8)
            cols = AP.take()
            kc_ = None
            for j in range(6):
                w, kw = use(f"a{l}ada{j}")
                w = rows_of(w, 8)
                b = DP.take()
                for kk in range(8):
                    k = mm(b.t[0:2, :], cs3[:, kk, :], w[:, kk, :], kk == 0, kk == 7,
                           [kw, k_cs, b.free] if kk == 0 else None, inc=kk == 7)
                release(f"a{l}ada{j}", k)
                if j < 4:
                    b.free = [cp(V, ada[0:2, 512 * j:512 * j + 512], b.t[0:2, :], k)]
                else:
                    cg = slice(512 * (j - 4), 512 * (j - 3))
                    b.free = [tt(V, gate[0:2, cg], b.t[0:2, :], bg[0:2, cg], ALU.add, k, k_bg)]
                if j < 4:
                    for i in range(4):
                        q = 4 * j + i
                        kc_ = tr(cols.t[:, 2 * q:2 * q + 2], ada[0:2, 128 * q:128 * q + 128], ident[0:2, 0:2],
                                 b.free, cols.free if q == 0 else None, inc=i == 3)
            k_gate = b.free
            sc3 = r3(scol, 16)
            k = tt(V, sc3, r3(cols.t[:, 0:32], 16),
                   par[:, PA_BADA:PA_BADA + 16].unsqueeze(2).to_broadcast([128, 16, 2]), ALU.add, kc_, k_par)
            cols.free = [k]
            k_sc = ts(V, scol[:, 16:32], scol[:, 16:32], 1.0, None, ALU.add, None, k)

            if l == 0:
                top[0] = s0
                xT = r3(al(4096), 8)
                k_xt = dma(xT, xinT.rearrange("p (a b) -> p a b", a=8), k_sc, kc_, (V.sem, V.n))
                for kk in range(8):
                    for s in range(2):
                        c = 1 - s
                        E = V if s else G
                        ts(E, hT[:, kk, 256 * s:256 * s + 256], xT[:, kk, 256 * s:256 * s + 256],
                           sc3[:, 8 + kk, c:c + 1], sc3[:, kk, c:c + 1], ALU.mult, ALU.add, k_xt, k_sc)
            else:
                for kk in range(8):
                    b = GP.take()
                    for t in range(4):
                        src = (CX if t < 2 else X)[:, 1024 * (t % 2) + 128 * kk:1024 * (t % 2) + 128 * kk + 128]
                        k = tr(b.t[:, 128 * t:128 * t + 128], src, ident, k_x, b.free, inc=t == 3)
                    for s in range(2):
                        c = 1 - s
                        b.free = [ts(V, hT[:, kk, 256 * s:256 * s + 256], b.t[:, 256 * s:256 * s + 256],
                                     sc3[:, 8 + kk, c:c + 1], sc3[:, kk, c:c + 1], ALU.mult, ALU.add, k, k_sc)]
            k_h = [(V.sem, V.n), (G.sem, G.n)]
            top[0] = s0
            done = {}

            def dense():
                w, kw = use(f"a{l}qa")
                w = rows_of(w, 8)
                for t in tiles:
                    b = DP.take()
                    k = token(b, w, 0, 512, hT, 128 * t, [kw, k_h, b.free])
                    b.free = [act(QKV[:, t, 0:512], b.t, ACT.Copy, k)]
                    done[f"q{t}"] = b.free
                    yield
                release(f"a{l}qa", k)
                w, kw = use(f"a{l}kv")
                w = rows_of(w, 8)
                for t in range(4):
                    b = DP.take()
                    k = token(b, w, 0, 256, hT, 128 * t, [kw, b.free])
                    b.free = [act(QKV[:, t, 512:768], b.t[:, 0:256], ACT.Copy, k)]
                    done[f"kv{t}"] = b.free
                    yield
                b = DP.take()
                k = feat(b, w, 8, 256, 32, hT, 0, 512, 8, [b.free], m=32)
                b.free = [act(TH2[0:32, :], b.t[0:32, :], ACT.Copy, k)]
                done["lr"] = b.free
                release(f"a{l}kv", k)
                yield
                w, kw = use(f"a{l}gqk")
                w = rows_of(w, 8)
                for c in range(4):
                    b = DP.take()
                    k = feat(b, w, 8, 128 * c, 128, hT, 0, 512, 8, [kw, b.free])
                    if c < 2:
                        b.free = [act(GQ[:, c, :], b.t, ACT.Copy, k, scale=0.125)]
                    else:
                        b.free = [act(GK[:, c - 2, :], b.t, ACT.Copy, k)]
                    yield
                release(f"a{l}gqk", k)
                done["gqk"] = b.free
                w, kw = use(f"a{l}gv")
                w = rows_of(w, 8)
                for t in range(4):
                    b = DP.take()
                    k = token(b, w, 0, 512, hT, 128 * t, [kw, b.free])
                    b.free = [act(GV[:, t, :], b.t, ACT.Copy, k)]
                    if t == 3:
                        done["gv"] = b.free
                    yield
                release(f"a{l}gv", k)
                for name, dst in (("ag", AG), ("gg", GG)):
                    w, kw = use(f"a{l}{name}")
                    w = rows_of(w, 8)
                    for c in range(4):
                        b = DP.take()
                        k = feat(b, w, 8, 128 * c, 128, hT, l0, 512, 8, [kw, b.free])
                        n = 512 - l0
                        k1 = act(TH[:, 0:n], b.t[:, 0:n], ACT.Tanh, k, done.get("th"), scale=0.5)
                        k2 = stt(V, dst[:, c, l0:512], TH[:, 0:n], 1.0, b.t[:, 0:n], ALU.add, ALU.mult, k1)
                        b.free = [k2]
                        done["th"] = k2
                        done[f"{name}{c}"] = k2
                        yield
                    release(f"a{l}{name}", k)

            def attention(scr):
                stat = scr(10)
                KT = scr(512)
                QT = scr(512)
                Pb = [scr(512) for _ in range(2)]
                PT = [scr(1024) for _ in range(2)]
                sq, qk2 = PT[0][:, 0:640], PT[1][:, 0:640]
                small = [scr(4) for _ in range(2)]
                for t in range(4):
                    while f"kv{t}" not in done:
                        yield
                    wq = done[f"q{t}"] if t in tiles else None
                    lo = 0 if t in tiles else 512
                    nh = (640 - lo) // 64
                    w = [wq, done[f"kv{t}"]]
                    x = QKV[:, t, lo:640]
                    x3 = r3(x, nh)
                    k = tt(G, sq[:, lo:640], x, x, ALU.mult, w, (V.sem, V.n))
                    k = V.put(lambda e, a=stat[:, lo // 64:10], b=r3(sq[:, lo:640], nh): e.tensor_reduce(a, b, AX, ALU.add),
                              [k, (G.sem, G.n)])
                    k = ts(V, stat[:, lo // 64:10], stat[:, lo // 64:10], 1.0 / 64, None, ALU.mult, None)
                    kr = rstd_small(stat[:, lo // 64:10], stat[:, lo // 64:10], k)
                    tt(V, x, x, row[:, RA_QK + lo:RA_QK + 640], ALU.mult, k_row, w, kr)
                    k = tt(V, x3, x3, stat[:, lo // 64:10].unsqueeze(2).to_broadcast([128, nh, 64]), ALU.mult, kr)
                    if t >= 2:
                        cos = cst[:, C_COS + 64 * (t - 2):C_COS + 64 * (t - 1)].unsqueeze(1).to_broadcast([128, 10, 64])
                        sn = cst[:, C_SIN + 64 * (t - 2):C_SIN + 64 * (t - 1)]
                        x5 = x.rearrange("p (h a b c) -> p h a b c", h=10, a=2, b=2)
                        q5 = qk2.rearrange("p (h a b c) -> p h a b c", h=10, a=2, b=2)
                        s4 = sn.rearrange("p (a b c) -> p a b c", a=2, b=2)
                        for hf in range(2):
                            kg = tt(G, q5[:, :, :, hf, :], x5[:, :, :, 1 - hf, :],
                                    s4[:, :, hf, :].unsqueeze(1).to_broadcast([128, 10, 2, 16]), ALU.mult, k,
                                    done.get("qk2"))
                        k = tt(V, x3, x3, cos, ALU.mult, kg)
                        k = tt(V, x, x, qk2, ALU.add, kg)
                        done["qk2"] = k
                    done[f"n{t}"] = k
                    yield
                b = AP.take()
                for t in range(4):
                    k = tr(b.t[:, 128 * t:128 * t + 128], QKV[:, t, 512:640], ident, done[f"n{t}"], b.free, inc=t == 3)
                k_kt = cp(V, KT, b.t, k)
                b.free = [k_kt]
                yield
                pt_free = [None, None]
                n = 0
                for c in range(4):
                    b = AP.take()
                    for t in tiles:
                        k = tr(b.t[:, 128 * t:128 * t + 128], QKV[:, t, 128 * c:128 * c + 128], ident,
                               done[f"n{t}"], b.free, inc=t == 3)
                    k_qt = act(QT[:, l0:512], b.t[:, l0:512], ACT.Copy, k, k_kt, done.get("qt"))
                    b.free = [k_qt]
                    yield
                    for s in ((0, 1) if l == 0 else (1,)):
                        L = 256 + 256 * s
                        kpt = []
                        for p in range(2):
                            PTp = r3(PT[p], 4)
                            for i in range(2):
                                t = 2 * s + i
                                b = AP.take()
                                k = mm(b.t[:, 0:L], QT[64 * p:64 * p + 64, 128 * t:128 * t + 128],
                                       KT[64 * p:64 * p + 64, 0:L], True, True, k_qt, k_kt, b.free, inc=True)
                                done["qt"] = k
                                sm = small[n % 2]
                                pb = Pb[n % 2]
                                n += 1
                                wp = done.get(f"pb{n % 2}")
                                V.put(lambda e, o=sm[:, 0:1], x=b.t[:, 0:L]: e.reduce_max(o, x, AX), [k, wp])
                                k = ts(V, sm[:, 1:2], sm[:, 0:1], -0.125, None, ALU.mult, None)
                                k = act(pb[:, 0:L], b.t[:, 0:L], ACT.Exp, k, wp, bias=sm[:, 1:2], scale=0.125,
                                        acc=sm[:, 2:3])
                                b.free = [k]
                                V.put(lambda e, o=sm[:, 3:4], x=sm[:, 2:3]: e.reciprocal(o, x), [k])
                                k = ts(V, pb[:, 0:L], pb[:, 0:L], sm[:, 3:4], None, ALU.mult, None, k)
                                yield
                                b = AP.take()
                                for j in range(L // 128):
                                    kt_ = tr(b.t[:, 128 * j:128 * j + 128], pb[:, 128 * j:128 * j + 128], ident,
                                             k, b.free, inc=j == L // 128 - 1)
                                done[f"pb{n % 2}"] = kt_
                                k = act(PTp[:, 0:L // 128, 128 * i:128 * i + 128], r3(b.t[:, 0:L], L // 128), ACT.Copy,
                                        kt_, pt_free[p])
                                b.free = [k]
                                kpt.append(k)
                                yield
                        b = AP.take()
                        for p in range(2):
                            PTp = r3(PT[p], 4)
                            for j in range(L // 128):
                                k = mm(b.t[64 * p:64 * p + 64, 0:256], QKV[:, j, 640 + 64 * p:704 + 64 * p],
                                       PTp[:, j, :], j == 0, j == L // 128 - 1, kpt, done[f"kv{j}"], b.free,
                                       inc=j == L // 128 - 1)
                            pt_free[p] = k
                        while f"ag{c}" not in done:
                            yield
                        y = AG[:, c, 256 * s:256 * s + 256]
                        k = stt(V, y, b.t[:, 0:256], 0.5, y, ALU.mult, ALU.mult, k, done[f"ag{c}"])
                        b.free = [k]
                        done["ya"] = k
                        yield

            def gla(scr):
                B = [r3(scr(512), 1) for _ in range(2)]
                E = scr(512)
                QK = [scr(512) for _ in range(2)]
                att = scr(1024).rearrange("p (t h c) -> p t h c", t=4, h=2)
                KDT = [scr(512) for _ in range(2)]
                QB = [scr(512) for _ in range(2)]
                ST = scr(2048).rearrange("p (d n v) -> p d n v", d=2, n=8)
                SC = cst[:, C_SCAN:C_SCAN + 512]
                scr1 = scr(512)
                scr2 = scr(512)
                EL = scr(16)
                nt = len(tiles)
                W = 512 - l0
                while "lr" not in done:
                    yield
                for hp in range(2):
                    last = done.get("glalast")
                    for d in range(2):
                        b = GP.take()
                        k = mm(b.t, PM[0:32, 256 * d + 128 * hp:256 * d + 128 * hp + 128], TH2[0:32, :], True, True,
                               done["lr"], k_par, b.free, inc=True)
                        k = act(scr1, b.t, ACT.Identity, k, k_par, last, (V.sem, V.n),
                                bias=par[:, PA_AB + 2 * d + hp:PA_AB + 2 * d + hp + 1])
                        b.free = [k]
                        act(scr2, scr1, ACT.Abs)
                        act(scr2, scr2, ACT.Exp, scale=-1.0)
                        k = act(scr2, scr2, ACT.Ln, bias=one)
                        k = stt(V, scr2, scr1, 0.0, scr2, ALU.min, ALU.subtract, k, last)
                        o, g = B[d][:, 0, :], scr2
                        if d:
                            o, g = o[:, ::-1], g[:, ::-1]
                        V.put(lambda e, o=o, g=g: e.tensor_tensor_scan(o, SC, g, 0.0, ALU.mult, ALU.add), [])
                        yield
                    while "gqk" not in done:
                        yield
                    kB = (V.sem, V.n)
                    kel = []
                    for d in range(2):
                        b4 = B[d][:, 0, :].rearrange("p (n m) -> p n m", m=64)
                        r = b4[:, :, 0:1] if d else b4[:, :, 63:64]
                        k = tt(G, r3(E, 8), r.to_broadcast([128, 8, 64]), b4, ALU.subtract, kB, (A.sem, A.n),
                               (V.sem, V.n))
                        k = act(E, E, ACT.Exp, k, scale=1.0 / 16)
                        kel = act(EL[:, 8 * d:8 * d + 8].unsqueeze(2), r, ACT.Exp, kB, scale=1.0 / 16)
                        k = tt(V, QK[d], GK[:, hp, :], E, ALU.mult, k, (P.sem, P.n), done["gqk"])
                        yield
                        b = GP.take()
                        for t in range(4):
                            k2 = tr(b.t[:, 128 * t:128 * t + 128], QK[d][:, 128 * t:128 * t + 128], ident, k, b.free,
                                    inc=t == 3)
                        k = act(KDT[d], b.t, ACT.Copy, k2, last)
                        b.free = [k]
                        k2 = act(QB[d][:, l0:512], B[d][:, 0, l0:512], ACT.Exp, kB, last, scale=1.0 / 16)
                        tt(V, QB[d][:, l0:512], QB[d][:, l0:512], GQ[:, hp, l0:512], ALU.mult, k2)
                        yield
                    kQB = (V.sem, V.n)
                    kKD = (A.sem, A.n)
                    while "gv" not in done:
                        yield
                    order = [[0, 1, 2, 3, 4, 5, 6, 7], [3, 2, 1, 0, 7, 6, 5, 4]]
                    for i in range(7):
                        for d in range(2):
                            b = GP.take()
                            n, nx = order[d][i], order[d][i + 1]
                            t, r0 = n // 2, 64 * (n % 2)
                            for p in range(2):
                                h = 2 * hp + p
                                k = mm(b.t[64 * p:64 * p + 64, 0:128],
                                       KDT[d][r0:r0 + 64, 128 * t + 64 * p:128 * t + 64 * p + 64],
                                       GV[r0:r0 + 64, t, 128 * h:128 * h + 128], True, True,
                                       kKD, done["gv"], b.free, inc=True)
                            u = b.t[:, 0:128]
                            if i == 0:
                                k2 = cp(V, ST[:, d, nx, :], u, k, last)
                            else:
                                k2 = stt(V, ST[:, d, nx, :], ST[:, d, n, :], EL[:, 8 * d + n:8 * d + n + 1], u,
                                         ALU.mult, ALU.add, k, kel)
                            b.free = [k2]
                        yield
                    kST = k2
                    for p in range(2):
                        b = GP.take()
                        for t in tiles:
                            k = mm(b.t[:, 128 * t:128 * t + 128], GK[64 * p:64 * p + 64, hp, 128 * t:128 * t + 128],
                                   GQ[64 * p:64 * p + 64, hp, 128 * t:128 * t + 128], t == tiles[0], True, done["gqk"],
                                   b.free, inc=t == 3)
                        b.free = [tt(V, att[:, tiles[0]:4, p, :], r3(b.t[:, l0:512], nt),
                                     two.unsqueeze(1).to_broadcast([128, nt, 128]), ALU.mult, k, last)]
                        yield
                    n = 0
                    kq = [None, None]
                    for m in MS:
                        for d in range(2):
                            b4 = B[d][:, 0, l0:512].rearrange("p (n s m) -> p n s m", s=2, m=m)
                            e4 = E[:, l0:512].rearrange("p (n s m) -> p n s m", s=2, m=m)
                            nn = W // (2 * m)
                            r = b4[:, :, 1, 0:1] if d else b4[:, :, 0, m - 1:m]
                            r = r.to_broadcast([128, nn, m])
                            wv = (V.sem, V.n)
                            hk, hq = (1, 0) if d else (0, 1)
                            tt(G, e4[:, :, hk, :], r, b4[:, :, hk, :], ALU.subtract, wv)
                            k = tt(G, e4[:, :, hq, :], b4[:, :, hq, :], r, ALU.subtract, wv)
                            k = act(E[:, l0:512], E[:, l0:512], ACT.Exp, k, scale=1.0 / 16)
                            qk = QK[n % 2]
                            q4 = qk[:, l0:512].rearrange("p (n s m) -> p n s m", s=2, m=m)
                            for half, src in ((hk, GK), (hq, GQ)):
                                k = tt(V, q4[:, :, half, :], e4[:, :, half, :],
                                       src[:, hp, l0:512].rearrange("p (n s m) -> p n s m", s=2, m=m)[:, :, half, :],
                                       ALU.mult, k, kq[n % 2])
                            yield
                            for p in range(2):
                                b = GP.take()
                                for t in tiles:
                                    a = qk[64 * p:64 * p + 64, 128 * t:128 * t + 128]
                                    k2 = mm(b.t[:, 128 * t:128 * t + 128], a, a, t == tiles[0], True, k, b.free,
                                            inc=t == 3)
                                b.free = [pred(att[:, tiles[0]:4, p, :],
                                               mask(m, d).unsqueeze(1).to_broadcast([128, nt, 128]),
                                               r3(b.t[:, l0:512], nt), k2)]
                            kq[n % 2] = k2
                            n += 1
                            yield
                    katt = (V.sem, V.n)
                    for p in range(2):
                        h = 2 * hp + p
                        while f"gg{h}" not in done:
                            yield
                        b = GP.take()
                        first = True
                        for t in tiles:
                            mm(b.t[:, 128 * t:128 * t + 128], GV[:, t, 128 * h:128 * h + 128], att[:, t, p, :],
                               first, False, katt, b.free)
                            first = False
                            for n in (2 * t, 2 * t + 1):
                                for d in range(2):
                                    if (d == 0 and n == 0) or (d == 1 and n == 3):
                                        continue
                                    k = mm(b.t[:, 64 * n:64 * n + 64], ST[64 * p:64 * p + 64, d, n, :],
                                           QB[d][64 * p:64 * p + 64, 64 * n:64 * n + 64], False, True, kST, kQB,
                                           inc=True)
                        O, Q2 = scr1[:, l0:512], scr2[:, l0:512]
                        k = act(O, b.t[:, l0:512], ACT.Copy, k, (V.sem, V.n))
                        b.free = [k]
                        k = tt(V, Q2, O, O, ALU.mult, k)
                        yield
                        b = GP.take()
                        k = mm(b.t[:, l0:512], o128, Q2, True, True, k, b.free, inc=True)
                        b.free = [rstd_big(Q2, b.t[:, l0:512], k)]
                        k = stt(V, O, O, par[:, PA_ON:PA_ON + 1], Q2, ALU.mult, ALU.mult, b.free, k_par)
                        y = GG[:, h, l0:512]
                        done["yg"] = stt(V, y, O, 0.5, y, ALU.mult, ALU.mult, done[f"gg{h}"])
                        yield
                    done["glalast"] = [(V.sem, V.n), (A.sem, A.n), (P.sem, P.n)]

            marks = {}

            def scr(n):
                return al(n)

            weave((dense(), 1), (attention(scr), 2), (gla(scr), 3))
            allk = [(V.sem, V.n), (A.sem, A.n), (P.sem, P.n), (G.sem, G.n)]
            top[0] = s0

            VN = [al(512) for _ in range(2)]
            VC = al(512)
            bs = al(16)
            w, kw = use(f"a{l}sv")
            w = rows_of(w, 8)
            w2, kw2 = None, None
            mixed = {}
            SW = al(512)
            LGB = al(1024)
            k_sw = dma(SW, pa[l][:, PA_SW:PA_W], allk)
            k_lgb = dma(LGB, ra[l][640:RA_W].partition_broadcast(128), allk)
            SV = r3(al(2048), 4)

            def sgu_dense():
                for t in tiles:
                    b = DP.take()
                    k = token(b, w, 0, 512, hT, 128 * t, [kw, b.free])
                    b.free = [act(SV[:, t, :], b.t, ACT.Copy, k, allk)]
                    mixed[f"sv{t}"] = b.free
                    yield
                release(f"a{l}sv", k)
                SU = mixed["SU"]
                for name in ("su", "sg"):
                    ww, kww = use(f"a{l}{name}")
                    ww = rows_of(ww, 8)
                    n = 512 - l0
                    for c in range(4):
                        b = DP.take()
                        k = feat(b, ww, 8, 128 * c, 128, hT, l0, 512, 8, [kww, b.free])
                        if name == "su":
                            b.free = [act(SU[:, c, l0:512], b.t[:, 0:n], ACT.Copy, k)]
                        else:
                            k1 = act(TH[:, 0:n], b.t[:, 0:n], ACT.Tanh, k, mixed.get("th"), scale=0.5)
                            k2 = stt(V, SG[:, c, l0:512], TH[:, 0:n], 1.0, b.t[:, 0:n], ALU.add, ALU.mult, k1)
                            b.free = [k2]
                            mixed["th"] = k2
                            k3 = tt(G, SG[:, c, l0:512], SG[:, c, l0:512], SU[:, c, l0:512], ALU.mult, k2, k1)
                            mixed["sgsu"] = k3
                        yield
                    release(f"a{l}{name}", k)

            def sgu_mix():
                MX = mixed["MX"]
                for t in tiles:
                    while f"sv{t}" not in mixed:
                        yield
                    x = SV[:, t, :]
                    V.put(lambda e, x=x: e.bn_stats(bs[:, 0:6], x), [mixed[f"sv{t}"]])
                    k = V.put(lambda e: e.bn_aggr(bs[:, 6:8], bs[:, 0:6]), [])
                    kr = rstd_small(bs[:, 8:9], bs[:, 7:8], k)
                    ts(V, x, x, bs[:, 6:7], bs[:, 8:9], ALU.subtract, ALU.mult, kr)
                    k = tt(V, x, x, LGB[:, 0:512], ALU.mult, k_lgb)
                    k = tt(V, x, x, LGB[:, 512:1024], ALU.add, k_lgb)
                    yield
                    b = GP.take()
                    for g in range(4):
                        mm(b.t[:, 128 * g:128 * g + 128], x[:, 128 * g:128 * g + 128], SW[:, 128 * g:128 * g + 128],
                           g == 0, False, k, k_sw, b.free)
                    for g in range(4):
                        k2 = mm(b.t[:, 128 * g:128 * g + 128], ones[32:33, :], PM[32:33, 128 * g:128 * g + 128], False,
                                True, inc=g == 3)
                    b.free = [act(MX[:, :, 128 * t:128 * t + 128], r3(b.t, 4), ACT.Copy, k2, scale=0.5)]
                    mixed["mx"] = b.free
                    yield

            mixed["SU"] = r3(al(2048), 4)
            mixed["MX"] = r3(al(2048), 4)
            weave((sgu_dense(), 1), (sgu_mix(), 1))
            k_ys = tt(V, SG[:, :, l0:512], SG[:, :, l0:512], mixed["MX"][:, :, l0:512], ALU.mult, mixed["mx"],
                      mixed["sgsu"])

            n = 512 - l0
            DP2 = Pool(PS)
            SIG = [VN[0], VN[1]]
            TM = VC
            it = 0
            ys = {"a": (AG, done["ya"]), "g": (GG, done["yg"]), "s": (SG, k_ys)}
            free_sig = [None, None]
            ktm = None
            for j in range(2):
                for bi, br in enumerate("ags"):
                    w, kw = use(f"a{l}m{br}{j}")
                    w = rows_of(w, 8)
                    wb, kwb = use(f"a{l}b{br}{j}")
                    wb = rows_of(wb, 4)
                    Y, ky = ys[br]
                    for c in range(4):
                        b = DP2.take()
                        k = feat(b, w, 8, 128 * c, 128, hT, l0, 512, 8, [kw, b.free])
                        sg = SIG[it % 2][:, 0:n]
                        k = act(sg, b.t[:, 0:n], ACT.Tanh, k, free_sig[it % 2], k_ys, scale=0.5)
                        b.free = [k]
                        b = DP2.take()
                        k2 = feat(b, wb, 4, 128 * c, 128, Y, l0, 512, 4, [kwb, ky, b.free])
                        m = mT[:, 4 * j + c, l0:512]
                        if bi == 0:
                            k3 = stt(V, m, sg, 1.0, b.t[:, 0:n], ALU.add, ALU.mult, k, k2)
                        else:
                            k3 = stt(V, TM[:, 0:n], sg, 1.0, b.t[:, 0:n], ALU.add, ALU.mult, k, k2, ktm)
                            ktm = tt(G, m, m, TM[:, 0:n], ALU.add, k3)
                        b.free = [k3]
                        free_sig[it % 2] = k3
                        it += 1
                    release(f"a{l}m{br}{j}", k)
                    release(f"a{l}b{br}{j}", k2)
            km = [(V.sem, V.n), (G.sem, G.n)]

            top[0] = s0 + 512 * 3
            rp = al(2048)
            gb = al(2048)
            zz = al(1024)
            st6 = al(16)
            if l == 0:
                XR = al(4096)
                k_xr = dma(XR, xin, km)
                CXn = AGflat(AG)
            k_rp = dma(rp, rpost[l].partition_broadcast(128), km)
            for s in range(2):
                for hf in range(2):
                    if l == 1 and s == 0:
                        continue
                    b = DP2.take()
                    c = 1 - s
                    k = mm(b.t, ident[0:2, c:c + 1].to_broadcast([2, 128]), gate[0:2, 512 * hf:512 * hf + 512], True,
                           True, k_gate, b.free, inc=True)
                    b.free = [act(gb[:, 1024 * s + 512 * hf:1024 * s + 512 * hf + 512], b.t, ACT.Copy, k, km,
                                  scale=0.5)]
            k_gb = (A.sem, A.n)
            w0, kw0 = use(f"a{l}o0")
            w1, kw1 = use(f"a{l}o1")
            ws = [(rows_of(w0, 8), kw0), (rows_of(w1, 8), kw1)]
            for t in tiles:
                s = t // 2
                for hf in range(2):
                    b = DP2.take()
                    w, kw = ws[hf]
                    k = token(b, w, 0, 512, mT, 128 * t, [kw, km, b.free])
                    cs_ = slice(512 * hf, 512 * hf + 512)
                    k2 = tt(V, zz[:, cs_], b.t, gb[:, 1024 * s + 512 * hf:1024 * s + 512 * hf + 512], ALU.mult, k, k_gb)
                    b.free = [k2]
                    xr = (XR[:, 1024 * t + 512 * hf:1024 * t + 512 * hf + 512] if l == 0
                          else X[:, 1024 * (t % 2) + 512 * hf:1024 * (t % 2) + 512 * hf + 512])
                    stt(V, zz[:, cs_], xr, ALPHA, zz[:, cs_], ALU.mult, ALU.add, k_xr if l == 0 else None)
                    V.put(lambda e, o=st6[:, 6 * hf:6 * hf + 6], i=zz[:, cs_]: e.bn_stats(o, i), [])
                k = V.put(lambda e: e.bn_aggr(st6[:, 12:14], r3(st6[:, 0:12], 2)), [])
                kr = rstd_small(st6[:, 14:15], st6[:, 13:14], k)
                o = X[:, 1024 * (t % 2):1024 * (t % 2) + 1024] if t >= 2 else CX[:, 1024 * t:1024 * t + 1024]
                ts(V, zz, zz, st6[:, 12:13], st6[:, 14:15], ALU.subtract, ALU.mult, kr)
                tt(V, zz, zz, rp[:, 0:1024], ALU.mult, k_rp)
                k = tt(V, o, zz, rp[:, 1024:2048], ALU.add, k_rp)
                lastp = (P.sem, P.n)
            release(f"a{l}o0", lastp)
            release(f"a{l}o1", lastp)
            return [(V.sem, V.n), (G.sem, G.n), (P.sem, P.n), (A.sem, A.n)]

        CXh = {}

        def AGflat(AG):
            return None

        CX = arena[:, 53200 - 2048:53200]

        def layer_b(l, k_x):
            top[0] = base
            hT = r3(al(2048), 8)
            par = al(PB_W)
            QPf = al(12 * 260)
            QP = r3(QPf, 12)
            CV = r3(al(3072), 12)
            ZA = r3(al(1024), 4)
            CU = r3(al(4 * 286), 4)
            CA = r3(al(1024), 4)
            ZB = r3(al(1024), 4)
            TH = al(512)
            s0 = top[0]
            k_par = dma(par, pb[l], k_x)
            DP = Pool(PS[0:2])
            SP_ = Pool(PS[2:5])
            HP = Pool(PS[5:8])
            XS = al(2048)
            st2 = al(4)
            for t in range(2):
                k = act(XS[:, 1024 * t:1024 * t + 1024], X[:, 1024 * t:1024 * t + 1024], ACT.Square, k_x,
                        acc=st2[:, t:t + 1])
            k = ts(V, st2[:, 0:2], st2[:, 0:2], 1.0 / 1024, None, ALU.mult, None, k, k_x)
            kr = rstd_small(st2[:, 2:4], st2[:, 0:2], k)
            for t in range(2):
                k = ts(V, XS[:, 1024 * t:1024 * t + 1024], X[:, 1024 * t:1024 * t + 1024], st2[:, 2 + t:3 + t], None,
                       ALU.mult, None, kr)
            for kk in range(8):
                b = SP_.take()
                for t in range(2):
                    k2 = tr(b.t[:, 128 * t:128 * t + 128], XS[:, 1024 * t + 128 * kk:1024 * t + 128 * kk + 128], ident,
                            k, b.free, inc=t == 1)
                b.free = [act(hT[:, kk, :], b.t[:, 0:256], ACT.Copy, k2, k_par, scale=par[:, PB_NW + kk:PB_NW + kk + 1])]
            k_h = [(A.sem, A.n)]
            ms(G, QP[:, :, 0:2], 0.0, k_x)
            ms(G, QP[:, :, 258:260], 0.0)
            ms(G, CU[:, :, 0:15], 0.0)
            ms(G, CU[:, :, 271:286], 0.0)
            top[0] = s0
            done = {}

            def dense():
                for j in range(3):
                    w, kw = use(f"b{l}q{j}")
                    w = rows_of(w, 8)
                    for c in range(4):
                        b = DP.take()
                        k = feat(b, w, 8, 128 * c, 128, hT, 0, 256, 8, [kw, k_h, b.free])
                        b.free = [act(QP[:, 4 * j + c, 2:258], b.t[:, 0:256], ACT.Copy, k)]
                        done[f"q{4 * j + c}"] = b.free
                        yield
                    release(f"b{l}q{j}", k)
                w, kw = use(f"b{l}ab")
                w = rows_of(w, 8)
                b = DP.take()
                k = feat(b, w, 8, 0, 100, hT, 0, 256, 8, [kw, b.free], m=100)
                b.free = [act(TH[0:100, 0:256], b.t[0:100, 0:256], ACT.Copy, k)]
                done["ab"] = b.free
                release(f"b{l}ab", k)
                yield
                for name in ("za", "cv", "cg", "zb"):
                    w, kw = use(f"b{l}{name}")
                    w = rows_of(w, 8)
                    for c in range(4):
                        b = DP.take()
                        k = feat(b, w, 8, 128 * c, 128, hT, 0, 256, 8, [kw, b.free])
                        ps = b.t[:, 0:256]
                        if name == "cv":
                            b.free = [act(CU[:, c, 15:271], ps, ACT.Copy, k, (G.sem, G.n))]
                        else:
                            dst = {"za": ZA, "zb": ZB, "cg": CA}[name][:, c, :]
                            k1 = act(TH[:, 256:512], ps, ACT.Tanh, k, done.get("th"), scale=0.5)
                            if name == "cg":
                                k2 = stt(V, CU[:, c, 15:271], TH[:, 256:512], 1.0, CU[:, c, 15:271], ALU.add,
                                         ALU.mult, k1)
                                b.free = [k1]
                                done[f"cu{c}"] = k2
                            else:
                                k2 = stt(V, dst, TH[:, 256:512], 1.0, ps, ALU.add, ALU.mult, k1)
                                b.free = [k2]
                            done["th"] = k2
                            done[f"{name}{c}"] = k2
                        yield
                    release(f"b{l}{name}", k)

            def confconv(scr):
                UM = scr(256)
                UQ = scr(256)
                fw = par[:, PB_FW:PB_FW + 124]
                for c in range(4):
                    while f"cu{c}" not in done:
                        yield
                    E = V
                    k = ts(E, CA[:, c, :], CU[:, c, 0:256], fw[:, 31 * c:31 * c + 1], None, ALU.mult, None,
                           done[f"cu{c}"], k_par)
                    for i in range(1, 31):
                        stt(E, CA[:, c, :], CU[:, c, i:i + 256], fw[:, 31 * c + i:31 * c + i + 1], CA[:, c, :],
                            ALU.mult, ALU.add)
                        if i % 4 == 0:
                            yield
                    ts(E, CA[:, c, :], CA[:, c, :], 0.5, par[:, PB_FB + c:PB_FB + c + 1], ALU.mult, ALU.add)
                    yield
                kca = [(V.sem, V.n), (G.sem, G.n)]
                b = DP.take()
                for c in range(4):
                    k = mm(b.t[:, 0:256], o512, CA[:, c, :], c == 0, c == 3, kca, b.free, inc=c == 3)
                ub = UM.unsqueeze(1).to_broadcast([128, 4, 256])
                k = act(UM, b.t[:, 0:256], ACT.Copy, k)
                b.free = [k]
                k = tt(V, CA[:, :, :], CA[:, :, :], ub, ALU.subtract, k, kca)
                b = DP.take()
                for c in range(4):
                    k1 = act(UQ, CA[:, c, :], ACT.Square, k, (P.sem, P.n))
                    k2 = mm(b.t[:, 0:256], o512, UQ, c == 0, c == 3, k1, b.free, inc=True)
                b.free = [rstd_big(UM, b.t[:, 0:256], k2)]
                k = tt(V, CA[:, :, :], CA[:, :, :], ub, ALU.mult, b.free)
                for c in range(4):
                    k = ts(V, CA[:, c, :], CA[:, c, :], par[:, PB_LW + c:PB_LW + c + 1],
                           par[:, PB_LB + c:PB_LB + c + 1], ALU.mult, ALU.add)
                k1 = act(CU[:, :, 0:256], CA[:, :, :], ACT.Tanh, k, scale=0.5)
                while "zb3" not in done:
                    yield
                stt(V, CA[:, :, :], CU[:, :, 0:256], 1.0, CA[:, :, :], ALU.add, ALU.mult, k1)
                done["yb"] = stt(V, CA[:, :, :], CA[:, :, :], 0.25, ZB[:, :, :], ALU.mult, ALU.mult, done["zb3"])
                yield

            def delta(scr):
                cw = par[:, PB_CW:PB_CW + 60]
                K3 = r3(scr(1024), 2)
                V3 = r3(scr(1024), 2)
                EG = r3(scr(2048), 8)
                DT = r3(scr(2048), 16)
                AT = r3(scr(2048), 16)
                NL = r3(scr(2048), 16)
                XM = r3(scr(2048), 16)
                XT = r3(scr(2048), 16)
                Y = r3(scr(2048), 16)
                QD = r3(QPf[:, 0:2048], 8)
                KG = NL
                KC = Y
                KD = DT
                GB = scr(256)
                GB2 = scr(256)
                GC = r3(scr(200), 2)
                BC = scr(64)
                SS = r3(QPf[:, 2048:3072], 8)
                VW = [scr(512) for _ in range(2)]
                R = scr(512)
                order = (0, 4, 8, 1, 5, 9, 2, 6, 10, 3, 7, 11)
                for c in order:
                    while f"q{c}" not in done:
                        yield
                for c in order:
                    E = V
                    for i in range(5):
                        s = cw[:, 5 * c + i:5 * c + i + 1]
                        if i == 0:
                            k = ts(E, CV[:, c, :], QP[:, c, 0:256], s, None, ALU.mult, None, done[f"q{c}"], k_par,
                                   (G.sem, G.n))
                        else:
                            k = stt(E, CV[:, c, :], QP[:, c, i:i + 256], s, CV[:, c, :], ALU.mult, ALU.add)
                    k1 = act(QP[:, c, 0:256], CV[:, c, :], ACT.Tanh, k, scale=0.5)
                    k = stt(E, CV[:, c, :], QP[:, c, 0:256], 1.0, CV[:, c, :], ALU.add, ALU.mult, k1)
                    yield
                kcv = [(V.sem, V.n), (G.sem, G.n)]
                for c in range(8):
                    k = act(R[:, 0:256], CV[:, c, :], ACT.Square, kcv, (P.sem, P.n), (V.sem, V.n))
                    b = SP_.take()
                    k = mm(b.t[:, 0:256], o128, R[:, 0:256], True, True, k, b.free, inc=True)
                    act(R[:, 256:512], b.t[:, 0:256], ACT.Ln, k, bias=eps, scale=32.0)
                    k = act(R[:, 256:512], R[:, 256:512], ACT.Exp, scale=-0.5)
                    b.free = [k]
                    f = 0.5 * (128.0 ** -0.5 if c < 4 else 1.0)
                    k = stt(V, CV[:, c, :], CV[:, c, :], f, R[:, 256:512], ALU.mult, ALU.mult, k)
                    yield
                k = ts(V, CV[:, 8:12, :], CV[:, 8:12, :], 0.5, None, ALU.mult, None)
                kcv = k
                for src, dst in ((4, K3), (8, V3)):
                    for t in range(2):
                        b = SP_.take()
                        for h in range(4):
                            k = tr(b.t[:, 128 * h:128 * h + 128], CV[:, src + h, 128 * t:128 * t + 128], ident, kcv,
                                   b.free, inc=h == 3)
                        b.free = [act(dst[:, t, :], b.t, ACT.Copy, k)]
                        yield
                kkv = (A.sem, A.n)
                while "ab" not in done:
                    yield
                k = ms(V, GB[0:100, :], 0.0)
                act(GB2[0:36, :], TH[0:36, 0:256], ACT.Identity, done["ab"], k_par, k,
                    bias=par[0:36, PB_DT:PB_DT + 1])
                act(TH[0:36, 0:256], GB2[0:36, :], ACT.Abs)
                act(TH[0:36, 0:256], TH[0:36, 0:256], ACT.Exp, scale=-1.0)
                act(TH[0:36, 0:256], TH[0:36, 0:256], ACT.Ln, bias=one[0:36, :])
                k = act(BC[0:36, 0:1], par[0:36, PB_AL:PB_AL + 1], ACT.Exp)
                stt(V, GB2[0:36, :], GB2[0:36, :], 0.0, TH[0:36, 0:256], ALU.max, ALU.add, k)
                ts(V, BC[0:36, 1:2], BC[0:36, 0:1], -1.0, None, ALU.mult, None)
                ts(V, GB2[0:36, :], GB2[0:36, :], BC[0:36, 1:2], None, ALU.mult, None)
                SCN = cst[:, C_SCAN:C_SCAN + 256]
                V.put(lambda e: e.tensor_tensor_scan(GB[0:32, :], SCN[0:32, :], GB2[0:32, :], 0.0, ALU.mult, ALU.add), [])
                V.put(lambda e: e.tensor_tensor_scan(GB[32:36, ::-1], SCN[32:36, :], GB2[32:36, ::-1], 0.0, ALU.mult,
                                                     ALU.add), [])
                k = act(GB[64:100, :], TH[64:100, 0:256], ACT.Tanh, (V.sem, V.n), scale=0.5)
                k = ts(V, GB[64:100, :], GB[64:100, :], 0.5, 0.5, ALU.mult, ALU.add, k)
                b = SP_.take()
                for t in range(2):
                    k2 = tr(b.t[:, 128 * t:128 * t + 100], GB[0:100, 128 * t:128 * t + 128], ident[0:100, 0:100], k,
                            b.free, inc=t == 1)
                kgc = cp(V, GC, b.t[:, 0:256].rearrange("p (a b) -> p a b", a=2)[:, :, 0:100], k2)
                b.free = [kgc]
                for d in range(2):
                    for t in range(2):
                        o = 8 * d + 4 * t
                        cp(V, BC[:, o:o + 4], GC[:, t, 64 + 32 * d:68 + 32 * d])
                        ts(V, BC[:, 16 + o:20 + o], GC[:, t, 64 + 32 * d:68 + 32 * d], -1.0, None, ALU.mult, None)
                        kbc = act(BC[:, 32 + o:36 + o], GC[:, t, 32 * d:32 * d + 4], ACT.Exp, kgc, (V.sem, V.n))
                yield
                for d in range(2):
                    for hq in range(2):
                        b = SP_.take()
                        for i in range(2):
                            h = 2 * hq + i
                            rr = 32 * d + h
                            k = mm(b.t[:, 256 * i:256 * i + 256], ident[0:36, rr:rr + 1].to_broadcast([36, 128]),
                                   GB[0:36, :], i == 0, True, b.free, k2, inc=i == 1)
                        for i in range(2):
                            h = 2 * hq + i
                            for t in range(2):
                                kv_ = ts(V, DT[:, 8 * d + 4 * t + h, :], b.t[:, 256 * i + 128 * t:256 * i + 128 * t + 128],
                                         GC[:, t, 32 * d + h:32 * d + h + 1], 0.0, ALU.subtract, ALU.min, k)
                        b.free = [act(EG[:, 4 * d + 2 * hq:4 * d + 2 * hq + 2, :], r3(b.t, 2), ACT.Exp, kv_)]
                        yield
                for d in range(2):
                    k = act(DT[:, 8 * d:8 * d + 8, :], DT[:, 8 * d:8 * d + 8, :], ACT.Exp)
                    inc_ = cst[:, C_INC + 128 * d:C_INC + 128 * d + 128].unsqueeze(1).to_broadcast([128, 8, 128])
                    tt(G, AT[:, 8 * d:8 * d + 8, :], DT[:, 8 * d:8 * d + 8, :], inc_, ALU.mult, k)
                    for half in range(2):
                        rs = slice(64 * half, 64 * half + 64)
                        col = 64 * half + (0 if d else 63)
                        cp(V, BC[rs, 48 + 8 * d:56 + 8 * d].unsqueeze(2), DT[rs, 8 * d:8 * d + 8, col:col + 1], k)
                    yield
                kdt = (V.sem, V.n)
                kat = (G.sem, G.n)
                for t in range(2):
                    b = SP_.take()
                    for h in range(4):
                        kt = CV[:, 4 + h, 128 * t:128 * t + 128]
                        k = mm(b.t[:, 128 * h:128 * h + 128], kt, kt, h == 0, True, kcv, b.free, inc=h == 3)
                    for d in range(2):
                        for h in range(4):
                            o = 8 * d + 4 * t + h
                            k3 = stt(V, NL[:, o, :], b.t[:, 128 * h:128 * h + 128], BC[:, 16 + o:17 + o], DT[:, o, :],
                                     ALU.mult, ALU.mult, k, kdt)
                    b.free = [k3]
                    b = SP_.take()
                    for h in range(4):
                        k = mm(b.t[:, 128 * h:128 * h + 128], CV[:, 4 + h, 128 * t:128 * t + 128],
                               CV[:, h, 128 * t:128 * t + 128], h == 0, True, b.free, inc=h == 3)
                    for d in range(2):
                        o = 8 * d + 4 * t
                        b.free = [tt(V, AT[:, o:o + 4, :], r3(b.t, 4), AT[:, o:o + 4, :], ALU.mult, k, kat)]
                    yield
                idb = ident.unsqueeze(1).to_broadcast([128, 16, 128])
                cp(G, XM[:, :, :], idb)
                k = cp(V, XT[:, :, :], idb)
                kx = [(V.sem, V.n), (G.sem, G.n)]
                kxx = [kx] * 4
                for m in MS:
                    for q in range(4):
                        d = q // 2
                        g = slice(4 * q, 4 * q + 4)
                        mx = mask(m, 1 - d).unsqueeze(1).to_broadcast([128, 4, 128])
                        mt = mask(m, d).unsqueeze(1).to_broadcast([128, 4, 128])
                        b = SP_.take()
                        for i in range(4):
                            o = 4 * q + i
                            k = mm(b.t[:, 128 * i:128 * i + 128], NL[:, o, :], XM[:, o, :], i == 0, True, kxx[q],
                                   b.free, inc=i == 3)
                        if m == 1:
                            pred(XM[:, g, :], mx, r3(b.t, 4), k)
                            b.free = [(V.sem, V.n)]
                            kxx[q] = pred(XT[:, g, :], mt, NL[:, g, :])
                            yield
                            continue
                        k = act(Y[:, g, :], r3(b.t, 4), ACT.Copy, k)
                        b.free = [k]
                        yield
                        if m < 32:
                            b = SP_.take()
                            for i in range(4):
                                o = 4 * q + i
                                k2 = mm(b.t[:, 128 * i:128 * i + 128], XT[:, o, :], Y[:, o, :], i == 0, True, k,
                                        b.free, inc=i == 3)
                            kb1 = (b, k2)
                        b = SP_.take()
                        for i in range(4):
                            o = 4 * q + i
                            k2 = mm(b.t[:, 128 * i:128 * i + 128], Y[:, o, :], XT[:, o, :], i == 0, True, k, b.free,
                                    inc=i == 3)
                        if m < 32:
                            kb1[0].free = [pred(XM[:, g, :], mx, r3(kb1[0].t, 4), k2)]
                        b.free = [pred(XT[:, g, :], mt, r3(b.t, 4), k2)]
                        kxx[q] = b.free
                        yield
                kp = [(P.sem, P.n)]
                kxt = [(V.sem, V.n)]
                for d in range(2):
                    for t in range(2):
                        for h in range(4):
                            o = 8 * d + 4 * t + h
                            src = K3[:, t, 128 * h:128 * h + 128]
                            ts(V, KG[:, o, :], src, BC[:, 32 + o:33 + o], None, ALU.mult, None, kp, kbc, kkv)
                            ts(G, KD[:, o, :], src, BC[:, 48 + o:49 + o], None, ALU.mult, None, kp, kdt, kkv,
                               kxt)
                    tt(V, QD[:, 4 * d:4 * d + 4, :], CV[:, 0:4, :], EG[:, 4 * d:4 * d + 4, :], ALU.mult,
                       (A.sem, A.n))
                    yield
                kkg = [(V.sem, V.n), (G.sem, G.n)]
                for q in range(4):
                    b = SP_.take()
                    for i in range(4):
                        o = 4 * q + i
                        k = mm(b.t[:, 128 * i:128 * i + 128], KG[:, o, :], XT[:, o, :], i == 0, True, kkg, b.free,
                               inc=i == 3)
                    b.free = [act(KC[:, 4 * q:4 * q + 4, :], r3(b.t, 4), ACT.Copy, k, scale=-1.0)]
                    yield
                kkc = b.free
                OB = [HP.banks[0], HP.banks[1]]
                ofirst = [True, True]
                kss = [None, None]
                kvw = [None, None]
                UB = [SP_.banks[0], SP_.banks[1]]
                VB = [SP_.banks[2], HP.banks[2]]
                for i in range(4):
                    kv2 = [None, None]
                    for d in range(2):
                        n = 3 - i if d else i
                        t, r0 = n // 2, 64 * (n % 2)
                        b = VB[d]
                        for h in range(4):
                            o = 8 * d + 4 * t + h
                            k = mm(b.t[r0:r0 + 64, 128 * h:128 * h + 128], XT[r0:r0 + 64, o, r0:r0 + 64],
                                   V3[r0:r0 + 64, t, 128 * h:128 * h + 128], h == 0, i == 0, kxt, kkv, b.free, kkc,
                                   inc=True)
                            if i:
                                k = mm(b.t[r0:r0 + 64, 128 * h:128 * h + 128], KC[:, o, r0:r0 + 64],
                                       SS[:, 4 * d + h, :], False, True, kss[d], kkc, inc=True)
                        o = 8 * d + 4 * t
                        vw = r3(VW[d], 4)
                        kv2[d] = tt(V, vw[r0:r0 + 64], r3(b.t, 4)[r0:r0 + 64],
                                    BC[r0:r0 + 64, o:o + 4].unsqueeze(2).to_broadcast([64, 4, 128]), ALU.mult, k,
                                    kvw[d])
                        b.free = [kv2[d]]
                    yield
                    for d in range(2):
                        n = 3 - i if d else i
                        t, r0 = n // 2, 64 * (n % 2)
                        vw = r3(VW[d], 4)
                        if i < 3:
                            b = UB[d]
                            for h in range(4):
                                o = 8 * d + 4 * t + h
                                k = mm(b.t[:, 128 * h:128 * h + 128], KD[r0:r0 + 64, o, :], vw[r0:r0 + 64, h, :],
                                       h == 0, True, kv2[d], b.free, kkg, inc=h == 3)
                        for h in range(4):
                            o = 8 * d + 4 * t + h
                            dst = OB[t].t[:, 128 * h + r0:128 * h + r0 + 64]
                            if i:
                                k1 = mm(dst, SS[:, 4 * d + h, :], QD[:, 4 * d + h, 64 * n:64 * n + 64], ofirst[t], True,
                                        kss[d], kkg, OB[t].free, inc=True)
                                ofirst[t] = False
                            k1 = mm(dst, vw[r0:r0 + 64, h, :], AT[r0:r0 + 64, o, r0:r0 + 64], ofirst[t], True,
                                    kv2[d], OB[t].free, inc=True)
                            ofirst[t] = False
                        kvw[d] = k1
                        if i < 3:
                            e = 64 * n + (0 if d else 63)
                            for h in range(4):
                                s = SS[:, 4 * d + h, :]
                                u = b.t[:, 128 * h:128 * h + 128]
                                if i == 0:
                                    k2 = cp(V, s, u, k)
                                else:
                                    k2 = stt(V, s, s, EG[:, 4 * d + h, e:e + 1], u, ALU.mult, ALU.add, k, k1)
                            b.free = [k2]
                            kss[d] = k2
                        yield
                while "za3" not in done:
                    yield
                for t in range(2):
                    O3 = r3(R, 4)
                    k = act(O3, r3(OB[t].t, 4), ACT.Copy, k1, (V.sem, V.n))
                    OB[t].free = [k]
                    Q2 = VW[t]
                    k = tt(V, Q2, R, R, ALU.mult, k, k1)
                    b = SP_.take()
                    k = mm(b.t, o128, Q2, True, True, k, b.free, inc=True)
                    b.free = [rstd_big(Q2, b.t, k)]
                    k = stt(V, R, R, par[:, PB_DN:PB_DN + 1], Q2, ALU.mult, ALU.mult, b.free)
                    z = ZA[:, :, 128 * t:128 * t + 128]
                    done["yd"] = stt(V, z, O3, 0.5, z, ALU.mult, ALU.mult, done["za3"])
                    yield

            def scr(n):
                return al(n)

            weave((dense(), 1), (delta(scr), 3), (confconv(scr), 2))
            top[0] = s0
            allk = [(V.sem, V.n), (A.sem, A.n), (P.sem, P.n), (G.sem, G.n)]
            DP2 = Pool(PS)
            SIG = [al(256) for _ in range(2)]
            TM = al(256)
            gh = al(16)
            mT = r3(al(2048), 8)
            fr = al(1024)
            zz = al(1024)
            f2 = al(4)
            kgh = ts(V, gh, par[:, PB_GB:PB_GB + 16], 0.5, None, ALU.mult, None, allk)
            it = 0
            free_sig = [None, None]
            ktm = None
            ys = [(ZA, done["yd"]), (CA, done["yb"])]
            for j in range(2):
                for bi in range(2):
                    w, kw = use(f"b{l}m{bi}{j}")
                    w = rows_of(w, 8)
                    wb, kwb = use(f"b{l}b{bi}{j}")
                    wb = rows_of(wb, 4)
                    Yt, ky = ys[bi]
                    for c in range(4):
                        b = DP2.take()
                        k = feat(b, w, 8, 128 * c, 128, hT, 0, 256, 8, [kw, b.free])
                        sg = SIG[it % 2]
                        q = 8 * bi + 4 * j + c
                        k = act(sg, b.t[:, 0:256], ACT.Tanh, k, free_sig[it % 2], kgh, scale=0.5, bias=gh[:, q:q + 1])
                        b.free = [k]
                        b = DP2.take()
                        k2 = feat(b, wb, 4, 128 * c, 128, Yt, 0, 256, 4, [kwb, ky, b.free])
                        m = mT[:, 4 * j + c, :]
                        if bi == 0:
                            k3 = stt(V, m, sg, 1.0, b.t[:, 0:256], ALU.add, ALU.mult, k, k2, allk)
                        else:
                            k3 = stt(V, TM, sg, 1.0, b.t[:, 0:256], ALU.add, ALU.mult, k, k2, ktm)
                            ktm = tt(G, m, m, TM, ALU.add, k3)
                        b.free = [k3]
                        free_sig[it % 2] = k3
                        it += 1
                    release(f"b{l}m{bi}{j}", k2)
                    release(f"b{l}b{bi}{j}", k2)
            km = [(V.sem, V.n), (G.sem, G.n)]
            if l == 1:
                k_fr = dma(fr, rfin.partition_broadcast(128), km)
            w0, kw0 = use(f"b{l}o0")
            w1, kw1 = use(f"b{l}o1")
            ws = [(rows_of(w0, 8), kw0), (rows_of(w1, 8), kw1)]
            stores = []
            for t in range(2):
                for hf in range(2):
                    b = DP2.take()
                    w, kw = ws[hf]
                    k = token(b, w, 0, 512, mT, 128 * t, [kw, km, b.free])
                    x = X[:, 1024 * t + 512 * hf:1024 * t + 512 * hf + 512]
                    b.free = [stt(V, x, b.t, 0.5, x, ALU.mult, ALU.add, k)]
                if l == 1:
                    x = X[:, 1024 * t:1024 * t + 1024]
                    k = act(zz, x, ACT.Square, b.free, (V.sem, V.n), acc=f2[:, 0:1])
                    k = ts(V, f2[:, 1:2], f2[:, 0:1], 1.0 / 1024, None, ALU.mult, None, k)
                    kr = rstd_small(f2[:, 2:3], f2[:, 1:2], k)
                    ts(V, x, x, f2[:, 2:3], None, ALU.mult, None, kr)
                    k = tt(V, x, x, fr, ALU.mult, k_fr)
                    stores.append(dma(out[128 * t:128 * t + 128, :], x, k))
            lastp = (P.sem, P.n)
            release(f"b{l}o0", lastp)
            release(f"b{l}o1", lastp)
            if stores:
                S.todo.append((stores, None, False))
            return [(V.sem, V.n), (G.sem, G.n), (P.sem, P.n), (A.sem, A.n)]

        k = layer_a(0, None)
        k = layer_a(1, k)
        k = layer_b(0, k)
        layer_b(1, k)

        def play(E, eng):
            for need, fn, inc in E.todo:
                for s, v in need:
                    eng.wait_ge(s, v)
                if fn is None:
                    continue
                ins = fn(eng)
                if inc:
                    ins.then_inc(E.sem, 1)

        block = ctx.enter_context(nc.Block())

        @block.sync
        def _(e):
            play(S, e)

        @block.gpsimd
        def _(e):
            play(G, e)

        @block.scalar
        def _(e):
            play(A, e)

        @block.tensor
        def _(e):
            play(P, e)

        @block.vector
        def _(e):
            play(V, e)


def make_consts():
    c = np.zeros((128, C_W), np.float32)
    i = np.arange(128)
    c[:, C_ID:C_ID + 128] = np.eye(128)
    for n, m in enumerate(MS):
        a = i[:, None]
        b = i[None, :]
        mk = (a // (2 * m) == b // (2 * m)) & ((a // m) % 2 == 0) & ((b // m) % 2 == 1)
        c[:, C_MASK + 256 * n:C_MASK + 256 * n + 128] = mk
        c[:, C_MASK + 256 * n + 128:C_MASK + 256 * n + 256] = mk.T
    c[:, C_TWO:C_TWO + 128] = 2 * np.eye(128)
    fr = (np.float32(10000.0) ** (-np.arange(0, 32, 2, dtype=np.float32) / np.float32(32))).astype(np.float32)
    tok = np.arange(256)
    for t in range(2):
        p = tok[128 * t:128 * t + 128]
        ar = ((p // 64).astype(np.float32)[:, None] * fr).astype(np.float32)
        ac = ((p % 64).astype(np.float32)[:, None] * fr).astype(np.float32)
        c[:, C_COS + 64 * t:C_COS + 64 * t + 64] = np.concatenate([np.cos(ar)] * 2 + [np.cos(ac)] * 2, 1)
        c[:, C_SIN + 64 * t:C_SIN + 64 * t + 64] = np.concatenate([-np.sin(ar), np.sin(ar), -np.sin(ac), np.sin(ac)], 1)
    c[:, C_SCAN:C_SCAN + 512] = (np.arange(512) % 64 != 0)
    c[:, C_O128:C_O128 + 128] = 1.0 / 128
    c[:, C_O512:C_O512 + 128] = 1.0 / 512
    c[:, C_ONE:C_ONE + 128] = 1.0
    same = (i[:, None] // 64) == (i[None, :] // 64)
    c[:, C_INC:C_INC + 128] = same & (i[:, None] <= i[None, :])
    c[:, C_INC + 128:C_INC + 256] = same & (i[:, None] >= i[None, :])
    c[:, C_COL:C_COL + 4] = [EPS, 1.0, 0.0, -0.5]
    return c


def lay(w):
    return w.reshape(-1, 128, w.shape[1]).transpose(1, 0, 2).reshape(128, -1)


def cols(v):
    return v.reshape(-1, 128).T


def kernel(**inputs):
    import concourse.bacc as bacc
    from concourse.bass_utils import run_bass_kernel_spmd as run

    I = {k: np.asarray(v) for k, v in inputs.items()}
    perm = np.concatenate([np.arange(64 * h, 64 * h + 64) for h in HEADS])
    pieces = {}
    for l in range(2):
        wi = I["w_in"][l]
        for j in range(6):
            pieces[f"a{l}ada{j}"] = lay(I["w_ada"][l][:, 512 * j:512 * j + 512])
        pieces[f"a{l}qa"] = lay(wi[:, 0:512][:, perm])
        pieces[f"a{l}kv"] = lay(np.concatenate([wi[:, 512:768], wi[:, 2304:2336]], 1))
        for n, o in (("gqk", 1280), ("gv", 1792), ("gg", 2336), ("su", 2848), ("sv", 3360), ("sg", 3872)):
            pieces[f"a{l}{n}"] = lay(wi[:, o:o + 512])
        pieces[f"a{l}ag"] = lay(wi[:, 768:1280][:, perm])
        for j in range(2):
            for n, b, wb in ((0, "a", I["w_br_attn"][l][perm]), (1, "g", I["w_br_gla"][l]), (2, "s", I["w_br_sgu"][l])):
                o = 4384 + 1024 * n + 512 * j
                pieces[f"a{l}m{b}{j}"] = lay(wi[:, o:o + 512])
                pieces[f"a{l}b{b}{j}"] = lay(wb[:, 512 * j:512 * j + 512])
            pieces[f"a{l}o{j}"] = lay(I["w_out"][l][:, 512 * j:512 * j + 512])
        wi = I["w_in_2"][l]
        for j in range(3):
            pieces[f"b{l}q{j}"] = lay(wi[:, 512 * j:512 * j + 512])
        ab = np.zeros((1024, 100), np.float32)
        for n in range(4):
            ab[:, 32 * n:32 * n + 4] = wi[:, 2048 + 4 * n:2052 + 4 * n]
        pieces[f"b{l}ab"] = lay(ab)
        for n, o in (("za", 1536), ("cv", 2064), ("cg", 2576), ("zb", 3088)):
            pieces[f"b{l}{n}"] = lay(wi[:, o:o + 512])
        for j in range(2):
            for b, wb in ((0, I["w_dn_out_2"][l]), (1, I["w_cf_out_2"][l])):
                o = 3600 + 1024 * b + 512 * j
                pieces[f"b{l}m{b}{j}"] = lay(wi[:, o:o + 512])
                pieces[f"b{l}b{b}{j}"] = lay(wb[:, 512 * j:512 * j + 512])
            pieces[f"b{l}o{j}"] = lay(I["w_out_2"][l][:, 512 * j:512 * j + 512])
    wf = np.concatenate([pieces[n].reshape(-1) for n, _ in PLAN])
    assert wf.size == 128 * sum(w for _, w in PLAN)

    pa = np.zeros((2, 128, PA_W), np.float32)
    ra = np.zeros((2, RA_W + 1024), np.float32)
    rp = np.zeros((2, 2048), np.float32)
    pb = np.zeros((2, 128, PB_W), np.float32)
    for l in range(2):
        pa[l][:, 0:16] = cols(I["b_ada"][l][0:2048])
        pa[l][:, PA_AB:PA_AB + 2] = cols(I["gla_ab_f"][l])
        pa[l][:, PA_AB + 2:PA_AB + 4] = cols(I["gla_ab_b"][l])
        pa[l][:, PA_ON] = I["gla_o_norm"][l]
        pa[l][0:16, PA_PM:PA_PM + 256] = I["gla_a2_f"][l]
        pa[l][16:32, PA_PM + 256:PA_PM + 512] = I["gla_a2_b"][l]
        pa[l][32, PA_PM:PA_PM + 512] = I["sgu_b"][l].reshape(-1)
        pa[l][:, PA_SW:PA_SW + 512] = I["sgu_w"][l].transpose(2, 0, 1).reshape(128, 512)
        ra[l][0:512] = np.tile(I["attn_q_norm"][l], 8)
        ra[l][512:640] = np.tile(I["attn_k_norm"][l], 2)
        ra[l][RA_LG:RA_LG + 512] = I["sgu_ln_g"][l]
        ra[l][RA_LB:RA_LB + 512] = I["sgu_ln_b"][l]
        ra[l][RA_W:RA_W + 1024] = I["b_ada"][l][2048:3072]
        rp[l][0:1024] = I["post_ln_g"][l]
        rp[l][1024:2048] = I["post_ln_b"][l]
        q = pb[l]
        q[:, PB_NW:PB_NW + 8] = cols(I["norm_w_2"][l])
        q[:, PB_CW:PB_CW + 60] = I["qkv_conv_w_2"][l].T.reshape(12, 128, 5).transpose(1, 0, 2).reshape(128, 60)
        q[:, PB_FW:PB_FW + 124] = I["cf_conv_w_2"][l].T.reshape(4, 128, 31).transpose(1, 0, 2).reshape(128, 124)
        q[:, PB_FB:PB_FB + 4] = cols(I["cf_conv_b_2"][l])
        q[:, PB_LW:PB_LW + 4] = cols(I["cf_ln_w_2"][l])
        q[:, PB_LB:PB_LB + 4] = cols(I["cf_ln_b_2"][l])
        q[:, PB_GB:PB_GB + 16] = cols(I["gate_b_2"][l])
        q[:, PB_DN] = I["dn_norm_w_2"][l]
        for d in range(2):
            q[32 * d:32 * d + 4, PB_AL] = I["a_log_2"][l][d]
            q[32 * d:32 * d + 4, PB_DT] = I["dt_bias_2"][l][d]

    both = np.concatenate([I["ctx"][0], I["x"][0]], 0)
    data = {
        "wf": wf, "consts": make_consts(),
        "cT": np.stack([cols(I["c"][0]), cols(I["c_ctx"])], 2).reshape(128, 16),
        "xin": both.reshape(4, 128, 1024).transpose(1, 0, 2).reshape(128, 4096),
        "xinT": both.T.reshape(8, 128, 512).transpose(1, 0, 2).reshape(128, 4096),
        "pa": pa, "ra": ra, "rp": rp, "pb": pb, "rfin": I["final_norm_w_2"],
    }
    nc = bacc.Bacc("TRN2", target_bir_lowering=False, num_devices=1)
    arrays, args = {}, []
    for name, a in data.items():
        a = np.ascontiguousarray(a)
        arrays[f"in_{name}"] = a
        args.append(nc.dram_tensor(f"in_{name}", a.shape, mybir.dt.from_np(a.dtype), kind="ExternalInput").ap())
    o = nc.dram_tensor("out_0", (256, 1024), F, kind="ExternalOutput").ap()
    build_program(nc, *args, o)
    r = run(nc, [arrays], core_ids=[0])
    return r.results[0]["out_0"].reshape(1, 256, 1024)
```

```python
from contextlib import ExitStack

import numpy as np

import concourse.bass as bass
from concourse import mybir

F = mybir.dt.float32
U32 = mybir.dt.uint32
ALU = mybir.AluOpType
ACT = mybir.ActivationFunctionType
AX = mybir.AxisListType.X

D = 1024
ALPHA = 4.0 ** 0.25
X_T = 53200 - 4096
EPS = 1e-6
MS = (1, 2, 4, 8, 16, 32)
HEADS = (0, 4, 1, 5, 2, 6, 3, 7)

COST = {"V": (0.15, 0.001), "A": (0.25, 0.0008), "G": (0.2, 0.002), "P": (0.03, 0.0017)}
LATENCY = 0.1
SLACK = 0.3
GFIRST = [False, False]

UNIT = 2048
NU = 7

C_ID, C_MASK, C_TWO, C_COS, C_SIN, C_SCAN, C_O128, C_O512, C_ONE, C_INC, C_COL = (
    0, 128, 1664, 1792, 1920, 2048, 2560, 2688, 2816, 2944, 3200)
C_STK = 3204
C_W = 3208

PA_BADA, PA_AB, PA_ON, PA_LG, PA_PM, PA_SW, PA_W = 0, 24, 28, 29, 40, 552, 1064
RA_QK, RA_W = 0, 640
PB_NW, PB_CW, PB_FW, PB_FB, PB_LW, PB_LB, PB_GB, PB_DN, PB_AL, PB_DT, PB_W = (
    0, 8, 68, 192, 196, 200, 204, 220, 221, 222, 224)


ADA = [(0, 4), (0, 5)] + [(1, j) for j in range(6)]


EARLY = [[("a", 0)], [("a", 0), ("g", 0), ("s", 0), ("a", 1), ("g", 1)]]


def plan_a(l):
    out = [(f"a{l}{n}", w) for n, w in (("qa", 4096), ("kv", 8 * 288), ("gqk", 4096), ("gv", 4096), ("ag", 4096),
                                        ("gg", 4096), ("su", 4096), ("sg", 4096), ("sv", 4096))]
    if l == 0:
        for n, (m, j) in enumerate(ADA):
            out.insert(2 * n + 1, (f"a{m}ada{j}", 4096))
    out += [(f"a{l}m{b}{j}", 4096) for b, j in EARLY[l]]
    for j in range(2):
        for b in "ags":
            if (b, j) not in EARLY[l]:
                out += [(f"a{l}m{b}{j}", 4096)]
            out += [(f"a{l}b{b}{j}", 2048)]
    return out + [(f"a{l}o{j}", 4096) for j in range(2)]


def plan_b(l):
    out = [(f"b{l}{n}", w) for n, w in (("q0", 4096), ("q1", 4096), ("q2", 4096), ("ab", 800), ("za", 4096),
                                        ("cv", 4096), ("cg", 4096), ("zb", 4096))]
    out += [(f"b{l}m{b}{j}", 4096) for j in range(2) for b in range(2)]
    out += [(f"b{l}b{b}{j}", 2048) for j in range(2) for b in range(2)]
    return out + [(f"b{l}o{j}", 4096) for j in range(2)]


PLAN = [(f"a0ada{j}", 4096) for j in (0, 2, 1, 3)] + plan_a(0) + plan_a(1) + plan_b(0) + plan_b(1)


class Engine:

    def __init__(self, sem, chained, plan, fixed, per):
        self.sem, self.chained, self.n, self.seen, self.todo = sem, chained, 0, {}, []
        self.plan, self.fixed, self.per, self.t = plan, fixed, per, 0.0

    def put(self, fn, waits, inc=True, size=0):
        flat = []

        def add(w):
            if w is None:
                return
            if isinstance(w, list):
                for x in w:
                    add(x)
            else:
                flat.append(w)

        add(list(waits))
        if self.chained and self.n:
            flat.append((self.sem, self.n))
        need = {}
        for sem, v in flat:
            if self.seen.get(id(sem), 0) < v and need.get(id(sem), (sem, 0))[1] < v:
                need[id(sem)] = (sem, v)
        for sem, v in need.values():
            self.seen[id(sem)] = v
        if inc:
            self.n += 1
        self.t = max([self.t] + [self.plan.at.get((id(sem), v), 0.0) for sem, v in need.values()])
        self.t += self.fixed + self.per * size
        if inc:
            self.plan.at[(id(self.sem), self.n)] = self.t + LATENCY
            self.plan.emitted = max(self.plan.emitted, self.t + LATENCY)
        self.todo.append((list(need.values()), fn, inc))
        return (self.sem, self.n)


class Plan:

    def __init__(self):
        self.at, self.emitted = {}, 0.0


class Bank:
    def __init__(self, t):
        self.t, self.free = t, []


class Pool:

    def __init__(self, banks):
        self.banks, self.i = banks, 0

    def take(self):
        b = self.banks[self.i % len(self.banks)]
        self.i += 1
        return b


def weave(plan, P, *parts):
    live = [[g, 0.0, False] for g in parts]
    filler = live[-1]
    while live:
        able = [it for it in live if not it[2]]
        it = next((x for x in able if x[1] <= P.t + SLACK), None) or min(able, key=lambda x: x[1])
        plan.emitted = 0.0
        try:
            more = next(it[0])
        except StopIteration:
            live.remove(it)
            continue
        if more == "blocked":
            it[2] = True
            if all(x[2] for x in live):
                raise RuntimeError("every stream waits")
            continue
        it[1] = P.t if it is filler else plan.emitted
        for x in live:
            x[2] = False


def drain(g):
    for _ in g:
        pass


def build_program(nc, wf, consts, cT, xin, xinT, pa, ra, rpost, pb, rfin, out):
    with ExitStack() as ctx:
        arena = ctx.enter_context(nc.sbuf_tensor("arena", [128, 53200], F))
        top = [0]

        def al(n):
            o = top[0]
            top[0] += n
            assert top[0] <= 53200, top[0]
            return arena[:, o:o + n]

        def sem(name):
            return ctx.enter_context(nc.semaphore(name))

        PS = [Bank(ctx.enter_context(nc.psum_tensor(f"ps{i}", [128, 512], F))[:, :]) for i in range(8)]

        plan = Plan()
        V = Engine(sem("s_v"), True, plan, *COST["V"])
        A = Engine(sem("s_a"), True, plan, *COST["A"])
        G = Engine(sem("s_g"), True, plan, *COST["G"])
        P = Engine(sem("s_p"), False, plan, *COST["P"])
        S = Engine(sem("s_sp"), False, plan, 0.0, 0.0)
        dman = [0]

        def size_of(ap):
            return int(np.prod(ap.shape[1:]))

        def mm(o, l, r, start, stop, *w, inc=False):
            return P.put(lambda e: e.matmul(o, l, r, start=start, stop=stop, skip_group_check=True), w, inc, size_of(o))

        def tr(o, i, idn, *w, inc=False):
            return P.put(lambda e: e.transpose(o, i, idn), w, inc, size_of(o))

        def tt(E, o, a, b, op, *w):
            return E.put(lambda e: e.tensor_tensor(o, a, b, op), w, size=size_of(o) * (100 if op == ALU.pow else 1))

        def ts(E, o, a, s1, s2, op0, op1, *w):
            if s2 is None:
                return E.put(lambda e: e.tensor_scalar(o, a, s1, None, op0), w, size=size_of(o))
            return E.put(lambda e: e.tensor_scalar(o, a, s1, s2, op0, op1), w, size=size_of(o))

        def stt(E, o, a, s, b, op0, op1, *w):
            return E.put(lambda e: e.scalar_tensor_tensor(out=o, in0=a, scalar=s, in1=b, op0=op0, op1=op1), w,
                         size=size_of(o))

        def act(o, i, f, *w, bias=None, scale=None, acc=None):
            kw = {}
            if bias is not None:
                kw["bias"] = bias
            if scale is not None:
                kw["scale"] = scale
            if acc is not None:
                kw["accum_out"] = acc
            return A.put(lambda e: e.activation(o, i, f, **kw), w, size=size_of(o))

        def cp(E, o, i, *w):
            return E.put(lambda e: e.tensor_copy(o, i), w, size=size_of(o))

        def ms(E, o, v, *w):
            return E.put(lambda e: e.memset(o, v), w, size=size_of(o))

        def pred(o, mask, data, *w):
            return V.put(lambda e: e.copy_predicated(o, mask, data), w, size=size_of(o))

        def dma(o, i, *w, s=None):
            if s is None:
                s = sem(f"s_d{dman[0]}")
                dman[0] += 1

            def go(e):
                e.dma_start(o, i).then_inc(s, 16)

            S.put(go, w, inc=False)
            if (id(s), 16) not in plan.at:
                st["t"] = max(st["t"], P.t) + size_of(o) * o.shape[0] * 4 / 330e3
                plan.at[(id(s), 16)] = st["t"] + 2.0
            return (s, 16)

        def r3(ap, n):
            return ap.rearrange("p (a b) -> p a b", a=n)

        ring = al(NU * UNIT)
        st = {"next": 0, "at": 0, "off": 0, "t": 0.0}
        usem = [sem(f"s_u{i}") for i in range(NU)]
        ucount = [0] * NU
        ufree = [[] for _ in range(NU)]
        ubusy = [False] * NU
        loaded = {}

        def fill(most=len(PLAN)):
            while st["next"] < len(PLAN) and most:
                most -= 1
                name, w = PLAN[st["next"]]
                k = -(-w // UNIT)
                at = st["at"] if st["at"] + k <= NU else 0
                if any(ubusy[at:at + k]):
                    return
                for u in range(at, at + k):
                    ubusy[u] = True
                off = st["off"]
                dst, src = ring[:, at * UNIT:at * UNIT + w], wf[off:off + 128 * w].rearrange("(p n) -> p n", p=128)
                waits = [t for u in range(at, at + k) for t in ufree[u]]
                dma(dst, src, waits, s=usem[at])
                ucount[at] += 16
                loaded[name] = (dst, (usem[at], ucount[at]), at, k)
                st["t"] = max([st["t"], P.t] + [plan.at.get((id(a), v), 0.0) for a, v in waits]) + 128 * w * 4 / 330e3
                plan.at[(id(usem[at]), ucount[at])] = st["t"] + 2.0
                st["next"] += 1
                st["at"] = (at + k) % NU
                st["off"] += 128 * w

        def use(name):
            fill()
            return loaded[name][0], loaded[name][1]

        def release(name, tok):
            _, _, at, k = loaded[name]
            for u in range(at, at + k):
                ubusy[u] = False
                ufree[u] = [tok]
            fill()

        cst = al(C_W)
        ident = cst[:, C_ID:C_ID + 128]

        def mask(m, swapped):
            o = C_MASK + (2 * MS.index(m) + swapped) * 128
            return cst[:, o:o + 128].bitcast(U32)

        two = cst[:, C_TWO:C_TWO + 128]
        o128 = cst[:, C_O128:C_O128 + 128]
        o512 = cst[:, C_O512:C_O512 + 128]
        ones = cst[:, C_ONE:C_ONE + 128]
        eps = cst[:, C_COL:C_COL + 1]
        one = cst[:, C_COL + 1:C_COL + 2]
        zero = cst[:, C_COL + 2:C_COL + 3]
        mhalf = cst[:, C_COL + 3:C_COL + 4]
        X = al(2048)
        cc = al(16)
        cs = al(16)
        PT4 = X[:, 0:512]
        SCOL = [al(48), al(48)]
        BADA = al(48)
        base = top[0]
        k_c = dma(cc, cT)
        fill(1)
        k_bada = [dma(BADA[:, 24 * l:24 * l + 24], pa[l][:, 0:24]) for l in range(2)]
        k_cst = dma(cst, consts)
        fill(2)
        k_xt = dma(arena[:, X_T:X_T + 4096], xinT)
        fill()
        act(cs, cc, ACT.Tanh, k_c, scale=0.5)
        k = stt(V, cs, cs, 1.0, cc, ALU.add, ALU.mult, (A.sem, A.n), k_c)
        k_cs = ts(V, cs, cs, 0.5, None, ALU.mult, None, k)
        k_pt4 = [ms(V, PT4, 0.0)]
        cs3 = r3(cs, 8)

        def await_constants(*engines):
            for E in engines:
                E.todo.append(([k_cst], None, False))
                E.seen[id(k_cst[0])] = 16
                E.t = max(E.t, plan.at[(id(k_cst[0]), 16)])

        def rows_of(w, n):
            return w.rearrange("p (k n) -> p k n", k=n)

        def feat(bank, w, n, c0, cols, hT, t0, t1, nk, waits, m=128, o=0, start=True, stop=True, kh=None):
            tok = None
            for k in range(nk):
                tok = mm(bank.t[0:m, o:o + t1 - t0], w[:, k, c0:c0 + m], hT[:, k, t0:t1],
                         start and k == 0, stop and k == nk - 1, waits if k == 0 else None, kh[k] if kh else None,
                         inc=(k == nk - 1))
            return tok

        def token(bank, w, c0, c1, hT, t0, waits, nk=8, kh=None):
            tok = None
            for k in range(nk):
                tok = mm(bank.t[:, 0:c1 - c0], hT[:, k, t0:t0 + 128], w[:, k, c0:c1],
                         k == 0, k == nk - 1, waits if k == 0 else None, kh[k] if kh else None, inc=(k == nk - 1))
            return tok

        def ada(pool, js):
            for l, j in js:
                sc3 = r3(SCOL[l], 24)
                w, kw = use(f"a{l}ada{j}")
                w = rows_of(w, 8)
                b = pool.take()
                for kk in range(8):
                    g = 32 * (kk % 4)
                    k = mm(b.t[g:g + 2, :], cs3[:, kk, :], w[:, kk, :], kk < 4, kk >= 4,
                           [kw, k_cs, b.free] if kk == 0 else None, inc=kk >= 4)
                release(f"a{l}ada{j}", k)
                for g in range(4):
                    kr = act(PT4[32 * g:32 * g + 2, :], b.t[32 * g:32 * g + 2, :], ACT.Copy, k, k_pt4[0])
                b.free = [kr]
                yield
                b = pool.take()
                for i in range(4):
                    k = mm(b.t[:, 2 * i:2 * i + 2], PT4[:, 128 * i:128 * i + 128], cst[:, C_STK:C_STK + 2], i == 0, True,
                           kr, b.free, inc=i == 3)
                k_pt4[0] = k
                one_ = 1.0 if j in (2, 3) else 0.0
                b.free = [stt(V, sc3[:, 4 * j:4 * j + 4, :], r3(b.t[:, 0:8], 4), one_,
                              BADA[:, 24 * l + 4 * j:24 * l + 4 * j + 4].unsqueeze(2).to_broadcast([128, 4, 2]),
                              ALU.add, ALU.add, k, k_bada[l])]
                yield

        def rstd_small(o, i, *w):
            n = i.shape[1]
            a = ts(G, o, i, eps, None, ALU.add, None, *w)
            return tt(G, o, o, mhalf.to_broadcast([128, n]), ALU.pow, a)

        def rstd_big(o, i, *w):
            act(o, i, ACT.Ln, *w, bias=eps)
            return act(o, o, ACT.Exp, scale=-0.5)

        def layer_a(l, k_x):
            top[0] = base
            hT = r3(al(4096), 8)
            qkv_gv = al(5120)
            QKV = r3(qkv_gv[:, 0:3072], 4)
            GV = r3(qkv_gv[:, 3072:5120], 4)
            mT = r3(qkv_gv[:, 0:4096], 8)
            AG, GG, SG = (r3(al(2048), 4) for _ in range(3))
            GQ, GK = (r3(al(1024), 2) for _ in range(2))
            par = al(PA_SW)
            row = al(640)
            TH = al(512)
            TH2 = al(512)
            s0 = top[0]
            l0 = 0 if l == 0 else 256
            tiles = range(4) if l == 0 else range(2, 4)

            k_par = dma(par, pa[l][:, 0:PA_SW], k_x)
            k_row = dma(row, ra[l][0:640].partition_broadcast(128), k_x)
            PM = par[:, PA_PM:PA_PM + 512]
            DP, AP, GP = Pool(PS[0:3]), Pool(PS[3:5]), Pool(PS[5:8])
            VN = [al(512) for _ in range(2)]
            SW = al(512)
            BT = al(512)
            bs = al(16)
            s0 = top[0]
            k_sw = dma(SW, pa[l][:, PA_SW:PA_W], k_x)
            k_bs = dma(BT[65:66, :], pa[l][96:97, PA_PM:PA_PM + 512], k_x)

            if l == 0:
                await_constants(A)
                drain(ada(DP, [(0, j) for j in (0, 2, 1, 3)]))
                await_constants(V, G)
            k_sc = (V.sem, V.n)
            sc3 = r3(SCOL[l], 24)

            k_hk = []
            if l == 0:
                top[0] = s0
                assert s0 <= X_T
                xT = r3(arena[:, X_T:X_T + 4096], 8)
                for kk in range(8):
                    k_hk.append([])
                    for s in range(2):
                        c = 1 - s
                        E = V if s else G
                        k_hk[kk] += [ts(E, hT[:, kk, 256 * s:256 * s + 256], xT[:, kk, 256 * s:256 * s + 256],
                           sc3[:, 8 + kk, c:c + 1], sc3[:, kk, c:c + 1], ALU.mult, ALU.add, k_xt, k_sc)]
            else:
                for kk in range(8):
                    b = GP.take()
                    for t in range(4):
                        src = (CX if t < 2 else X)[:, 1024 * (t % 2) + 128 * kk:1024 * (t % 2) + 128 * kk + 128]
                        k = tr(b.t[:, 128 * t:128 * t + 128], src, ident, k_x, b.free, inc=t == 3)
                    for s in range(2):
                        c = 1 - s
                        b.free = [ts(V, hT[:, kk, 256 * s:256 * s + 256], b.t[:, 256 * s:256 * s + 256],
                                     sc3[:, 8 + kk, c:c + 1], sc3[:, kk, c:c + 1], ALU.mult, ALU.add, k, k_sc)]
                    k_hk.append(b.free)
            k_h = [(V.sem, V.n), (G.sem, G.n)]
            top[0] = s0
            done = {}

            later = ada(DP, ADA) if l == 0 else iter(())

            def ada_next():
                for _ in range(2 if done.get("ada") else 1):
                    next(later, None)
                done["ada"] = True
                yield

            early = {}
            if l == 0:
                spare = [X[:, 512 * c:512 * c + 512] for c in range(4)]
            else:
                spare = [qkv_gv[:, 256:512], qkv_gv[:, 768:1024], qkv_gv[:, 0:256], qkv_gv[:, 1024:1280]]
                spare += [y[:, c, 0:256] for y in (AG, GG, SG) for c in range(4)]
                spare += [GQ[:, c, 0:256] for c in range(2)]

            def dense():
                w, kw = use(f"a{l}qa")
                w = rows_of(w, 8)
                for t in tiles:
                    b = DP.take()
                    k = token(b, w, 0, 512, hT, 128 * t, [kw, b.free], kh=k_hk)
                    b.free = [act(QKV[:, t, 0:512], b.t, ACT.Copy, k)]
                    done[f"q{t}"] = b.free
                    yield
                release(f"a{l}qa", k)
                yield from ada_next()
                w, kw = use(f"a{l}kv")
                w = rows_of(w, 8)
                for t in range(4):
                    b = DP.take()
                    k = token(b, w, 0, 256, hT, 128 * t, [kw, b.free])
                    b.free = [act(QKV[:, t, 512:768], b.t[:, 0:256], ACT.Copy, k)]
                    done[f"kv{t}"] = b.free
                    yield
                b = DP.take()
                k = feat(b, w, 8, 256, 32, hT, 0, 512, 8, [b.free], m=32)
                b.free = [act(TH2[0:32, :], b.t[0:32, :], ACT.Copy, k)]
                done["lr"] = b.free
                release(f"a{l}kv", k)
                yield from ada_next()
                yield
                w, kw = use(f"a{l}gqk")
                w = rows_of(w, 8)
                for c in range(4):
                    b = DP.take()
                    k = feat(b, w, 8, 128 * c, 128, hT, l0 if c < 2 else 0, 512, 8, [kw, b.free])
                    if c < 2:
                        b.free = [act(GQ[:, c, l0:512], b.t[:, 0:512 - l0], ACT.Copy, k, scale=0.125)]
                    else:
                        b.free = [act(GK[:, c - 2, :], b.t, ACT.Copy, k)]
                    yield
                release(f"a{l}gqk", k)
                yield from ada_next()
                done["gqk"] = b.free
                w, kw = use(f"a{l}gv")
                w = rows_of(w, 8)
                for t in range(4):
                    b = DP.take()
                    k = token(b, w, 0, 512, hT, 128 * t, [kw, b.free])
                    b.free = [act(GV[:, t, :], b.t, ACT.Copy, k)]
                    if t == 3:
                        done["gv"] = b.free
                    yield
                release(f"a{l}gv", k)
                yield from ada_next()
                for name, dst in (("ag", AG), ("gg", GG)):
                    w, kw = use(f"a{l}{name}")
                    w = rows_of(w, 8)
                    for c in range(4):
                        b = DP.take()
                        k = feat(b, w, 8, 128 * c, 128, hT, l0, 512, 8, [kw, b.free])
                        n = 512 - l0
                        k1 = act(TH[:, 0:n], b.t[:, 0:n], ACT.Tanh, k, done.get("th"), scale=0.5)
                        k2 = stt(V, dst[:, c, l0:512], TH[:, 0:n], 1.0, b.t[:, 0:n], ALU.add, ALU.mult, k1)
                        b.free = [k2]
                        done["th"] = k2
                        done[f"{name}{c}"] = k2
                        yield
                    release(f"a{l}{name}", k)
                    yield from ada_next()
                n = 512 - l0
                for name in ("su", "sg"):
                    w, kw = use(f"a{l}{name}")
                    w = rows_of(w, 8)
                    for c in range(4):
                        b = DP.take()
                        k = feat(b, w, 8, 128 * c, 128, hT, l0, 512, 8, [kw, b.free])
                        g = SG[:, c, l0:512]
                        if name == "su":
                            b.free = [act(g, b.t[:, 0:n], ACT.Copy, k)]
                            done[f"su{c}"] = b.free
                        else:
                            k1 = act(TH[:, 0:n], b.t[:, 0:n], ACT.Tanh, k, done.get("th"), scale=0.5)
                            k2 = stt(V, TH[:, 0:n], TH[:, 0:n], 1.0, b.t[:, 0:n], ALU.add, ALU.mult, k1)
                            b.free = [k2]
                            done["th"] = tt(V, g, g, TH[:, 0:n], ALU.mult, done[f"su{c}"])
                            done["sg"] = done["th"]
                        yield
                    release(f"a{l}{name}", k)
                    yield from ada_next()
                w, kw = use(f"a{l}sv")
                w = rows_of(w, 8)
                b = DP.take()
                k = mm(b.t[0:1, :], ones[:, 0:1], SW, True, True, k_sw, b.free, inc=True)
                kr = cp(V, BT[64:65, :], b.t[0:1, :], k)
                b.free = [kr]
                b = DP.take()
                for g in range(4):
                    k = mm(b.t[:, 128 * g:128 * g + 128], PM[64:66, 128 * g:128 * g + 128],
                           BT[64:66, 128 * g:128 * g + 128], g == 0, True, kr, k_bs, k_par, b.free, inc=g == 3)
                kbt = act(BT, b.t, ACT.Copy, k)
                b.free = [kbt]
                yield
                for t in tiles:
                    x = VN[t % 2]
                    b = DP.take()
                    k = token(b, w, 0, 512, hT, 128 * t, [kw, b.free])
                    k = act(x, b.t, ACT.Copy, k, done.get(f"vn{t % 2}"), k_h)
                    b.free = [k]
                    V.put(lambda e, x=x: e.bn_stats(bs[:, 0:6], x), [k])
                    k = V.put(lambda e: e.bn_aggr(bs[:, 6:8], bs[:, 0:6]), [])
                    kr = rstd_small(bs[:, 8:9], bs[:, 7:8], k)
                    k = ts(V, x, x, bs[:, 6:7], bs[:, 8:9], ALU.subtract, ALU.mult, kr)
                    yield
                    b = DP.take()
                    for g in range(4):
                        k2 = mm(b.t[:, 128 * g:128 * g + 128], x[:, 128 * g:128 * g + 128],
                                SW[:, 128 * g:128 * g + 128], g == 0, True, k, k_sw, b.free, inc=g == 3)
                    done[f"vn{t % 2}"] = k2
                    y = TH[:, 0:512]
                    for g in range(4):
                        cg = slice(128 * g, 128 * g + 128)
                        k = stt(V, y[:, cg], b.t[:, cg], par[:, PA_LG + g:PA_LG + g + 1], BT[:, cg], ALU.mult, ALU.add,
                                k2, kbt, k_par)
                    b.free = [k]
                    z = SG[:, :, 128 * t:128 * t + 128]
                    done["th"] = done["ys"] = stt(V, z, r3(y, 4), 0.5, z, ALU.mult, ALU.mult)
                    yield
                release(f"a{l}sv", k2)
                yield from ada_next()
                for br, j in EARLY[l]:
                    w, kw = use(f"a{l}m{br}{j}")
                    w = rows_of(w, 8)
                    for c in range(4):
                        b = DP.take()
                        k = feat(b, w, 8, 128 * c, 128, hT, l0, 512, 8, [kw, b.free])
                        sg = spare[len(early)]
                        b.free = [act(sg, b.t[:, 0:n], ACT.Tanh, k, k_pt4[0], k_h, k_x, scale=0.5)]
                        early[(br, j, c)] = (sg, b.free)
                        yield
                    release(f"a{l}m{br}{j}", k)

            def attention(scr):
                stat = scr(10)
                KT = scr(512)
                QT = scr(512)
                Pb = [scr(512) for _ in range(2)]
                PT = [scr(1024) for _ in range(2)]
                sq, qk2 = PT[0][:, 0:640], PT[1][:, 0:640]
                small = [scr(4) for _ in range(2)]
                for t in range(4):
                    while f"kv{t}" not in done:
                        yield "blocked"
                    wq = done[f"q{t}"] if t in tiles else None
                    lo = 0 if t in tiles else 512
                    nh = (640 - lo) // 64
                    w = [wq, done[f"kv{t}"]]
                    x = QKV[:, t, lo:640]
                    x3 = r3(x, nh)
                    k = tt(G, sq[:, lo:640], x, x, ALU.mult, w, (V.sem, V.n))
                    k = V.put(lambda e, a=stat[:, lo // 64:10], b=r3(sq[:, lo:640], nh): e.tensor_reduce(a, b, AX, ALU.add),
                              [k, (G.sem, G.n)])
                    k = ts(V, stat[:, lo // 64:10], stat[:, lo // 64:10], 1.0 / 64, None, ALU.mult, None)
                    yield
                    kr = rstd_small(stat[:, lo // 64:10], stat[:, lo // 64:10], k)
                    tt(V, x, x, row[:, RA_QK + lo:RA_QK + 640], ALU.mult, k_row, w, kr)
                    k = tt(V, x3, x3, stat[:, lo // 64:10].unsqueeze(2).to_broadcast([128, nh, 64]), ALU.mult, kr)
                    if t >= 2:
                        cos = cst[:, C_COS + 64 * (t - 2):C_COS + 64 * (t - 1)].unsqueeze(1).to_broadcast([128, 10, 64])
                        sn = cst[:, C_SIN + 64 * (t - 2):C_SIN + 64 * (t - 1)]
                        x5 = x.rearrange("p (h a b c) -> p h a b c", h=10, a=2, b=2)
                        q5 = qk2.rearrange("p (h a b c) -> p h a b c", h=10, a=2, b=2)
                        s4 = sn.rearrange("p (a b c) -> p a b c", a=2, b=2)
                        for hf in range(2):
                            kg = tt(G, q5[:, :, :, hf, :], x5[:, :, :, 1 - hf, :],
                                    s4[:, :, hf, :].unsqueeze(1).to_broadcast([128, 10, 2, 16]), ALU.mult, k,
                                    done.get("qk2"))
                        k = tt(V, x3, x3, cos, ALU.mult, kg)
                        k = tt(V, x, x, qk2, ALU.add, kg)
                        done["qk2"] = k
                    done[f"n{t}"] = k
                    yield
                b = AP.take()
                for t in range(4):
                    k = tr(b.t[:, 128 * t:128 * t + 128], QKV[:, t, 512:640], ident, done[f"n{t}"], b.free, inc=t == 3)
                k_kt = cp(V, KT, b.t, k)
                b.free = [k_kt]
                yield
                pt_free = [None, None]
                units, ready, num = [], [], [0]

                def scores(c, s, p, i, k_qt):
                    L = 256 + 256 * s
                    t = 2 * s + i
                    b = AP.take()
                    k = mm(b.t[:, 0:L], QTs[c % 2][64 * p:64 * p + 64, 128 * t:128 * t + 128],
                           KT[64 * p:64 * p + 64, 0:L], True, True, k_qt, k_kt, b.free, inc=True)
                    done[f"qt{c % 2}"] = k
                    j = num[0] % 2
                    num[0] += 1
                    sm, pb, wp = small[j], Pb[j], done.get(f"pb{j}")
                    V.put(lambda e, o=sm[:, 0:1], x=b.t[:, 0:L]: e.reduce_max(o, x, AX), [k, wp])
                    k = ts(V, sm[:, 1:2], sm[:, 0:1], -0.125, None, ALU.mult, None)
                    k = act(pb[:, 0:L], b.t[:, 0:L], ACT.Exp, k, wp, bias=sm[:, 1:2], scale=0.125, acc=sm[:, 2:3])
                    b.free = [k]
                    return (c, s, p, i, j, k)

                def weights(u, kpt):
                    c, s, p, i, j, k = u
                    L = 256 + 256 * s
                    sm, pb = small[j], Pb[j]
                    V.put(lambda e, o=sm[:, 3:4], x=sm[:, 2:3]: e.reciprocal(o, x), [k])
                    k = ts(V, pb[:, 0:L], pb[:, 0:L], sm[:, 3:4], None, ALU.mult, None, k)
                    yield
                    b = AP.take()
                    for x in range(L // 128):
                        kt_ = tr(b.t[:, 128 * x:128 * x + 128], pb[:, 128 * x:128 * x + 128], ident, k, b.free,
                                 inc=x == L // 128 - 1)
                    done[f"pb{j}"] = kt_
                    PTp = r3(PT[p], 4)
                    k = act(PTp[:, 0:L // 128, 128 * i:128 * i + 128], r3(b.t[:, 0:L], L // 128), ACT.Copy, kt_,
                            pt_free[p])
                    b.free = [k]
                    kpt.append(k)

                def turn(units, last):
                    while units:
                        c, s, k_qt = units.pop(0)
                        for p in range(2):
                            for i in range(2):
                                ready.append(scores(c, s, p, i, k_qt))
                                yield
                                if len(ready) > 1:
                                    u = ready.pop(0)
                                    yield from weights(u, kpts.setdefault(u[:2], []))
                                    yield
                                    if u[2] == 1 and u[3] == 1:
                                        yield from values(u[0], u[1])
                    if last:
                        u = ready.pop(0)
                        yield from weights(u, kpts.setdefault(u[:2], []))
                        yield
                        yield from values(u[0], u[1])

                kpts = {}

                def values(c, s):
                    L = 256 + 256 * s
                    while f"ag{c}" not in done:
                        yield "blocked"
                    b = AP.take()
                    for p in range(2):
                        PTp = r3(PT[p], 4)
                        for j in range(L // 128):
                            k = mm(b.t[64 * p:64 * p + 64, 0:256], QKV[:, j, 640 + 64 * p:704 + 64 * p],
                                   PTp[:, j, :], j == 0, j == L // 128 - 1, kpts[(c, s)], done[f"kv{j}"], b.free,
                                   inc=j == L // 128 - 1)
                        pt_free[p] = k
                    y = AG[:, c, 256 * s:256 * s + 256]
                    k = stt(V, y, b.t[:, 0:256], 0.5, y, ALU.mult, ALU.mult, k, done[f"ag{c}"])
                    b.free = [k]
                    done["ya"] = k
                    yield

                QTs = [QT, QT]
                for c in range(4):
                    QT = QTs[c % 2]
                    b = AP.take()
                    for t in tiles:
                        k = tr(b.t[:, 128 * t:128 * t + 128], QKV[:, t, 128 * c:128 * c + 128], ident,
                               done[f"n{t}"], b.free, inc=t == 3)
                    k_qt = act(QT[:, l0:512], b.t[:, l0:512], ACT.Copy, k, k_kt, done.get("qt0"), done.get("qt1"))
                    b.free = [k_qt]
                    yield
                    for s in ((0, 1) if l == 0 else (1,)):
                        units.append((c, s, k_qt))
                        yield from turn(units, False)
                yield from turn(units, True)

            def gla(scr):
                B = [r3(scr(512), 1) for _ in range(2)]
                EE = [scr(512) for _ in range(2)]
                QK = [scr(512) for _ in range(2)]
                attf = scr(1024)
                att = attf.rearrange("p (t h c) -> p t h c", t=4, h=2)
                KDT = [attf[:, 0:512], attf[:, 512:1024]]
                QB = [scr(512) for _ in range(2)]
                if l == 1:
                    spare.extend(q[:, 0:256] for q in QB)
                ST = scr(2048).rearrange("p (d n v) -> p d n v", d=2, n=8)
                SC = cst[:, C_SCAN:C_SCAN + 512]
                scr1, scr2 = EE
                EL = scr(16)
                nt = len(tiles)
                W = 512 - l0
                while "lr" not in done:
                    yield "blocked"
                for hp in range(2):
                    last = done.get("glalast")
                    for d in range(2):
                        b = GP.take()
                        k = mm(b.t, PM[0:32, 256 * d + 128 * hp:256 * d + 128 * hp + 128], TH2[0:32, :], True, True,
                               done["lr"], k_par, b.free, inc=True)
                        k = act(EE[d], b.t, ACT.Identity, k, k_par, last,
                                bias=par[:, PA_AB + 2 * d + hp:PA_AB + 2 * d + hp + 1])
                        b.free = [k]
                        yield
                        act(QK[d], EE[d], ACT.Abs)
                        act(QK[d], QK[d], ACT.Exp, scale=-1.0)
                    for d in range(2):
                        act(QK[d], QK[d], ACT.Ln, bias=one)
                    for d in range(2):
                        k = stt(V, QK[d], EE[d], 0.0, QK[d], ALU.min, ALU.subtract, (A.sem, A.n), last)
                        o, g = B[d][:, 0, :], QK[d]
                        if d:
                            o, g = o[:, ::-1], g[:, ::-1]
                        V.put(lambda e, o=o, g=g: e.tensor_tensor_scan(o, SC, g, 0.0, ALU.mult, ALU.add), [])
                    yield
                    while "gqk" not in done:
                        yield "blocked"
                    kB = (V.sem, V.n)
                    kel = []
                    for d in range(2):
                        b4 = B[d][:, 0, :].rearrange("p (n m) -> p n m", m=64)
                        r = b4[:, :, 0:1] if d else b4[:, :, 63:64]
                        E = EE[d]
                        k = tt(G, r3(E, 8), r.to_broadcast([128, 8, 64]), b4, ALU.subtract, kB)
                        k = act(E, E, ACT.Exp, k, scale=1.0 / 16)
                        kel = act(EL[:, 8 * d:8 * d + 8].unsqueeze(2), r, ACT.Exp, kB, scale=1.0 / 16)
                        k = tt(V, QK[d], GK[:, hp, :], E, ALU.mult, k, last, done["gqk"])
                        yield
                        b = GP.take()
                        for t in range(4):
                            k2 = tr(b.t[:, 128 * t:128 * t + 128], QK[d][:, 128 * t:128 * t + 128], ident, k, b.free,
                                    inc=t == 3)
                        k = act(KDT[d], b.t, ACT.Copy, k2, last)
                        b.free = [k]
                        k2 = act(QB[d][:, l0:512], B[d][:, 0, l0:512], ACT.Exp, kB, last, scale=1.0 / 16)
                        tt(V, QB[d][:, l0:512], QB[d][:, l0:512], GQ[:, hp, l0:512], ALU.mult, k2)
                        yield
                    kQB = (V.sem, V.n)
                    kKD = (A.sem, A.n)
                    while "gv" not in done:
                        yield "blocked"
                    order = [[0, 1, 2, 3, 4, 5, 6, 7], [3, 2, 1, 0, 7, 6, 5, 4]]
                    for i in range(7):
                        for d in range(2):
                            b = GP.take()
                            n, nx = order[d][i], order[d][i + 1]
                            t, r0 = n // 2, 64 * (n % 2)
                            for p in range(2):
                                h = 2 * hp + p
                                k = mm(b.t[64 * p:64 * p + 64, 0:128],
                                       KDT[d][r0:r0 + 64, 128 * t + 64 * p:128 * t + 64 * p + 64],
                                       GV[r0:r0 + 64, t, 128 * h:128 * h + 128], True, True,
                                       kKD, done["gv"], b.free, inc=True)
                            u = b.t[:, 0:128]
                            if i == 0:
                                k2 = cp(V, ST[:, d, nx, :], u, k, last)
                            else:
                                k2 = stt(V, ST[:, d, nx, :], ST[:, d, n, :], EL[:, 8 * d + n:8 * d + n + 1], u,
                                         ALU.mult, ALU.add, k, kel)
                            b.free = [k2]
                        yield
                    kST, ku = k2, (P.sem, P.n)
                    for p in range(2):
                        b = GP.take()
                        for t in tiles:
                            k = mm(b.t[:, 128 * t:128 * t + 128], GK[64 * p:64 * p + 64, hp, 128 * t:128 * t + 128],
                                   GQ[64 * p:64 * p + 64, hp, 128 * t:128 * t + 128], t == tiles[0], True, done["gqk"],
                                   b.free, inc=t == 3)
                        b.free = [stt(V, att[:, tiles[0]:4, p, :], r3(b.t[:, l0:512], nt), 2.0,
                                      ident.unsqueeze(1).to_broadcast([128, nt, 128]), ALU.mult, ALU.mult, k, ku)]
                        yield
                    steps = [(m, d) for m in MS for d in range(2)]
                    ke = [kQB, kQB]

                    def factors(n):
                        m, d = steps[n]
                        e = EE[n % 2]
                        b4 = B[d][:, 0, l0:512].rearrange("p (n s m) -> p n s m", s=2, m=m)
                        e4 = e[:, l0:512].rearrange("p (n s m) -> p n s m", s=2, m=m)
                        r = (b4[:, :, 1, 0:1] if d else b4[:, :, 0, m - 1:m]).to_broadcast([128, W // (2 * m), m])
                        hk, hq = (1, 0) if d else (0, 1)
                        tt(G, e4[:, :, hk, :], r, b4[:, :, hk, :], ALU.subtract, ke[n % 2])
                        k = tt(G, e4[:, :, hq, :], b4[:, :, hq, :], r, ALU.subtract)
                        k = act(e[:, l0:512], e[:, l0:512], ACT.Exp, k, scale=1.0 / 16)
                        q4 = QK[n % 2][:, l0:512].rearrange("p (n s m) -> p n s m", s=2, m=m)
                        for half, src in ((hk, GK), (hq, GQ)):
                            k2 = tt(V, q4[:, :, half, :], e4[:, :, half, :],
                                    src[:, hp, l0:512].rearrange("p (n s m) -> p n s m", s=2, m=m)[:, :, half, :],
                                    ALU.mult, k, kq[n % 2])
                        ke[n % 2] = k2
                        return k2

                    kq = [kKD, kKD]
                    kf = factors(0)
                    yield
                    for n, (m, d) in enumerate(steps):
                        kn = factors(n + 1) if n + 1 < len(steps) else None
                        yield
                        qk = QK[n % 2]
                        for p in range(2):
                            b = GP.take()
                            for t in tiles:
                                a = qk[64 * p:64 * p + 64, 128 * t:128 * t + 128]
                                k2 = mm(b.t[:, 128 * t:128 * t + 128], a, a, t == tiles[0], True, kf, b.free,
                                        inc=t == 3)
                            b.free = [pred(att[:, tiles[0]:4, p, :],
                                           mask(m, d).unsqueeze(1).to_broadcast([128, nt, 128]),
                                           r3(b.t[:, l0:512], nt), k2)]
                        kq[n % 2] = k2
                        kf = kn
                        yield
                    katt = (V.sem, V.n)
                    for p in range(2):
                        h = 2 * hp + p
                        while f"gg{h}" not in done:
                            yield "blocked"
                        b = GP.take()
                        first = True
                        for t in tiles:
                            mm(b.t[:, 128 * t:128 * t + 128], GV[:, t, 128 * h:128 * h + 128], att[:, t, p, :],
                               first, False, katt, b.free)
                            first = False
                            for n in (2 * t, 2 * t + 1):
                                for d in range(2):
                                    if (d == 0 and n == 0) or (d == 1 and n == 3):
                                        continue
                                    k = mm(b.t[:, 64 * n:64 * n + 64], ST[64 * p:64 * p + 64, d, n, :],
                                           QB[d][64 * p:64 * p + 64, 64 * n:64 * n + 64], False, True, kST, kQB,
                                           inc=True)
                        O, Q2 = scr1[:, l0:512], scr2[:, l0:512]
                        k = act(O, b.t[:, l0:512], ACT.Copy, k, (V.sem, V.n))
                        b.free = [k]
                        k = tt(V, Q2, O, O, ALU.mult, k)
                        yield
                        b = GP.take()
                        k = mm(b.t[:, l0:512], o128, Q2, True, True, k, b.free, inc=True)
                        b.free = [rstd_big(Q2, b.t[:, l0:512], k)]
                        k = stt(V, O, O, par[:, PA_ON:PA_ON + 1], Q2, ALU.mult, ALU.mult, b.free, k_par)
                        y = GG[:, h, l0:512]
                        done["yg"] = stt(V, y, O, 0.5, y, ALU.mult, ALU.mult, done[f"gg{h}"])
                        yield
                    done["glalast"] = [(V.sem, V.n), (A.sem, A.n), (P.sem, P.n)]

            def scr(n):
                return al(n)

            weave(plan, P, *((gla(scr), attention(scr)) if GFIRST[l] else (attention(scr), gla(scr))), dense())
            allk = [(V.sem, V.n), (A.sem, A.n), (P.sem, P.n), (G.sem, G.n)]
            top[0] = s0

            n = 512 - l0
            DP2 = Pool(PS)
            SIG = [al(512) for _ in range(2)]
            TM = al(512)
            it = 0
            ys = {"a": (AG, done["ya"]), "g": (GG, done["yg"]), "s": (SG, done["ys"])}
            free_sig = [None, None]
            ktm = None
            for j in range(2):
                for bi, br in enumerate("ags"):
                    if (br, j) not in EARLY[l]:
                        w, kw = use(f"a{l}m{br}{j}")
                        w = rows_of(w, 8)
                    wb, kwb = use(f"a{l}b{br}{j}")
                    wb = rows_of(wb, 4)
                    Y, ky = ys[br]
                    for c in range(4):
                        if (br, j) in EARLY[l]:
                            sg, k = early[(br, j, c)]
                        else:
                            b = DP2.take()
                            kd = feat(b, w, 8, 128 * c, 128, hT, l0, 512, 8, [kw, b.free])
                            sg = SIG[it % 2][:, 0:n]
                            k = act(sg, b.t[:, 0:n], ACT.Tanh, kd, free_sig[it % 2], allk, scale=0.5)
                            b.free = [k]
                        b = DP2.take()
                        k2 = feat(b, wb, 4, 128 * c, 128, Y, l0, 512, 4, [kwb, ky, b.free])
                        m = mT[:, 4 * j + c, l0:512]
                        if bi == 0:
                            k3 = stt(V, m, sg, 1.0, b.t[:, 0:n], ALU.add, ALU.mult, k, k2, allk)
                        else:
                            k3 = stt(V, TM[:, 0:n], sg, 1.0, b.t[:, 0:n], ALU.add, ALU.mult, k, k2, ktm, allk)
                            ktm = tt(G, m, m, TM[:, 0:n], ALU.add, k3)
                        b.free = [k3]
                        if (br, j) not in EARLY[l]:
                            free_sig[it % 2] = k3
                            it += 1
                    if (br, j) not in EARLY[l]:
                        release(f"a{l}m{br}{j}", kd)
                    release(f"a{l}b{br}{j}", k2)
            km = [(V.sem, V.n), (G.sem, G.n)]

            top[0] = s0 + 512 * 3
            zz = al(1024)
            rp = al(2048)
            gb = al(2048)
            st6 = al(16)
            if l == 0:
                XR = [al(1024) for _ in range(2)]
                assert top[0] <= 53200 - 2048
                k_xr = [dma(XR[t], xin[:, 1024 * t:1024 * t + 1024], km) for t in range(2)]
            k_rp = dma(rp, rpost[l].partition_broadcast(128), km)
            for s in range(2):
                for hf in range(2):
                    if l == 1 and s == 0:
                        continue
                    b = DP2.take()
                    c = 1 - s
                    for i in range(4):
                        k = mm(b.t[:, 128 * i:128 * i + 128],
                               sc3[:, 16 + 4 * hf + i, c:c + 1].to_broadcast([128, 128]), ident, i == 0, True, k_sc,
                               b.free, inc=i == 3)
                    b.free = [act(gb[:, 1024 * s + 512 * hf:1024 * s + 512 * hf + 512], b.t, ACT.Copy, k, km,
                                  scale=0.5)]
            k_gb = (A.sem, A.n)
            w0, kw0 = use(f"a{l}o0")
            w1, kw1 = use(f"a{l}o1")
            ws = [(rows_of(w0, 8), kw0), (rows_of(w1, 8), kw1)]
            for t in tiles:
                s = t // 2
                for hf in range(2):
                    b = DP2.take()
                    w, kw = ws[hf]
                    k = token(b, w, 0, 512, mT, 128 * t, [kw, km, b.free])
                    cs_ = slice(512 * hf, 512 * hf + 512)
                    k2 = tt(V, zz[:, cs_], b.t, gb[:, 1024 * s + 512 * hf:1024 * s + 512 * hf + 512], ALU.mult, k, k_gb)
                    b.free = [k2]
                    xr = (XR[t % 2][:, 512 * hf:512 * hf + 512] if l == 0
                          else X[:, 1024 * (t % 2) + 512 * hf:1024 * (t % 2) + 512 * hf + 512])
                    stt(V, zz[:, cs_], xr, ALPHA, zz[:, cs_], ALU.mult, ALU.add, k_xr[t] if l == 0 else None)
                    V.put(lambda e, o=st6[:, 6 * hf:6 * hf + 6], i=zz[:, cs_]: e.bn_stats(o, i), [])
                if l == 0 and t < 2:
                    k_xr.append(dma(XR[t], xin[:, 1024 * t + 2048:1024 * t + 3072], (V.sem, V.n)))
                k = V.put(lambda e: e.bn_aggr(st6[:, 12:14], r3(st6[:, 0:12], 2)), [])
                kr = rstd_small(st6[:, 14:15], st6[:, 13:14], k)
                o = X[:, 1024 * (t % 2):1024 * (t % 2) + 1024] if t >= 2 else CX[:, 1024 * t:1024 * t + 1024]
                ts(V, zz, zz, st6[:, 12:13], st6[:, 14:15], ALU.subtract, ALU.mult, kr)
                tt(V, zz, zz, rp[:, 0:1024], ALU.mult, k_rp)
                k = tt(V, o, zz, rp[:, 1024:2048], ALU.add, k_rp)
                lastp = (P.sem, P.n)
            release(f"a{l}o0", lastp)
            release(f"a{l}o1", lastp)
            return [(V.sem, V.n), (G.sem, G.n), (P.sem, P.n), (A.sem, A.n)]

        CX = arena[:, 53200 - 2048:53200]

        def layer_b(l, k_x):
            top[0] = base
            hT = r3(al(2048), 8)
            par = al(PB_W)
            QPf = al(12 * 260)
            QP = r3(QPf, 12)
            CV = r3(al(3072), 12)
            ZA = r3(al(1024), 4)
            CU = r3(al(4 * 286), 4)
            CA = r3(al(1024), 4)
            ZB = r3(al(1024), 4)
            TH = al(512)
            gh = al(16)
            s0 = top[0]
            k_par = dma(par, pb[l], k_x)
            kgh = ts(V, gh, par[:, PB_GB:PB_GB + 16], 0.5, None, ALU.mult, None, k_par)
            SIG = {}
            for c in range(4):
                SIG[(0, 0, c)], SIG[(0, 1, c)], SIG[(1, 0, c)] = CV[:, c, :], CV[:, 4 + c, :], CV[:, 8 + c, :]
                SIG[(1, 1, c)] = CU[:, c, 0:256]
            DP = Pool(PS[0:2])
            SP_ = Pool(PS[2:5])
            HP = Pool(PS[5:8])
            XS = al(2048)
            st2 = al(4)
            for t in range(2):
                k = act(XS[:, 1024 * t:1024 * t + 1024], X[:, 1024 * t:1024 * t + 1024], ACT.Square, k_x,
                        acc=st2[:, t:t + 1])
            k = ts(V, st2[:, 0:2], st2[:, 0:2], 1.0 / 1024, None, ALU.mult, None, k, k_x)
            kr = rstd_small(st2[:, 2:4], st2[:, 0:2], k)
            for t in range(2):
                k = ts(V, XS[:, 1024 * t:1024 * t + 1024], X[:, 1024 * t:1024 * t + 1024], st2[:, 2 + t:3 + t], None,
                       ALU.mult, None, kr)
            k_hk = []
            for kk in range(8):
                b = SP_.take()
                for t in range(2):
                    k2 = tr(b.t[:, 128 * t:128 * t + 128], XS[:, 1024 * t + 128 * kk:1024 * t + 128 * kk + 128], ident,
                            k, b.free, inc=t == 1)
                b.free = [act(hT[:, kk, :], b.t[:, 0:256], ACT.Copy, k2, k_par, scale=par[:, PB_NW + kk:PB_NW + kk + 1])]
                k_hk.append(b.free)
            k_h = [(A.sem, A.n)]
            ms(G, QP[:, :, 0:2], 0.0, k_x)
            ms(G, QP[:, :, 258:260], 0.0)
            ms(G, CU[:, :, 0:15], 0.0)
            ms(G, CU[:, :, 271:286], 0.0)
            top[0] = s0
            done = {}

            def dense():
                for j in range(3):
                    w, kw = use(f"b{l}q{j}")
                    w = rows_of(w, 8)
                    for c in range(4):
                        b = DP.take()
                        k = feat(b, w, 8, 128 * c, 128, hT, 0, 256, 8, [kw, b.free], kh=k_hk)
                        b.free = [act(QP[:, 4 * j + c, 2:258], b.t[:, 0:256], ACT.Copy, k)]
                        done[f"q{4 * j + c}"] = b.free
                        yield
                    release(f"b{l}q{j}", k)
                w, kw = use(f"b{l}ab")
                w = rows_of(w, 8)
                b = DP.take()
                k = feat(b, w, 8, 0, 100, hT, 0, 256, 8, [kw, b.free], m=100)
                b.free = [act(TH[0:100, 0:256], b.t[0:100, 0:256], ACT.Copy, k)]
                done["ab"] = b.free
                release(f"b{l}ab", k)
                yield
                for name in ("za", "cv", "cg", "zb"):
                    w, kw = use(f"b{l}{name}")
                    w = rows_of(w, 8)
                    for c in range(4):
                        b = DP.take()
                        k = feat(b, w, 8, 128 * c, 128, hT, 0, 256, 8, [kw, b.free])
                        ps = b.t[:, 0:256]
                        if name == "cv":
                            b.free = [act(CU[:, c, 15:271], ps, ACT.Copy, k, (G.sem, G.n))]
                        else:
                            dst = {"za": ZA, "zb": ZB, "cg": CA}[name][:, c, :]
                            k1 = act(TH[:, 256:512], ps, ACT.Tanh, k, done.get("th"), scale=0.5)
                            if name == "cg":
                                k2 = stt(V, CU[:, c, 15:271], TH[:, 256:512], 1.0, CU[:, c, 15:271], ALU.add,
                                         ALU.mult, k1)
                                b.free = [k1]
                                done[f"cu{c}"] = k2
                            else:
                                k2 = stt(V, dst, TH[:, 256:512], 1.0, ps, ALU.add, ALU.mult, k1)
                                b.free = [k2]
                            done["th"] = k2
                            done[f"{name}{c}"] = k2
                        yield
                    release(f"b{l}{name}", k)
                while "cv" not in done:
                    yield "blocked"
                for j in range(2):
                    for bi in range(2):
                        while (j, bi) == (1, 1) and "yb" not in done:
                            yield "blocked"
                        w, kw = use(f"b{l}m{bi}{j}")
                        w = rows_of(w, 8)
                        for c in range(4):
                            b = DP.take()
                            k = feat(b, w, 8, 128 * c, 128, hT, 0, 256, 8, [kw, b.free])
                            q = 8 * bi + 4 * j + c
                            done[f"sig{q}"] = act(SIG[(j, bi, c)], b.t[:, 0:256], ACT.Tanh, k, kgh, done["cv"],
                                                  done.get("yb") if (j, bi) == (1, 1) else None, scale=0.5,
                                                  bias=gh[:, q:q + 1])
                            b.free = [done[f"sig{q}"]]
                            yield
                        release(f"b{l}m{bi}{j}", k)

            def confconv(scr):
                UM = scr(256)
                UQ = scr(256)
                fw = par[:, PB_FW:PB_FW + 124]
                for c in range(4):
                    while f"cu{c}" not in done:
                        yield "blocked"
                    E = V
                    k = ts(E, CA[:, c, :], CU[:, c, 0:256], fw[:, 31 * c:31 * c + 1], None, ALU.mult, None,
                           done[f"cu{c}"], k_par)
                    for i in range(1, 31):
                        stt(E, CA[:, c, :], CU[:, c, i:i + 256], fw[:, 31 * c + i:31 * c + i + 1], CA[:, c, :],
                            ALU.mult, ALU.add)
                        if i % 4 == 0:
                            yield
                    ts(E, CA[:, c, :], CA[:, c, :], 0.5, par[:, PB_FB + c:PB_FB + c + 1], ALU.mult, ALU.add)
                    yield
                kca = [(V.sem, V.n), (G.sem, G.n)]
                b = DP.take()
                for c in range(4):
                    k = mm(b.t[:, 0:256], o512, CA[:, c, :], c == 0, c == 3, kca, b.free, inc=c == 3)
                ub = UM.unsqueeze(1).to_broadcast([128, 4, 256])
                k = act(UM, b.t[:, 0:256], ACT.Copy, k)
                b.free = [k]
                k = tt(V, CA[:, :, :], CA[:, :, :], ub, ALU.subtract, k, kca)
                yield
                b = DP.take()
                for c in range(4):
                    k1 = act(UQ, CA[:, c, :], ACT.Square, k, (P.sem, P.n))
                    k2 = mm(b.t[:, 0:256], o512, UQ, c == 0, c == 3, k1, b.free, inc=True)
                b.free = [rstd_big(UM, b.t[:, 0:256], k2)]
                k = tt(V, CA[:, :, :], CA[:, :, :], ub, ALU.mult, b.free)
                for c in range(4):
                    k = ts(V, CA[:, c, :], CA[:, c, :], par[:, PB_LW + c:PB_LW + c + 1],
                           par[:, PB_LB + c:PB_LB + c + 1], ALU.mult, ALU.add)
                k1 = act(CU[:, :, 0:256], CA[:, :, :], ACT.Tanh, k, scale=0.5)
                while "zb3" not in done:
                    yield "blocked"
                stt(V, CA[:, :, :], CU[:, :, 0:256], 1.0, CA[:, :, :], ALU.add, ALU.mult, k1)
                done["yb"] = stt(V, CA[:, :, :], CA[:, :, :], 0.25, ZB[:, :, :], ALU.mult, ALU.mult, done["zb3"])
                yield

            def delta(scr):
                cw = par[:, PB_CW:PB_CW + 60]
                K3 = r3(scr(1024), 2)
                V3 = r3(scr(1024), 2)
                EG = r3(scr(2048), 8)
                DT = r3(scr(2048), 16)
                AT = r3(scr(2048), 16)
                NL = r3(scr(2048), 16)
                XM = r3(scr(2048), 16)
                XT = r3(scr(2048), 16)
                Y = r3(scr(2048), 16)
                QD = r3(QPf[:, 0:2048], 8)
                KG = NL
                KC = Y
                KD = DT
                GB = scr(256)
                GB2 = scr(256)
                GC = r3(scr(200), 2)
                BC = scr(64)
                SS = r3(QPf[:, 2048:3072], 8)
                VW = [scr(512) for _ in range(2)]
                R = scr(512)
                for c in range(12):
                    while f"q{c}" not in done:
                        yield "blocked"
                    E = V
                    for i in range(5):
                        s = cw[:, 5 * c + i:5 * c + i + 1]
                        if i == 0:
                            k = ts(E, CV[:, c, :], QP[:, c, 0:256], s, None, ALU.mult, None, done[f"q{c}"], k_par,
                                   (G.sem, G.n))
                        else:
                            k = stt(E, CV[:, c, :], QP[:, c, i:i + 256], s, CV[:, c, :], ALU.mult, ALU.add)
                    k1 = act(QP[:, c, 0:256], CV[:, c, :], ACT.Tanh, k, scale=0.5)
                    k = stt(E, CV[:, c, :], QP[:, c, 0:256], 1.0, CV[:, c, :], ALU.add, ALU.mult, k1)
                    yield
                kcv = [(V.sem, V.n), (G.sem, G.n)]
                NB = SP_.banks + HP.banks[0:1]
                RN = XM.rearrange("p a b -> p (a b)")
                SQ = XT.rearrange("p a b -> p (a b)")
                for c in range(8):
                    k = act(SQ[:, 256 * c:256 * c + 256], CV[:, c, :], ACT.Square, kcv)
                    yield
                    b = NB[c // 2]
                    k = mm(b.t[:, 256 * (c % 2):256 * (c % 2) + 256], o128, SQ[:, 256 * c:256 * c + 256], c % 2 == 0,
                           True, k, b.free, inc=True)
                    if c % 2:
                        yield
                for c in range(4):
                    NB[c].free = [act(RN[:, 512 * c:512 * c + 512], NB[c].t, ACT.Ln, k, bias=eps, scale=32.0)]
                for c in range(2):
                    k = act(RN[:, 1024 * c:1024 * c + 1024], RN[:, 1024 * c:1024 * c + 1024], ACT.Exp, scale=-0.5)
                    f = 128.0 ** -0.5 / 2 if c == 0 else 0.5
                    k = stt(V, CV[:, 4 * c:4 * c + 4, :], CV[:, 4 * c:4 * c + 4, :], f,
                            RN[:, 1024 * c:1024 * c + 1024].rearrange("p (a b) -> p a b", a=4), ALU.mult, ALU.mult, k)
                yield
                k = ts(V, CV[:, 8:12, :], CV[:, 8:12, :], 0.5, None, ALU.mult, None)
                kcv = k
                yield
                for src, dst in ((4, K3), (8, V3)):
                    for t in range(2):
                        b = SP_.take()
                        for h in range(4):
                            k = tr(b.t[:, 128 * h:128 * h + 128], CV[:, src + h, 128 * t:128 * t + 128], ident, kcv,
                                   b.free, inc=h == 3)
                        b.free = [act(dst[:, t, :], b.t, ACT.Copy, k)]
                        yield
                kkv = (A.sem, A.n)
                while "ab" not in done:
                    yield "blocked"
                k = ms(V, GB[0:100, :], 0.0)
                act(GB2[0:36, :], TH[0:36, 0:256], ACT.Identity, done["ab"], k_par, k,
                    bias=par[0:36, PB_DT:PB_DT + 1])
                act(TH[0:36, 0:256], GB2[0:36, :], ACT.Abs)
                act(TH[0:36, 0:256], TH[0:36, 0:256], ACT.Exp, scale=-1.0)
                act(TH[0:36, 0:256], TH[0:36, 0:256], ACT.Ln, bias=one[0:36, :])
                k = act(BC[0:36, 0:1], par[0:36, PB_AL:PB_AL + 1], ACT.Exp)
                stt(V, GB2[0:36, :], GB2[0:36, :], 0.0, TH[0:36, 0:256], ALU.max, ALU.add, k)
                ts(V, BC[0:36, 1:2], BC[0:36, 0:1], -1.0, None, ALU.mult, None)
                ts(V, GB2[0:36, :], GB2[0:36, :], BC[0:36, 1:2], None, ALU.mult, None)
                SCN = cst[:, C_SCAN:C_SCAN + 256]
                V.put(lambda e: e.tensor_tensor_scan(GB[0:32, :], SCN[0:32, :], GB2[0:32, :], 0.0, ALU.mult, ALU.add), [])
                V.put(lambda e: e.tensor_tensor_scan(GB[32:36, ::-1], SCN[32:36, :], GB2[32:36, ::-1], 0.0, ALU.mult,
                                                     ALU.add), [])
                k = act(GB[64:100, :], TH[64:100, 0:256], ACT.Tanh, (V.sem, V.n), scale=0.5)
                k = ts(V, GB[64:100, :], GB[64:100, :], 0.5, 0.5, ALU.mult, ALU.add, k)
                yield
                b = SP_.take()
                for t in range(2):
                    k2 = tr(b.t[:, 128 * t:128 * t + 100], GB[0:100, 128 * t:128 * t + 128], ident[0:100, 0:100], k,
                            b.free, inc=t == 1)
                kgc = cp(V, GC, b.t[:, 0:256].rearrange("p (a b) -> p a b", a=2)[:, :, 0:100], k2)
                b.free = [kgc]
                for d in range(2):
                    for t in range(2):
                        o = 8 * d + 4 * t
                        cp(V, BC[:, o:o + 4], GC[:, t, 64 + 32 * d:68 + 32 * d])
                        ts(V, BC[:, 16 + o:20 + o], GC[:, t, 64 + 32 * d:68 + 32 * d], -1.0, None, ALU.mult, None)
                        kbc = act(BC[:, 32 + o:36 + o], GC[:, t, 32 * d:32 * d + 4], ACT.Exp, kgc, (V.sem, V.n))
                yield
                for d in range(2):
                    for hq in range(2):
                        b = SP_.take()
                        for i in range(2):
                            h = 2 * hq + i
                            rr = 32 * d + h
                            k = mm(b.t[:, 256 * i:256 * i + 256], ident[0:36, rr:rr + 1].to_broadcast([36, 128]),
                                   GB[0:36, :], i == 0, True, b.free, k2, inc=i == 1)
                        for i in range(2):
                            h = 2 * hq + i
                            for t in range(2):
                                kv_ = ts(V, DT[:, 8 * d + 4 * t + h, :], b.t[:, 256 * i + 128 * t:256 * i + 128 * t + 128],
                                         GC[:, t, 32 * d + h:32 * d + h + 1], 0.0, ALU.subtract, ALU.min, k)
                        b.free = [act(EG[:, 4 * d + 2 * hq:4 * d + 2 * hq + 2, :], r3(b.t, 2), ACT.Exp, kv_)]
                        yield
                for d in range(2):
                    k = act(DT[:, 8 * d:8 * d + 8, :], DT[:, 8 * d:8 * d + 8, :], ACT.Exp)
                    inc_ = cst[:, C_INC + 128 * d:C_INC + 128 * d + 128].unsqueeze(1).to_broadcast([128, 8, 128])
                    tt(G, AT[:, 8 * d:8 * d + 8, :], DT[:, 8 * d:8 * d + 8, :], inc_, ALU.mult, k)
                    for half in range(2):
                        rs = slice(64 * half, 64 * half + 64)
                        col = 64 * half + (0 if d else 63)
                        cp(V, BC[rs, 48 + 8 * d:56 + 8 * d].unsqueeze(2), DT[rs, 8 * d:8 * d + 8, col:col + 1], k)
                    yield
                kdt = (V.sem, V.n)
                kat = (G.sem, G.n)
                for t in range(2):
                    b = SP_.take()
                    for h in range(4):
                        kt = CV[:, 4 + h, 128 * t:128 * t + 128]
                        k = mm(b.t[:, 128 * h:128 * h + 128], kt, kt, h == 0, True, kcv, b.free, inc=h == 3)
                    for d in range(2):
                        for h in range(4):
                            o = 8 * d + 4 * t + h
                            k3 = stt(V, NL[:, o, :], b.t[:, 128 * h:128 * h + 128], BC[:, 16 + o:17 + o], DT[:, o, :],
                                     ALU.mult, ALU.mult, k, kdt)
                    b.free = [k3]
                    b = SP_.take()
                    for h in range(4):
                        k = mm(b.t[:, 128 * h:128 * h + 128], CV[:, 4 + h, 128 * t:128 * t + 128],
                               CV[:, h, 128 * t:128 * t + 128], h == 0, True, b.free, inc=h == 3)
                    for d in range(2):
                        o = 8 * d + 4 * t
                        b.free = [tt(V, AT[:, o:o + 4, :], r3(b.t, 4), AT[:, o:o + 4, :], ALU.mult, k, kat)]
                    yield
                for d in range(2):
                    kqd = tt(V, QD[:, 4 * d:4 * d + 4, :], CV[:, 0:4, :], EG[:, 4 * d:4 * d + 4, :], ALU.mult,
                             (A.sem, A.n))
                done["cv"] = [kqd, k]
                idb = ident.unsqueeze(1).to_broadcast([128, 16, 128])
                cp(G, XM[:, :, :], idb)
                k = cp(V, XT[:, :, :], idb)
                kx = [(V.sem, V.n), (G.sem, G.n)]
                kxx = [kx] * 4
                for m in MS:
                    for q in range(4):
                        d = q // 2
                        g = slice(4 * q, 4 * q + 4)
                        mx = mask(m, 1 - d).unsqueeze(1).to_broadcast([128, 4, 128])
                        mt = mask(m, d).unsqueeze(1).to_broadcast([128, 4, 128])
                        b = SP_.take()
                        for i in range(4):
                            o = 4 * q + i
                            k = mm(b.t[:, 128 * i:128 * i + 128], NL[:, o, :], XM[:, o, :], i == 0, True, kxx[q],
                                   b.free, inc=i == 3)
                        if m == 1:
                            pred(XM[:, g, :], mx, r3(b.t, 4), k)
                            b.free = [(V.sem, V.n)]
                            kxx[q] = pred(XT[:, g, :], mt, NL[:, g, :])
                            yield
                            continue
                        k = act(Y[:, g, :], r3(b.t, 4), ACT.Copy, k)
                        b.free = [k]
                        yield
                        if m < 32:
                            b = SP_.take()
                            for i in range(4):
                                o = 4 * q + i
                                k2 = mm(b.t[:, 128 * i:128 * i + 128], XT[:, o, :], Y[:, o, :], i == 0, True, k,
                                        b.free, inc=i == 3)
                            kb1 = (b, k2)
                        b = SP_.take()
                        for i in range(4):
                            o = 4 * q + i
                            k2 = mm(b.t[:, 128 * i:128 * i + 128], Y[:, o, :], XT[:, o, :], i == 0, True, k, b.free,
                                    inc=i == 3)
                        if m < 32:
                            kb1[0].free = [pred(XM[:, g, :], mx, r3(kb1[0].t, 4), k2)]
                        b.free = [pred(XT[:, g, :], mt, r3(b.t, 4), k2)]
                        kxx[q] = b.free
                        yield
                kp = [(P.sem, P.n)]
                kxt = [(V.sem, V.n)]
                for d in range(2):
                    for t in range(2):
                        for h in range(4):
                            o = 8 * d + 4 * t + h
                            src = K3[:, t, 128 * h:128 * h + 128]
                            ts(V, KG[:, o, :], src, BC[:, 32 + o:33 + o], None, ALU.mult, None, kp, kbc, kkv)
                            ts(G, KD[:, o, :], src, BC[:, 48 + o:49 + o], None, ALU.mult, None, kp, kdt, kkv,
                               kxt)
                    yield
                kkg = [(V.sem, V.n), (G.sem, G.n), kqd]
                for q in range(4):
                    b = SP_.take()
                    for i in range(4):
                        o = 4 * q + i
                        k = mm(b.t[:, 128 * i:128 * i + 128], KG[:, o, :], XT[:, o, :], i == 0, True, kkg, b.free,
                               inc=i == 3)
                    b.free = [act(KC[:, 4 * q:4 * q + 4, :], r3(b.t, 4), ACT.Copy, k, scale=-1.0)]
                    yield
                kkc = b.free
                OB = [HP.banks[0], HP.banks[1]]
                ofirst = [True, True]
                kss = [None, None]
                kvw = [None, None]
                UB = [SP_.banks[0], SP_.banks[1]]
                VB = [SP_.banks[2], HP.banks[2]]
                for i in range(4):
                    kv2 = [None, None]
                    for d in range(2):
                        n = 3 - i if d else i
                        t, r0 = n // 2, 64 * (n % 2)
                        b = VB[d]
                        for h in range(4):
                            o = 8 * d + 4 * t + h
                            k = mm(b.t[r0:r0 + 64, 128 * h:128 * h + 128], XT[r0:r0 + 64, o, r0:r0 + 64],
                                   V3[r0:r0 + 64, t, 128 * h:128 * h + 128], h == 0, i == 0, kxt, kkv, b.free, kkc,
                                   inc=True)
                            if i:
                                k = mm(b.t[r0:r0 + 64, 128 * h:128 * h + 128], KC[:, o, r0:r0 + 64],
                                       SS[:, 4 * d + h, :], False, True, kss[d], kkc, inc=True)
                        o = 8 * d + 4 * t
                        vw = r3(VW[d], 4)
                        kv2[d] = tt(V, vw[r0:r0 + 64], r3(b.t, 4)[r0:r0 + 64],
                                    BC[r0:r0 + 64, o:o + 4].unsqueeze(2).to_broadcast([64, 4, 128]), ALU.mult, k,
                                    kvw[d])
                        b.free = [kv2[d]]
                    yield
                    for d in range(2):
                        n = 3 - i if d else i
                        t, r0 = n // 2, 64 * (n % 2)
                        vw = r3(VW[d], 4)
                        if i < 3:
                            b = UB[d]
                            for h in range(4):
                                o = 8 * d + 4 * t + h
                                k = mm(b.t[:, 128 * h:128 * h + 128], KD[r0:r0 + 64, o, :], vw[r0:r0 + 64, h, :],
                                       h == 0, True, kv2[d], b.free, kkg, inc=h == 3)
                        for h in range(4):
                            o = 8 * d + 4 * t + h
                            dst = OB[t].t[:, 128 * h + r0:128 * h + r0 + 64]
                            if i:
                                k1 = mm(dst, SS[:, 4 * d + h, :], QD[:, 4 * d + h, 64 * n:64 * n + 64], ofirst[t], True,
                                        kss[d], kkg, OB[t].free, inc=True)
                                ofirst[t] = False
                            k1 = mm(dst, vw[r0:r0 + 64, h, :], AT[r0:r0 + 64, o, r0:r0 + 64], ofirst[t], True,
                                    kv2[d], OB[t].free, inc=True)
                            ofirst[t] = False
                        kvw[d] = k1
                        if i < 3:
                            e = 64 * n + (0 if d else 63)
                            for h in range(4):
                                s = SS[:, 4 * d + h, :]
                                u = b.t[:, 128 * h:128 * h + 128]
                                if i == 0:
                                    k2 = cp(V, s, u, k)
                                else:
                                    k2 = stt(V, s, s, EG[:, 4 * d + h, e:e + 1], u, ALU.mult, ALU.add, k, k1)
                            b.free = [k2]
                            kss[d] = k2
                        yield
                while "za3" not in done:
                    yield "blocked"
                for t in range(2):
                    O3 = r3(R, 4)
                    k = act(O3, r3(OB[t].t, 4), ACT.Copy, k1, (V.sem, V.n))
                    OB[t].free = [k]
                    Q2 = VW[t]
                    k = tt(V, Q2, R, R, ALU.mult, k, k1)
                    yield
                    b = SP_.take()
                    k = mm(b.t, o128, Q2, True, True, k, b.free, inc=True)
                    b.free = [rstd_big(Q2, b.t, k)]
                    k = stt(V, R, R, par[:, PB_DN:PB_DN + 1], Q2, ALU.mult, ALU.mult, b.free)
                    z = ZA[:, :, 128 * t:128 * t + 128]
                    done["yd"] = stt(V, z, O3, 0.5, z, ALU.mult, ALU.mult, done["za3"])
                    yield

            def scr(n):
                return al(n)

            weave(plan, P, delta(scr), confconv(scr), dense())
            top[0] = s0
            allk = [(V.sem, V.n), (A.sem, A.n), (P.sem, P.n), (G.sem, G.n)]
            DP2 = Pool(PS)
            TM = al(256)
            mT = r3(al(2048), 8)
            fr = al(1024)
            zz = al(1024)
            f2 = al(4)
            ktm = None
            ys = [(ZA, done["yd"]), (CA, done["yb"])]
            for j in range(2):
                for bi in range(2):
                    wb, kwb = use(f"b{l}b{bi}{j}")
                    wb = rows_of(wb, 4)
                    Yt, ky = ys[bi]
                    for c in range(4):
                        sg = SIG[(j, bi, c)]
                        b = DP2.take()
                        k2 = feat(b, wb, 4, 128 * c, 128, Yt, 0, 256, 4, [kwb, ky, b.free])
                        m = mT[:, 4 * j + c, :]
                        k = done[f"sig{8 * bi + 4 * j + c}"]
                        if bi == 0:
                            k3 = stt(V, m, sg, 1.0, b.t[:, 0:256], ALU.add, ALU.mult, k, k2, allk)
                        else:
                            k3 = stt(V, TM, sg, 1.0, b.t[:, 0:256], ALU.add, ALU.mult, k, k2, ktm)
                            ktm = tt(G, m, m, TM, ALU.add, k3)
                        b.free = [k3]
                    release(f"b{l}b{bi}{j}", k2)
            km = [(V.sem, V.n), (G.sem, G.n)]
            if l == 1:
                k_fr = dma(fr, rfin.partition_broadcast(128), km)
            w0, kw0 = use(f"b{l}o0")
            w1, kw1 = use(f"b{l}o1")
            ws = [(rows_of(w0, 8), kw0), (rows_of(w1, 8), kw1)]
            stores = []
            for t in range(2):
                for hf in range(2):
                    b = DP2.take()
                    w, kw = ws[hf]
                    k = token(b, w, 0, 512, mT, 128 * t, [kw, km, b.free])
                    x = X[:, 1024 * t + 512 * hf:1024 * t + 512 * hf + 512]
                    b.free = [stt(V, x, b.t, 0.5, x, ALU.mult, ALU.add, k)]
                if l == 1:
                    x = X[:, 1024 * t:1024 * t + 1024]
                    k = act(zz, x, ACT.Square, b.free, (V.sem, V.n), acc=f2[:, 0:1])
                    k = ts(V, f2[:, 1:2], f2[:, 0:1], 1.0 / 1024, None, ALU.mult, None, k)
                    kr = rstd_small(f2[:, 2:3], f2[:, 1:2], k)
                    ts(V, x, x, f2[:, 2:3], None, ALU.mult, None, kr)
                    k = tt(V, x, x, fr, ALU.mult, k_fr)
                    stores.append(dma(out[128 * t:128 * t + 128, :], x, k))
            lastp = (P.sem, P.n)
            release(f"b{l}o0", lastp)
            release(f"b{l}o1", lastp)
            if stores:
                S.todo.append((stores, None, False))
            return [(V.sem, V.n), (G.sem, G.n), (P.sem, P.n), (A.sem, A.n)]

        k = layer_a(0, None)
        k = layer_a(1, k)
        k = layer_b(0, k)
        layer_b(1, k)

        def play(E, eng):
            for need, fn, inc in E.todo:
                for s, v in need:
                    eng.wait_ge(s, v)
                if fn is None:
                    continue
                ins = fn(eng)
                if inc:
                    ins.then_inc(E.sem, 1)

        block = ctx.enter_context(nc.Block())

        @block.sync
        def _(e):
            play(S, e)

        @block.gpsimd
        def _(e):
            play(G, e)

        @block.scalar
        def _(e):
            play(A, e)

        @block.tensor
        def _(e):
            play(P, e)

        @block.vector
        def _(e):
            play(V, e)


def make_consts():
    c = np.zeros((128, C_W), np.float32)
    i = np.arange(128)
    c[:, C_ID:C_ID + 128] = np.eye(128)
    for n, m in enumerate(MS):
        a = i[:, None]
        b = i[None, :]
        mk = (a // (2 * m) == b // (2 * m)) & ((a // m) % 2 == 0) & ((b // m) % 2 == 1)
        c[:, C_MASK + 256 * n:C_MASK + 256 * n + 128] = mk
        c[:, C_MASK + 256 * n + 128:C_MASK + 256 * n + 256] = mk.T
    c[:, C_TWO:C_TWO + 128] = 2 * np.eye(128)
    fr = (np.float32(10000.0) ** (-np.arange(0, 32, 2, dtype=np.float32) / np.float32(32))).astype(np.float32)
    tok = np.arange(256)
    for t in range(2):
        p = tok[128 * t:128 * t + 128]
        ar = ((p // 64).astype(np.float32)[:, None] * fr).astype(np.float32)
        ac = ((p % 64).astype(np.float32)[:, None] * fr).astype(np.float32)
        c[:, C_COS + 64 * t:C_COS + 64 * t + 64] = np.concatenate([np.cos(ar)] * 2 + [np.cos(ac)] * 2, 1)
        c[:, C_SIN + 64 * t:C_SIN + 64 * t + 64] = np.concatenate([-np.sin(ar), np.sin(ar), -np.sin(ac), np.sin(ac)], 1)
    c[:, C_SCAN:C_SCAN + 512] = (np.arange(512) % 64 != 0)
    c[:, C_O128:C_O128 + 128] = 1.0 / 128
    c[:, C_O512:C_O512 + 128] = 1.0 / 512
    c[:, C_ONE:C_ONE + 128] = 1.0
    same = (i[:, None] // 64) == (i[None, :] // 64)
    c[:, C_INC:C_INC + 128] = same & (i[:, None] <= i[None, :])
    c[:, C_INC + 128:C_INC + 256] = same & (i[:, None] >= i[None, :])
    c[:, C_COL:C_COL + 4] = [EPS, 1.0, 0.0, -0.5]
    for g in range(4):
        c[32 * g:32 * g + 2, C_STK:C_STK + 2] = np.eye(2)
    return c


def lay(w):
    return w.reshape(-1, 128, w.shape[1]).transpose(1, 0, 2).reshape(128, -1)


def cols(v):
    return v.reshape(-1, 128).T


def kernel(**inputs):
    import concourse.bacc as bacc
    from concourse.bass_utils import run_bass_kernel_spmd as run

    I = {k: np.asarray(v) for k, v in inputs.items()}
    perm = np.concatenate([np.arange(64 * h, 64 * h + 64) for h in HEADS])
    pieces = {}
    for l in range(2):
        wi = I["w_in"][l]
        for j in range(6):
            pieces[f"a{l}ada{j}"] = lay(I["w_ada"][l][:, 512 * j:512 * j + 512])
        pieces[f"a{l}qa"] = lay(wi[:, 0:512][:, perm])
        pieces[f"a{l}kv"] = lay(np.concatenate([wi[:, 512:768], wi[:, 2304:2336]], 1))
        for n, o in (("gqk", 1280), ("gv", 1792), ("gg", 2336), ("su", 2848), ("sv", 3360), ("sg", 3872)):
            pieces[f"a{l}{n}"] = lay(wi[:, o:o + 512])
        pieces[f"a{l}ag"] = lay(wi[:, 768:1280][:, perm])
        for j in range(2):
            for n, b, wb in ((0, "a", I["w_br_attn"][l][perm]), (1, "g", I["w_br_gla"][l]), (2, "s", I["w_br_sgu"][l])):
                o = 4384 + 1024 * n + 512 * j
                pieces[f"a{l}m{b}{j}"] = lay(wi[:, o:o + 512])
                pieces[f"a{l}b{b}{j}"] = lay(wb[:, 512 * j:512 * j + 512])
            pieces[f"a{l}o{j}"] = lay(I["w_out"][l][:, 512 * j:512 * j + 512])
        wi = I["w_in_2"][l]
        for j in range(3):
            pieces[f"b{l}q{j}"] = lay(wi[:, 512 * j:512 * j + 512])
        ab = np.zeros((1024, 100), np.float32)
        for n in range(4):
            ab[:, 32 * n:32 * n + 4] = wi[:, 2048 + 4 * n:2052 + 4 * n]
        pieces[f"b{l}ab"] = lay(ab)
        for n, o in (("za", 1536), ("cv", 2064), ("cg", 2576), ("zb", 3088)):
            pieces[f"b{l}{n}"] = lay(wi[:, o:o + 512])
        for j in range(2):
            for b, wb in ((0, I["w_dn_out_2"][l]), (1, I["w_cf_out_2"][l])):
                o = 3600 + 1024 * b + 512 * j
                pieces[f"b{l}m{b}{j}"] = lay(wi[:, o:o + 512])
                pieces[f"b{l}b{b}{j}"] = lay(wb[:, 512 * j:512 * j + 512])
            pieces[f"b{l}o{j}"] = lay(I["w_out_2"][l][:, 512 * j:512 * j + 512])
    wf = np.concatenate([pieces[n].reshape(-1) for n, _ in PLAN])
    assert wf.size == 128 * sum(w for _, w in PLAN)

    pa = np.zeros((2, 128, PA_W), np.float32)
    ra = np.zeros((2, RA_W), np.float32)
    rp = np.zeros((2, 2048), np.float32)
    pb = np.zeros((2, 128, PB_W), np.float32)
    for l in range(2):
        pa[l][:, 0:24] = cols(I["b_ada"][l])
        pa[l][:, PA_AB:PA_AB + 2] = cols(I["gla_ab_f"][l])
        pa[l][:, PA_AB + 2:PA_AB + 4] = cols(I["gla_ab_b"][l])
        pa[l][:, PA_ON] = I["gla_o_norm"][l]
        pa[l][0:16, PA_PM:PA_PM + 256] = I["gla_a2_f"][l]
        pa[l][16:32, PA_PM + 256:PA_PM + 512] = I["gla_a2_b"][l]
        pa[l][96, PA_PM:PA_PM + 512] = I["sgu_b"][l].reshape(-1)
        pa[l][:, PA_SW:PA_SW + 512] = I["sgu_w"][l].transpose(2, 0, 1).reshape(128, 512)
        ra[l][0:512] = np.tile(I["attn_q_norm"][l], 8)
        ra[l][512:640] = np.tile(I["attn_k_norm"][l], 2)
        pa[l][:, PA_LG:PA_LG + 4] = cols(I["sgu_ln_g"][l])
        pa[l][64, PA_PM:PA_PM + 512] = I["sgu_ln_b"][l]
        pa[l][65, PA_PM:PA_PM + 512] = 1.0
        rp[l][0:1024] = I["post_ln_g"][l]
        rp[l][1024:2048] = I["post_ln_b"][l]
        q = pb[l]
        q[:, PB_NW:PB_NW + 8] = cols(I["norm_w_2"][l])
        q[:, PB_CW:PB_CW + 60] = I["qkv_conv_w_2"][l].T.reshape(12, 128, 5).transpose(1, 0, 2).reshape(128, 60)
        q[:, PB_FW:PB_FW + 124] = I["cf_conv_w_2"][l].T.reshape(4, 128, 31).transpose(1, 0, 2).reshape(128, 124)
        q[:, PB_FB:PB_FB + 4] = cols(I["cf_conv_b_2"][l])
        q[:, PB_LW:PB_LW + 4] = cols(I["cf_ln_w_2"][l])
        q[:, PB_LB:PB_LB + 4] = cols(I["cf_ln_b_2"][l])
        q[:, PB_GB:PB_GB + 16] = cols(I["gate_b_2"][l])
        q[:, PB_DN] = I["dn_norm_w_2"][l]
        for d in range(2):
            q[32 * d:32 * d + 4, PB_AL] = I["a_log_2"][l][d]
            q[32 * d:32 * d + 4, PB_DT] = I["dt_bias_2"][l][d]

    both = np.concatenate([I["ctx"][0], I["x"][0]], 0)
    data = {
        "wf": wf, "consts": make_consts(),
        "cT": np.stack([cols(I["c"][0]), cols(I["c_ctx"])], 2).reshape(128, 16),
        "xin": both.reshape(4, 128, 1024).transpose(1, 0, 2).reshape(128, 4096),
        "xinT": both.T.reshape(8, 128, 512).transpose(1, 0, 2).reshape(128, 4096),
        "pa": pa, "ra": ra, "rp": rp, "pb": pb, "rfin": I["final_norm_w_2"],
    }
    nc = bacc.Bacc("TRN2", target_bir_lowering=False, num_devices=1)
    arrays, args = {}, []
    for name, a in data.items():
        a = np.ascontiguousarray(a)
        arrays[f"in_{name}"] = a
        args.append(nc.dram_tensor(f"in_{name}", a.shape, mybir.dt.from_np(a.dtype), kind="ExternalInput").ap())
    o = nc.dram_tensor("out_0", (256, 1024), F, kind="ExternalOutput").ap()
    build_program(nc, *args, o)
    r = run(nc, [arrays], core_ids=[0])
    return r.results[0]["out_0"].reshape(1, 256, 1024)
```

```python
from contextlib import ExitStack

import numpy as np

import concourse.bass as bass
from concourse import mybir

F = mybir.dt.float32
U32 = mybir.dt.uint32
ALU = mybir.AluOpType
ACT = mybir.ActivationFunctionType
AX = mybir.AxisListType.X

D = 1024
ALPHA = 4.0 ** 0.25
X_T = 53200 - 4096
EPS = 1e-6
MS = (1, 2, 4, 8, 16, 32)
HEADS = (0, 4, 1, 5, 2, 6, 3, 7)

COST = {"V": (0.25, 0.001), "A": (0.25, 0.0008), "G": (0.2, 0.002), "P": (0.03, 0.0017)}
LATENCY = 0.0
SLACK = (0.2, 0.3, 0.3)
IDLE = 1.0
AHEAD = 4.0
CHAIN = 0.1
GFIRST = [False, False]

UNIT = 2048
NU = 7

C_ID, C_MASK, C_COS, C_SIN, C_SCAN, C_O128, C_O512, C_INC, C_COL, C_STK = (
    0, 128, 1664, 1792, 1920, 2432, 2560, 2688, 2944, 2948)
C_W = 2952

PA_BADA, PA_AB, PA_ON, PA_LG, PA_PM, PA_SW, PA_W = 0, 24, 28, 29, 40, 552, 1064
RA_QK, RA_W = 0, 640
PB_NW, PB_CW, PB_FW, PB_FB, PB_LW, PB_LB, PB_GB, PB_DN, PB_AL, PB_DT, PB_W = (
    0, 8, 68, 192, 196, 200, 204, 220, 221, 222, 224)


ADA = [(0, 4), (0, 5)] + [(1, j) for j in range(6)]


EARLY = [[("a", 0)], [("a", 0), ("g", 0), ("s", 0), ("a", 1), ("g", 1)]]


def plan_a(l):
    first = (("qa", 4096), ("kv", 8 * 288))
    out = [(f"a{l}{n}", w) for n, w in (first if l == 0 else first[::-1]) + (("gqk", 4096), ("gv", 4096), ("ag", 4096),
                                        ("gg", 4096), ("su", 4096), ("sg", 4096), ("sv", 4096))]
    if l == 0:
        for n, (m, j) in enumerate(ADA):
            out.insert(2 * n + 1, (f"a{m}ada{j}", 4096))
    out += [(f"a{l}m{b}{j}", 4096) for b, j in EARLY[l]]
    for j in range(2):
        for b in "ags":
            if (b, j) not in EARLY[l]:
                out += [(f"a{l}m{b}{j}", 4096)]
            out += [(f"a{l}b{b}{j}", 2048)]
    return out + [(f"a{l}o{j}", 4096) for j in range(2)]


def plan_b(l):
    out = [(f"b{l}{n}", w) for n, w in (("ab", 800), ("q0", 4096), ("q1", 4096), ("q2", 4096), ("za", 4096),
                                        ("cv", 4096), ("cg", 4096), ("zb", 4096))]
    out += [(f"b{l}m{b}{j}", 4096) for b, j in ((0, 0), (1, 0), (0, 1))]
    out += [(f"b{l}b0{j}", 2048) for j in range(2)] + [(f"b{l}m11", 4096)]
    out += [(f"b{l}b1{j}", 2048) for j in range(2)]
    return out + [(f"b{l}o{j}", 4096) for j in range(2)]


PLAN = [(f"a0ada{j}", 4096) for j in (0, 2, 1, 3)] + plan_a(0) + plan_a(1) + plan_b(0) + plan_b(1)


class Engine:

    def __init__(self, sem, chained, plan, fixed, per):
        self.sem, self.chained, self.n, self.seen, self.todo = sem, chained, 0, {}, []
        self.plan, self.fixed, self.per, self.t = plan, fixed, per, 0.0

    def put(self, fn, waits, inc=True, size=0, loose=False):
        flat = []

        def add(w):
            if w is None:
                return
            if isinstance(w, list):
                for x in w:
                    add(x)
            else:
                flat.append(w)

        add(list(waits))
        if self.chained and self.n and not loose:
            flat.append((self.sem, self.n))
        need = {}
        for sem, v in flat:
            if self.seen.get(id(sem), 0) < v and need.get(id(sem), (sem, 0))[1] < v:
                need[id(sem)] = (sem, v)
        for sem, v in need.values():
            self.seen[id(sem)] = v
        if inc:
            self.n += 1
        self.t = max([self.t] + [self.plan.at.get((id(sem), v), 0.0) for sem, v in need.values()])
        self.t += self.fixed + self.per * size - (CHAIN if loose else 0.0)
        if inc:
            self.plan.at[(id(self.sem), self.n)] = self.t + LATENCY
            self.plan.emitted = max(self.plan.emitted, self.t + LATENCY)
        self.todo.append((list(need.values()), fn, inc))
        return (self.sem, self.n)


class Plan:

    def __init__(self):
        self.at, self.emitted = {}, 0.0

    def time(self, tokens):
        t = 0.0
        for x in tokens:
            if isinstance(x, list):
                t = max(t, self.time(x))
            elif x is not None:
                t = max(t, self.at.get((id(x[0]), x[1]), 0.0))
        return t


class Bank:
    def __init__(self, t):
        self.t, self.free = t, []


class Pool:

    def __init__(self, banks):
        self.banks, self.i = banks, 0

    def take(self):
        b = self.banks[self.i % len(self.banks)]
        self.i += 1
        return b


def weave(plan, P, slack, *parts, idle=None):
    live = [[g, 0.0, False] for g in parts]
    spare, spare_engine = (live[idle[0]], idle[1]) if idle else (None, None)
    filler = live[-1]
    while live:
        able = [it for it in live if not it[2]]
        it = next((x for x in able if x[1] <= P.t + slack and (x is not spare or spare_engine.t <= P.t + IDLE)),
                  None) or min(able, key=lambda x: x[1])
        plan.emitted = 0.0
        try:
            more = next(it[0])
        except StopIteration:
            live.remove(it)
            continue
        if more == "blocked":
            it[2] = True
            if all(x[2] for x in live):
                raise RuntimeError("every stream waits")
            continue
        if it is filler:
            it[1] = P.t
        elif isinstance(more, list):
            it[1] = plan.time(more)
        else:
            it[1] = plan.emitted - (AHEAD if more == "ahead" else 0.0)
        for x in live:
            x[2] = False


def drain(g):
    for _ in g:
        pass


def build_program(nc, wf, consts, cT, xin, xinT, pa, ra, rpost, pb, rfin, out):
    with ExitStack() as ctx:
        arena = ctx.enter_context(nc.sbuf_tensor("arena", [128, 53200], F))
        top = [0]

        def al(n):
            o = top[0]
            top[0] += n
            assert top[0] <= 53200, top[0]
            return arena[:, o:o + n]

        def sem(name):
            return ctx.enter_context(nc.semaphore(name))

        k_scs = [None, None]
        k_next = [None]
        PS = [Bank(ctx.enter_context(nc.psum_tensor(f"ps{i}", [128, 512], F))[:, :]) for i in range(8)]

        plan = Plan()
        V = Engine(sem("s_v"), True, plan, *COST["V"])
        A = Engine(sem("s_a"), True, plan, *COST["A"])
        G = Engine(sem("s_g"), True, plan, *COST["G"])
        P = Engine(sem("s_p"), False, plan, *COST["P"])
        S = Engine(sem("s_sp"), False, plan, 0.0, 0.0)
        dman = [0]

        def size_of(ap):
            return int(np.prod(ap.shape[1:]))

        def mm(o, l, r, start, stop, *w, inc=False):
            return P.put(lambda e: e.matmul(o, l, r, start=start, stop=stop, skip_group_check=True), w, inc, size_of(o))

        def tr(o, i, idn, *w, inc=False):
            return P.put(lambda e: e.transpose(o, i, idn), w, inc, size_of(o))

        def tt(E, o, a, b, op, *w, loose=False):
            return E.put(lambda e: e.tensor_tensor(o, a, b, op), w, size=size_of(o) * (100 if op == ALU.pow else 1),
                         loose=loose)

        def ts(E, o, a, s1, s2, op0, op1, *w, loose=False):
            if s2 is None:
                return E.put(lambda e: e.tensor_scalar(o, a, s1, None, op0), w, size=size_of(o), loose=loose)
            return E.put(lambda e: e.tensor_scalar(o, a, s1, s2, op0, op1), w, size=size_of(o), loose=loose)

        def stt(E, o, a, s, b, op0, op1, *w, loose=False):
            return E.put(lambda e: e.scalar_tensor_tensor(out=o, in0=a, scalar=s, in1=b, op0=op0, op1=op1), w,
                         size=size_of(o), loose=loose)

        def act(o, i, f, *w, bias=None, scale=None, acc=None):
            kw = {}
            if bias is not None:
                kw["bias"] = bias
            if scale is not None:
                kw["scale"] = scale
            if acc is not None:
                kw["accum_out"] = acc
            return A.put(lambda e: e.activation(o, i, f, **kw), w, size=size_of(o))

        def cp(E, o, i, *w):
            return E.put(lambda e: e.tensor_copy(o, i), w, size=size_of(o))

        def ms(E, o, v, *w):
            return E.put(lambda e: e.memset(o, v), w, size=size_of(o))

        def pred(o, mask, data, *w, loose=False):
            return V.put(lambda e: e.copy_predicated(o, mask, data), w, size=size_of(o), loose=loose)

        def dma(o, i, *w, s=None):
            if s is None:
                s = sem(f"s_d{dman[0]}")
                dman[0] += 1

            def go(e):
                e.dma_start(o, i).then_inc(s, 16)

            S.put(go, w, inc=False)
            if (id(s), 16) not in plan.at:
                st["t"] = max(st["t"], P.t) + size_of(o) * o.shape[0] * 4 / 330e3
                plan.at[(id(s), 16)] = st["t"] + 2.0
            return (s, 16)

        def r3(ap, n):
            return ap.rearrange("p (a b) -> p a b", a=n)

        ring = al(NU * UNIT)
        st = {"next": 0, "at": 0, "off": 0, "t": 0.0}
        usem = [sem(f"s_u{i}") for i in range(NU)]
        ucount = [0] * NU
        ufree = [[] for _ in range(NU)]
        ubusy = [False] * NU
        loaded = {}

        def fill(most=len(PLAN)):
            while st["next"] < len(PLAN) and most:
                most -= 1
                name, w = PLAN[st["next"]]
                k = -(-w // UNIT)
                at = st["at"] if st["at"] + k <= NU else 0
                if any(ubusy[at:at + k]):
                    return
                for u in range(at, at + k):
                    ubusy[u] = True
                off = st["off"]
                dst, src = ring[:, at * UNIT:at * UNIT + w], wf[off:off + 128 * w].rearrange("(p n) -> p n", p=128)
                waits = [t for u in range(at, at + k) for t in ufree[u]]
                dma(dst, src, waits, s=usem[at])
                ucount[at] += 16
                loaded[name] = (dst, (usem[at], ucount[at]), at, k)
                st["t"] = max([st["t"], P.t] + [plan.at.get((id(a), v), 0.0) for a, v in waits]) + 128 * w * 4 / 330e3
                plan.at[(id(usem[at]), ucount[at])] = st["t"] + 2.0
                st["next"] += 1
                st["at"] = (at + k) % NU
                st["off"] += 128 * w

        def use(name):
            fill()
            return loaded[name][0], loaded[name][1]

        def release(name, tok):
            _, _, at, k = loaded[name]
            for u in range(at, at + k):
                ubusy[u] = False
                ufree[u] = [tok]
            fill()

        cst = al(C_W)
        ident = cst[:, C_ID:C_ID + 128]

        def mask(m, swapped):
            o = C_MASK + (2 * MS.index(m) + swapped) * 128
            return cst[:, o:o + 128].bitcast(U32)

        o128 = cst[:, C_O128:C_O128 + 128]
        o512 = cst[:, C_O512:C_O512 + 128]
        eps = cst[:, C_COL:C_COL + 1]
        one = cst[:, C_COL + 1:C_COL + 2]
        zero = cst[:, C_COL + 2:C_COL + 3]
        mhalf = cst[:, C_COL + 3:C_COL + 4]
        X = al(2048)
        cc = al(16)
        cs = al(16)
        st2 = al(4)
        PT4 = [X[:, 512 * i:512 * i + 512] for i in range(2)]
        SCOL = [al(48), al(48)]
        BADA = al(48)
        base = top[0]
        k_c = dma(cc, cT)
        fill(1)
        k_bada = [dma(BADA[:, 24 * l:24 * l + 24], pa[l][:, 0:24]) for l in range(2)]
        fill(1)
        k_cst = dma(cst, consts)
        fill()
        act(cs, cc, ACT.Tanh, k_c, scale=0.5)
        k = stt(V, cs, cs, 1.0, cc, ALU.add, ALU.mult, (A.sem, A.n), k_c)
        k_cs = ts(V, cs, cs, 0.5, None, ALU.mult, None, k)
        k_pt4 = [ms(V, PT4[i], 0.0) for i in range(2)]
        cs3 = r3(cs, 8)

        def await_constants(*engines):
            for E in engines:
                E.todo.append(([k_cst], None, False))
                E.seen[id(k_cst[0])] = 16
                E.t = max(E.t, plan.at[(id(k_cst[0]), 16)])

        def rows_of(w, n):
            return w.rearrange("p (k n) -> p k n", k=n)

        def feat(bank, w, n, c0, cols, hT, t0, t1, nk, waits, m=128, o=0, start=True, stop=True, kh=None):
            tok = None
            for k in range(nk):
                tok = mm(bank.t[0:m, o:o + t1 - t0], w[:, k, c0:c0 + m], hT[:, k, t0:t1],
                         start and k == 0, stop and k == nk - 1, waits if k == 0 else None, kh[k] if kh else None,
                         inc=(k == nk - 1))
            return tok

        def token(bank, w, c0, c1, hT, t0, waits, nk=8, kh=None):
            tok = None
            for k in range(nk):
                tok = mm(bank.t[:, 0:c1 - c0], hT[:, k, t0:t0 + 128], w[:, k, c0:c1],
                         k == 0, k == nk - 1, waits if k == 0 else None, kh[k] if kh else None, inc=(k == nk - 1))
            return tok

        def ada(pool, js, lag=False):
            def first(n, l, j):
                w, kw = use(f"a{l}ada{j}")
                w = rows_of(w, 8)
                b = pool.take()
                for kk in range(8):
                    g = 32 * (kk % 4)
                    k = mm(b.t[g:g + 2, :], cs3[:, kk, :], w[:, kk, :], kk < 4, kk >= 4,
                           [kw, k_cs, b.free] if kk == 0 else None, inc=kk >= 4)
                release(f"a{l}ada{j}", k)
                for g in range(4):
                    kr = act(PT4[n % 2][32 * g:32 * g + 2, :], b.t[32 * g:32 * g + 2, :], ACT.Copy, k, k_pt4)
                b.free = [kr]
                return n, l, j, kr

            def second(n, l, j, kr):
                sc3 = r3(SCOL[l], 24)
                b = pool.take()
                for i in range(4):
                    k = mm(b.t[:, 2 * i:2 * i + 2], PT4[n % 2][:, 128 * i:128 * i + 128], cst[:, C_STK:C_STK + 2],
                           i == 0, True, kr, b.free, inc=i == 3)
                k_pt4[n % 2] = k
                one_ = 1.0 if j in (2, 3) else 0.0
                b.free = [stt(V, sc3[:, 4 * j:4 * j + 4, :], r3(b.t[:, 0:8], 4), one_,
                              BADA[:, 24 * l + 4 * j:24 * l + 4 * j + 4].unsqueeze(2).to_broadcast([128, 4, 2]),
                              ALU.add, ALU.add, k, k_bada[l])]

            half = None
            for n, (l, j) in enumerate(js):
                if lag:
                    last, half = half, first(n, l, j)
                    if last:
                        second(*last)
                else:
                    half = first(n, l, j)
                yield
                if not lag or n == len(js) - 1:
                    second(*half)
                    yield

        def rstd_small(o, i, *w):
            n = i.shape[1]
            a = ts(G, o, i, eps, None, ALU.add, None, *w)
            return tt(G, o, o, mhalf.to_broadcast([128, n]), ALU.pow, a)

        def rstd_big(o, i, *w):
            act(o, i, ACT.Ln, *w, bias=eps)
            return act(o, o, ACT.Exp, scale=-0.5)

        def layer_a(l, k_x, k_pre, k_tile):
            top[0] = base
            hT = r3(al(4096), 8)
            qkv_gv = al(5120)
            QKV = r3(qkv_gv[:, 0:3072], 4)
            GV = r3(qkv_gv[:, 3072:5120], 4)
            mT = r3(qkv_gv[:, 0:4096], 8)
            AG, GG, SG = (r3(al(2048), 4) for _ in range(3))
            GQ, GK = (r3(al(1024), 2) for _ in range(2))
            par = al(PA_SW)
            row = al(640)
            TH = al(512)
            TH2 = al(512)
            s0 = top[0]
            l0 = 0 if l == 0 else 256
            tiles = range(4) if l == 0 else range(2, 4)

            k_par = dma(par, pa[l][:, 0:PA_SW], k_x)
            k_row = dma(row, ra[l][0:640].partition_broadcast(128), k_x)
            PM = par[:, PA_PM:PA_PM + 512]
            DP, AP, GP = Pool(PS[0:3]), Pool(PS[3:5]), Pool(PS[5:8])
            VN = [al(512) for _ in range(2)]
            SW = al(512)
            BT = al(512)
            bs = al(32)
            s0 = top[0]
            k_sw = dma(SW, pa[l][:, PA_SW:PA_W], k_x)
            k_bs = dma(BT[65:66, :], pa[l][96:97, PA_PM:PA_PM + 512], k_x)

            if l == 0:
                start = ada(DP, [(0, j) for j in (0, 2, 1, 3)], lag=True)
                next(start)
                k_xt = dma(arena[:, X_T:X_T + 4096], xinT)
                await_constants(P)
                drain(start)
                await_constants(A, V, G)
            if l == 0:
                k_scs[0] = (V.sem, V.n)
            k_sc = k_scs[l]
            sc3 = r3(SCOL[l], 24)

            k_hk = []
            if l == 0:
                top[0] = s0
                assert s0 <= X_T
                xT = r3(arena[:, X_T:X_T + 4096], 8)
                for kk in range(8):
                    k_hk.append([])
                    for s in range(2):
                        c = 1 - s
                        o, x = hT[:, kk, 256 * s:256 * s + 256], xT[:, kk, 256 * s:256 * s + 256]
                        a_, b_ = sc3[:, 8 + kk, c:c + 1], sc3[:, kk, c:c + 1]
                        if s or kk % 4 == 3:
                            k = ts(V, o, x, a_, b_, ALU.mult, ALU.add, k_xt, k_sc)
                        elif kk % 4 == 1:
                            k = ts(G, o, x, a_, b_, ALU.mult, ALU.add, k_xt, k_sc)
                        else:
                            k = act(o, x, ACT.Identity, k_xt, k_sc, scale=a_, bias=b_)
                        k_hk[kk].append(k)
            else:
                TP = Pool(AP.banks + GP.banks)
                for s in range(2):
                    c = 1 - s
                    for kp_ in range(4):
                        b = TP.take()
                        for i in range(4):
                            kk, t = 2 * kp_ + i // 2, i % 2
                            src = (X if s else CX)[:, 1024 * t + 128 * kk:1024 * t + 128 * kk + 128]
                            k = tr(b.t[:, 128 * i:128 * i + 128], src, ident, k_tile[2 * s + t], k_pre, b.free,
                                   inc=i == 3)
                        for i in range(2):
                            kk = 2 * kp_ + i
                            o, x, a_, b_ = (hT[:, kk, 256 * s:256 * s + 256], b.t[:, 256 * i:256 * i + 256],
                                            sc3[:, 8 + kk, c:c + 1], sc3[:, kk, c:c + 1])
                            if s:
                                k2 = ts(V, o, x, a_, b_, ALU.mult, ALU.add, k, k_sc)
                                k_hk[kk].append(k2)
                            else:
                                k2 = act(o, x, ACT.Identity, k, k_sc, k_pre, scale=a_, bias=b_)
                                k_hk.append([k2])
                        b.free = [k2]
            k_h = [(V.sem, V.n), (G.sem, G.n), (A.sem, A.n)]
            top[0] = s0
            done = {}

            later = ada(DP, ADA) if l == 0 else iter(())

            def ada_next():
                for _ in range(2 if done.get("ada") else 1):
                    next(later, None)
                done["ada"] = True
                yield

            early = {}
            if l == 0:
                spare = [X[:, 512 * c:512 * c + 512] for c in range(4)]
            else:
                spare = [qkv_gv[:, 256:512], qkv_gv[:, 768:1024], qkv_gv[:, 0:256], qkv_gv[:, 1024:1280]]
                spare += [y[:, c, 0:256] for y in (AG, GG, SG) for c in range(4)]
                spare += [GQ[:, c, 0:256] for c in range(2)]

            def dense():
                def queries():
                    w, kw = use(f"a{l}qa")
                    w = rows_of(w, 8)
                    for t in tiles:
                        b = DP.take()
                        k = token(b, w, 0, 512, hT, 128 * t, [kw, b.free], kh=k_hk)
                        b.free = [act(QKV[:, t, 0:512], b.t, ACT.Copy, k)]
                        done[f"q{t}"] = b.free
                        yield
                    release(f"a{l}qa", k)
                    yield from ada_next()

                def keys():
                    w, kw = use(f"a{l}kv")
                    w = rows_of(w, 8)
                    for t in range(4):
                        b = DP.take()
                        k = token(b, w, 0, 256, hT, 128 * t, [kw, b.free],
                                  kh=[x[t // 2] if l else x for x in k_hk])
                        b.free = [act(QKV[:, t, 512:768], b.t[:, 0:256], ACT.Copy, k)]
                        done[f"kv{t}"] = b.free
                        yield
                    b = DP.take()
                    k = feat(b, w, 8, 256, 32, hT, 0, 512, 8, [b.free], m=32, kh=k_hk)
                    b.free = [act(TH2[0:32, :], b.t[0:32, :], ACT.Copy, k)]
                    done["lr"] = b.free
                    release(f"a{l}kv", k)
                    yield from ada_next()
                    yield

                for part in (queries, keys) if l == 0 else (keys, queries):
                    yield from part()
                w, kw = use(f"a{l}gqk")
                w = rows_of(w, 8)
                for c in range(4):
                    b = DP.take()
                    k = feat(b, w, 8, 128 * c, 128, hT, l0 if c < 2 else 0, 512, 8, [kw, b.free])
                    if c < 2:
                        b.free = [act(GQ[:, c, l0:512], b.t[:, 0:512 - l0], ACT.Copy, k, scale=0.125)]
                    else:
                        b.free = [act(GK[:, c - 2, :], b.t, ACT.Copy, k)]
                    yield
                release(f"a{l}gqk", k)
                yield from ada_next()
                done["gqk"] = b.free
                w, kw = use(f"a{l}gv")
                w = rows_of(w, 8)
                for t in range(4):
                    b = DP.take()
                    k = token(b, w, 0, 512, hT, 128 * t, [kw, b.free])
                    b.free = [act(GV[:, t, :], b.t, ACT.Copy, k)]
                    if t == 3:
                        done["gv"] = b.free
                    yield
                release(f"a{l}gv", k)
                yield from ada_next()
                for name, dst in (("ag", AG), ("gg", GG)):
                    w, kw = use(f"a{l}{name}")
                    w = rows_of(w, 8)
                    for c in range(4):
                        b = DP.take()
                        k = feat(b, w, 8, 128 * c, 128, hT, l0, 512, 8, [kw, b.free])
                        n = 512 - l0
                        k1 = act(TH[:, 0:n], b.t[:, 0:n], ACT.Tanh, k, done.get("th"), scale=0.5)
                        k2 = stt(V, dst[:, c, l0:512], TH[:, 0:n], 1.0, b.t[:, 0:n], ALU.add, ALU.mult, k1)
                        b.free = [k2]
                        done["th"] = k2
                        done[f"{name}{c}"] = k2
                        yield
                    release(f"a{l}{name}", k)
                    yield from ada_next()
                n = 512 - l0
                for name in ("su", "sg"):
                    w, kw = use(f"a{l}{name}")
                    w = rows_of(w, 8)
                    for c in range(4):
                        b = DP.take()
                        k = feat(b, w, 8, 128 * c, 128, hT, l0, 512, 8, [kw, b.free])
                        g = SG[:, c, l0:512]
                        if name == "su":
                            b.free = [act(g, b.t[:, 0:n], ACT.Copy, k)]
                            done[f"su{c}"] = b.free
                        else:
                            k1 = act(TH[:, 0:n], b.t[:, 0:n], ACT.Tanh, k, done.get("th"), scale=0.5)
                            k2 = stt(V, TH[:, 0:n], TH[:, 0:n], 1.0, b.t[:, 0:n], ALU.add, ALU.mult, k1)
                            b.free = [k2]
                            done["th"] = tt(V, g, g, TH[:, 0:n], ALU.mult, done[f"su{c}"])
                            done["sg"] = done["th"]
                        yield
                    release(f"a{l}{name}", k)
                    yield from ada_next()
                w, kw = use(f"a{l}sv")
                w = rows_of(w, 8)
                b = DP.take()
                k = mm(b.t[0:1, :], one, SW, True, True, k_sw, b.free, inc=True)
                kr = cp(V, BT[64:65, :], b.t[0:1, :], k)
                b.free = [kr]
                yield
                b = DP.take()
                for g in range(4):
                    k = mm(b.t[:, 128 * g:128 * g + 128], PM[64:66, 128 * g:128 * g + 128],
                           BT[64:66, 128 * g:128 * g + 128], g == 0, True, kr, k_bs, k_par, b.free, inc=g == 3)
                kbt = act(BT, b.t, ACT.Copy, k)
                b.free = [kbt]
                yield
                def normed(t):
                    x, q = VN[t % 2], bs[:, 16 * (t % 2):16 * (t % 2) + 9]
                    b = DP.take()
                    kp = token(b, w, 0, 512, hT, 128 * t, [kw, b.free])
                    k = act(x, b.t, ACT.Copy, kp, done.get(f"vn{t % 2}"), k_h)
                    b.free = [k]
                    V.put(lambda e: e.bn_stats(q[:, 0:6], x), [k])
                    k = V.put(lambda e: e.bn_aggr(q[:, 6:8], q[:, 0:6]), [])
                    kr = rstd_small(q[:, 8:9], q[:, 7:8], k)
                    return ts(V, x, x, q[:, 6:7], q[:, 8:9], ALU.subtract, ALU.mult, kr), kp

                def mixed(t, k):
                    x = VN[t % 2]
                    b = DP.take()
                    for g in range(4):
                        k2 = mm(b.t[:, 128 * g:128 * g + 128], x[:, 128 * g:128 * g + 128],
                                SW[:, 128 * g:128 * g + 128], g == 0, True, k, k_sw, b.free, inc=g == 3)
                    done[f"vn{t % 2}"] = k2
                    y = TH[:, 0:512]
                    for g in range(4):
                        cg = slice(128 * g, 128 * g + 128)
                        k = stt(V, y[:, cg], b.t[:, cg], par[:, PA_LG + g:PA_LG + g + 1], BT[:, cg], ALU.mult, ALU.add,
                                k2, kbt, k_par, loose=g > 0)
                    b.free = [k]
                    z = SG[:, :, 128 * t:128 * t + 128]
                    done["th"] = done["ys"] = stt(V, z, r3(y, 4), 0.5, z, ALU.mult, ALU.mult)

                wait = []
                for t in tiles:
                    kn, kp = normed(t)
                    wait.append((t, kn))
                    yield
                    if len(wait) > 1:
                        mixed(*wait.pop(0))
                        yield
                release(f"a{l}sv", kp)
                yield
                mixed(*wait.pop(0))
                yield from ada_next()
                for br, j in EARLY[l]:
                    w, kw = use(f"a{l}m{br}{j}")
                    w = rows_of(w, 8)
                    for c in range(4):
                        b = DP.take()
                        k = feat(b, w, 8, 128 * c, 128, hT, l0, 512, 8, [kw, b.free])
                        sg = spare[len(early)]
                        b.free = [act(sg, b.t[:, 0:n], ACT.Tanh, k, k_pt4, k_h, k_x, scale=0.5)]
                        early[(br, j, c)] = (sg, b.free)
                        yield
                    release(f"a{l}m{br}{j}", k)

            def attention(scr):
                stat = scr(10)
                KT = scr(512)
                QT = scr(512)
                Pb = [scr(512) for _ in range(2)]
                PT = [scr(1024) for _ in range(2)]
                sq, qk2 = PT[0][:, 0:640], PT[1][:, 0:640]
                small = [scr(4) for _ in range(2)]
                for t in range(4):
                    while f"kv{t}" not in done or (t in tiles and f"q{t}" not in done):
                        yield "blocked"
                    wq = done[f"q{t}"] if t in tiles else None
                    lo = 0 if t in tiles else 512
                    nh = (640 - lo) // 64
                    w = [wq, done[f"kv{t}"]]
                    x = QKV[:, t, lo:640]
                    x3 = r3(x, nh)
                    k = tt(G, sq[:, lo:640], x, x, ALU.mult, w, (V.sem, V.n))
                    k = V.put(lambda e, a=stat[:, lo // 64:10], b=r3(sq[:, lo:640], nh): e.tensor_reduce(a, b, AX, ALU.add),
                              [k, (G.sem, G.n)])
                    k = ts(V, stat[:, lo // 64:10], stat[:, lo // 64:10], 1.0 / 64, None, ALU.mult, None)
                    yield
                    kr = rstd_small(stat[:, lo // 64:10], stat[:, lo // 64:10], k)
                    tt(V, x, x, row[:, RA_QK + lo:RA_QK + 640], ALU.mult, k_row, w, kr)
                    k = tt(V, x3, x3, stat[:, lo // 64:10].unsqueeze(2).to_broadcast([128, nh, 64]), ALU.mult, kr)
                    if t >= 2:
                        cos = cst[:, C_COS + 64 * (t - 2):C_COS + 64 * (t - 1)].unsqueeze(1).to_broadcast([128, 10, 64])
                        sn = cst[:, C_SIN + 64 * (t - 2):C_SIN + 64 * (t - 1)]
                        x5 = x.rearrange("p (h a b c) -> p h a b c", h=10, a=2, b=2)
                        q5 = qk2.rearrange("p (h a b c) -> p h a b c", h=10, a=2, b=2)
                        s4 = sn.rearrange("p (a b c) -> p a b c", a=2, b=2)
                        for hf in range(2):
                            kg = tt(G, q5[:, :, :, hf, :], x5[:, :, :, 1 - hf, :],
                                    s4[:, :, hf, :].unsqueeze(1).to_broadcast([128, 10, 2, 16]), ALU.mult, k,
                                    done.get("qk2"))
                        k = tt(V, x3, x3, cos, ALU.mult, kg)
                        k = tt(V, x, x, qk2, ALU.add, kg)
                        done["qk2"] = k
                    done[f"n{t}"] = k
                    yield
                b = AP.take()
                for t in range(4):
                    k = tr(b.t[:, 128 * t:128 * t + 128], QKV[:, t, 512:640], ident, done[f"n{t}"], b.free, inc=t == 3)
                k_kt = cp(V, KT, b.t, k)
                b.free = [k_kt]
                yield
                pt_free = [None, None]
                units, ready, num = [], [], [0]

                def scores(c, s, p, i, k_qt):
                    L = 256 + 256 * s
                    t = 2 * s + i
                    b = AP.take()
                    k = mm(b.t[:, 0:L], QTs[c % 2][64 * p:64 * p + 64, 128 * t:128 * t + 128],
                           KT[64 * p:64 * p + 64, 0:L], True, True, k_qt, k_kt, b.free, inc=True)
                    done[f"qt{c % 2}"] = k
                    j = num[0] % 2
                    num[0] += 1
                    sm, pb, wp = small[j], Pb[j], done.get(f"pb{j}")
                    V.put(lambda e, o=sm[:, 0:1], x=b.t[:, 0:L]: e.reduce_max(o, x, AX), [k, wp])
                    k = ts(V, sm[:, 1:2], sm[:, 0:1], -0.125, None, ALU.mult, None)
                    k = act(pb[:, 0:L], b.t[:, 0:L], ACT.Exp, k, wp, bias=sm[:, 1:2], scale=0.125, acc=sm[:, 2:3])
                    b.free = [k]
                    return (c, s, p, i, j, k)

                def weights(u, kpt):
                    c, s, p, i, j, k = u
                    L = 256 + 256 * s
                    sm, pb = small[j], Pb[j]
                    V.put(lambda e, o=sm[:, 3:4], x=sm[:, 2:3]: e.reciprocal(o, x), [k])
                    k = ts(V, pb[:, 0:L], pb[:, 0:L], sm[:, 3:4], None, ALU.mult, None, k)
                    yield
                    b = AP.take()
                    for x in range(L // 128):
                        kt_ = tr(b.t[:, 128 * x:128 * x + 128], pb[:, 128 * x:128 * x + 128], ident, k, b.free,
                                 inc=x == L // 128 - 1)
                    done[f"pb{j}"] = kt_
                    PTp = r3(PT[p], 4)
                    k = act(PTp[:, 0:L // 128, 128 * i:128 * i + 128], r3(b.t[:, 0:L], L // 128), ACT.Copy, kt_,
                            pt_free[p])
                    b.free = [k]
                    kpt.append(k)

                def turn(units, last):
                    while units:
                        c, s, k_qt = units.pop(0)
                        for p in range(2):
                            for i in range(2):
                                ready.append(scores(c, s, p, i, k_qt))
                                yield [ready[0][5]] if len(ready) > 1 else [k_qt]
                                if len(ready) > 1:
                                    u = ready.pop(0)
                                    yield from weights(u, kpts.setdefault(u[:2], []))
                                    yield
                                    if u[2] == 1 and u[3] == 1:
                                        yield from values(u[0], u[1])
                    if last:
                        u = ready.pop(0)
                        yield from weights(u, kpts.setdefault(u[:2], []))
                        yield
                        yield from values(u[0], u[1])

                kpts = {}

                def values(c, s):
                    L = 256 + 256 * s
                    while f"ag{c}" not in done:
                        yield "blocked"
                    b = AP.take()
                    for p in range(2):
                        PTp = r3(PT[p], 4)
                        for j in range(L // 128):
                            k = mm(b.t[64 * p:64 * p + 64, 0:256], QKV[:, j, 640 + 64 * p:704 + 64 * p],
                                   PTp[:, j, :], j == 0, j == L // 128 - 1, kpts[(c, s)], done[f"kv{j}"], b.free,
                                   inc=j == L // 128 - 1)
                        pt_free[p] = k
                    y = AG[:, c, 256 * s:256 * s + 256]
                    k = stt(V, y, b.t[:, 0:256], 0.5, y, ALU.mult, ALU.mult, k, done[f"ag{c}"])
                    b.free = [k]
                    done["ya"] = k
                    yield

                QTs = [QT, QT]
                for c in range(4):
                    QT = QTs[c % 2]
                    b = AP.take()
                    for t in tiles:
                        k = tr(b.t[:, 128 * t:128 * t + 128], QKV[:, t, 128 * c:128 * c + 128], ident,
                               done[f"n{t}"], b.free, inc=t == 3)
                    k_qt = act(QT[:, l0:512], b.t[:, l0:512], ACT.Copy, k, k_kt, done.get("qt0"), done.get("qt1"))
                    b.free = [k_qt]
                    yield
                    for s in ((0, 1) if l == 0 else (1,)):
                        units.append((c, s, k_qt))
                        yield from turn(units, False)
                yield from turn(units, True)

            def gla(scr):
                B = [r3(scr(512), 1) for _ in range(2)]
                EE = [scr(512) for _ in range(2)]
                QK = [scr(512) for _ in range(2)]
                attf = scr(1024)
                att = attf.rearrange("p (t h c) -> p t h c", t=4, h=2)
                KDT = [attf[:, 0:512], attf[:, 512:1024]]
                QB = [scr(512) for _ in range(2)]
                if l == 1:
                    spare.extend(q[:, 0:256] for q in QB)
                ST = scr(2048).rearrange("p (d n v) -> p d n v", d=2, n=8)
                SC = cst[:, C_SCAN:C_SCAN + 512]
                EL = scr(16)
                nt = len(tiles)
                W = 512 - l0
                while "lr" not in done:
                    yield "blocked"
                for hp in range(2):
                    last = done.get("glalast")
                    for d in range(2):
                        b = GP.take()
                        k = mm(b.t, PM[0:32, 256 * d + 128 * hp:256 * d + 128 * hp + 128], TH2[0:32, :], True, True,
                               done["lr"], k_par, b.free, inc=True)
                        k = act(EE[d], b.t, ACT.Identity, k, k_par, last,
                                bias=par[:, PA_AB + 2 * d + hp:PA_AB + 2 * d + hp + 1])
                        b.free = [k]
                        yield
                        act(QK[d], EE[d], ACT.Abs)
                        act(QK[d], QK[d], ACT.Exp, scale=-1.0)
                    for d in range(2):
                        act(QK[d], QK[d], ACT.Ln, bias=one)
                    for d in range(2):
                        k = stt(V, QK[d], EE[d], 0.0, QK[d], ALU.min, ALU.subtract, (A.sem, A.n), last)
                        o, g = B[d][:, 0, :], QK[d]
                        if d:
                            o, g = o[:, ::-1], g[:, ::-1]
                        V.put(lambda e, o=o, g=g: e.tensor_tensor_scan(o, SC, g, 0.0, ALU.mult, ALU.add), [])
                    yield
                    while "gqk" not in done:
                        yield "blocked"
                    kB = (V.sem, V.n)
                    kel = []
                    for d in range(2):
                        b4 = B[d][:, 0, :].rearrange("p (n m) -> p n m", m=64)
                        r = b4[:, :, 0:1] if d else b4[:, :, 63:64]
                        E = EE[d]
                        k = tt(G, r3(E, 8), r.to_broadcast([128, 8, 64]), b4, ALU.subtract, kB)
                        k = act(E, E, ACT.Exp, k, scale=1.0 / 16)
                        kel = act(EL[:, 8 * d:8 * d + 8].unsqueeze(2), r, ACT.Exp, kB, scale=1.0 / 16)
                        k = tt(V, QK[d], GK[:, hp, :], E, ALU.mult, k, last, done["gqk"])
                        yield
                        b = GP.take()
                        for t in range(4):
                            k2 = tr(b.t[:, 128 * t:128 * t + 128], QK[d][:, 128 * t:128 * t + 128], ident, k, b.free,
                                    inc=t == 3)
                        k = act(KDT[d], b.t, ACT.Copy, k2, last)
                        b.free = [k]
                        k2 = act(QB[d][:, l0:512], B[d][:, 0, l0:512], ACT.Exp, kB, last, scale=1.0 / 16)
                        tt(V, QB[d][:, l0:512], QB[d][:, l0:512], GQ[:, hp, l0:512], ALU.mult, k2)
                        yield
                    kQB = (V.sem, V.n)
                    kKD = (A.sem, A.n)
                    while "gv" not in done:
                        yield "blocked"
                    order = [[0, 1, 2, 3, 4, 5, 6, 7], [3, 2, 1, 0, 7, 6, 5, 4]]
                    for i in range(7):
                        for d in range(2):
                            b = GP.take()
                            n, nx = order[d][i], order[d][i + 1]
                            t, r0 = n // 2, 64 * (n % 2)
                            for p in range(2):
                                h = 2 * hp + p
                                k = mm(b.t[64 * p:64 * p + 64, 0:128],
                                       KDT[d][r0:r0 + 64, 128 * t + 64 * p:128 * t + 64 * p + 64],
                                       GV[r0:r0 + 64, t, 128 * h:128 * h + 128], True, True,
                                       kKD, done["gv"], b.free, inc=True)
                            u = b.t[:, 0:128]
                            if i == 0:
                                k2 = cp(V, ST[:, d, nx, :], u, k, last)
                            else:
                                k2 = stt(V, ST[:, d, nx, :], ST[:, d, n, :], EL[:, 8 * d + n:8 * d + n + 1], u,
                                         ALU.mult, ALU.add, k, kel)
                            b.free = [k2]
                        yield
                    kST, ku = k2, (P.sem, P.n)
                    bp = [GP.take(), GP.take()]
                    k = [None, None]
                    for t in tiles:
                        for p in range(2):
                            k[p] = mm(bp[p].t[:, 128 * t:128 * t + 128], GK[64 * p:64 * p + 64, hp, 128 * t:128 * t + 128],
                                      GQ[64 * p:64 * p + 64, hp, 128 * t:128 * t + 128], t == tiles[0], True,
                                      done["gqk"], bp[p].free, inc=t == 3)
                    for p in range(2):
                        bp[p].free = [stt(V, att[:, tiles[0]:4, p, :], r3(bp[p].t[:, l0:512], nt), 2.0,
                                          ident.unsqueeze(1).to_broadcast([128, nt, 128]), ALU.mult, ALU.mult, k[p],
                                          ku)]
                    yield
                    steps = [(m, d) for m in MS for d in range(2)]
                    ke = [kQB, kQB]

                    def factors(n):
                        m, d = steps[n]
                        e = EE[n % 2]
                        b4 = B[d][:, 0, l0:512].rearrange("p (n s m) -> p n s m", s=2, m=m)
                        e4 = e[:, l0:512].rearrange("p (n s m) -> p n s m", s=2, m=m)
                        r = (b4[:, :, 1, 0:1] if d else b4[:, :, 0, m - 1:m]).to_broadcast([128, W // (2 * m), m])
                        hk, hq = (1, 0) if d else (0, 1)
                        tt(G, e4[:, :, hk, :], r, b4[:, :, hk, :], ALU.subtract, ke[n % 2])
                        k = tt(G, e4[:, :, hq, :], b4[:, :, hq, :], r, ALU.subtract, loose=True)
                        k = act(e[:, l0:512], e[:, l0:512], ACT.Exp, k, scale=1.0 / 16)
                        q4 = QK[n % 2][:, l0:512].rearrange("p (n s m) -> p n s m", s=2, m=m)
                        for half, src in ((hk, GK), (hq, GQ)):
                            k2 = tt(V, q4[:, :, half, :], e4[:, :, half, :],
                                    src[:, hp, l0:512].rearrange("p (n s m) -> p n s m", s=2, m=m)[:, :, half, :],
                                    ALU.mult, k, kq[n % 2], loose=half == hq)
                        ke[n % 2] = k2
                        return k2

                    kq = [kKD, kKD]
                    kf = factors(0)
                    yield
                    for n, (m, d) in enumerate(steps):
                        kn = factors(n + 1) if n + 1 < len(steps) else None
                        yield [kf]
                        qk = QK[n % 2]
                        bp = [GP.take(), GP.take()]
                        k2 = [None, None]
                        for t in tiles:
                            for p in range(2):
                                a = qk[64 * p:64 * p + 64, 128 * t:128 * t + 128]
                                k2[p] = mm(bp[p].t[:, 128 * t:128 * t + 128], a, a, t == tiles[0], True, kf,
                                           bp[p].free, inc=t == 3)
                        for p in range(2):
                            bp[p].free = [pred(att[:, tiles[0]:4, p, :],
                                               mask(m, d).unsqueeze(1).to_broadcast([128, nt, 128]),
                                               r3(bp[p].t[:, l0:512], nt), k2[p])]
                        kq[n % 2] = k2
                        kf = kn
                        yield
                    katt = (V.sem, V.n)
                    ko = []
                    for p in range(2):
                        h = 2 * hp + p
                        while f"gg{h}" not in done:
                            yield "blocked"
                        b = GP.take()
                        first = True
                        for t in tiles:
                            mm(b.t[:, 128 * t:128 * t + 128], GV[:, t, 128 * h:128 * h + 128], att[:, t, p, :],
                               first, False, katt, b.free)
                            first = False
                            for n in (2 * t, 2 * t + 1):
                                for d in range(2):
                                    if (d == 0 and n == 0) or (d == 1 and n == 3):
                                        continue
                                    k = mm(b.t[:, 64 * n:64 * n + 64], ST[64 * p:64 * p + 64, d, n, :],
                                           QB[d][64 * p:64 * p + 64, 64 * n:64 * n + 64], False, True, kST, kQB,
                                           inc=True)
                        O, Q2 = (x[:, l0:512] for x in (QK if p else EE))
                        k = act(O, b.t[:, l0:512], ACT.Copy, k, (V.sem, V.n))
                        b.free = [k]
                        ko.append(tt(V, Q2, O, O, ALU.mult, k))
                        yield []
                    for p in range(2):
                        h = 2 * hp + p
                        O, Q2 = (x[:, l0:512] for x in (QK if p else EE))
                        k = ko[p]
                        yield [k]
                        b = GP.take()
                        k = mm(b.t[:, l0:512], o128, Q2, True, True, k, b.free, inc=True)
                        b.free = [rstd_big(Q2, b.t[:, l0:512], k)]
                        k = stt(V, O, O, par[:, PA_ON:PA_ON + 1], Q2, ALU.mult, ALU.mult, b.free, k_par)
                        y = GG[:, h, l0:512]
                        done["yg"] = stt(V, y, O, 0.5, y, ALU.mult, ALU.mult, done[f"gg{h}"])
                        yield
                    done["glalast"] = [(V.sem, V.n), (A.sem, A.n), (P.sem, P.n)]

            def scr(n):
                return al(n)

            weave(plan, P, SLACK[l], *((gla(scr), attention(scr)) if GFIRST[l] else (attention(scr), gla(scr))), dense())
            allk = [(V.sem, V.n), (A.sem, A.n), (P.sem, P.n), (G.sem, G.n)]
            if l == 0:
                k_scs[:] = [allk, allk]
                k_sc = allk
            top[0] = s0

            n = 512 - l0
            DP2 = Pool(PS)
            SIG = [al(512) for _ in range(2)]
            TM = al(512)
            it = 0
            ys = {"a": (AG, done["ya"]), "g": (GG, done["yg"]), "s": (SG, done["ys"])}
            free_sig = [None, None]
            ktm = None
            for j in range(2):
                for bi, br in enumerate("ags"):
                    if (br, j) not in EARLY[l]:
                        w, kw = use(f"a{l}m{br}{j}")
                        w = rows_of(w, 8)
                    wb, kwb = use(f"a{l}b{br}{j}")
                    wb = rows_of(wb, 4)
                    Y, ky = ys[br]
                    for c in range(4):
                        if (br, j) in EARLY[l]:
                            sg, k = early[(br, j, c)]
                        else:
                            b = DP2.take()
                            kd = feat(b, w, 8, 128 * c, 128, hT, l0, 512, 8, [kw, b.free])
                            sg = SIG[it % 2][:, 0:n]
                            k = act(sg, b.t[:, 0:n], ACT.Tanh, kd, free_sig[it % 2], allk, scale=0.5)
                            b.free = [k]
                        b = DP2.take()
                        k2 = feat(b, wb, 4, 128 * c, 128, Y, l0, 512, 4, [kwb, ky, b.free])
                        m = mT[:, 4 * j + c, l0:512]
                        if bi == 0:
                            k3 = stt(V, m, sg, 1.0, b.t[:, 0:n], ALU.add, ALU.mult, k, k2, allk)
                        else:
                            k3 = stt(V, TM[:, 0:n], sg, 1.0, b.t[:, 0:n], ALU.add, ALU.mult, k, k2, ktm, allk)
                            ktm = tt(G, m, m, TM[:, 0:n], ALU.add, k3)
                        b.free = [k3]
                        if (br, j) not in EARLY[l]:
                            free_sig[it % 2] = k3
                            it += 1
                    if (br, j) not in EARLY[l]:
                        release(f"a{l}m{br}{j}", kd)
                    release(f"a{l}b{br}{j}", k2)
            km = [(V.sem, V.n), (G.sem, G.n)]

            k_out = [(V.sem, V.n), (G.sem, G.n), (P.sem, P.n), (A.sem, A.n)]
            k_tiles = {}
            if l == 1:
                k_next[0] = dma(arena[:, base + 2048:base + 2048 + PB_W], pb[0], km)

            top[0] = s0 + 512 * 3
            zz = al(1024)
            rp = al(2048)
            gb = al(2048)
            st6 = al(16)
            if l == 0:
                XR = [al(1024) for _ in range(2)]
                assert top[0] <= 53200 - 2048
                k_xr = [dma(XR[t], xin[:, 1024 * t:1024 * t + 1024], km) for t in range(2)]
            k_rp = dma(rp, rpost[l].partition_broadcast(128), km)
            for s in range(2):
                for hf in range(2):
                    if l == 1 and s == 0:
                        continue
                    b = DP2.take()
                    c = 1 - s
                    for i in range(4):
                        k = mm(b.t[:, 128 * i:128 * i + 128],
                               sc3[:, 16 + 4 * hf + i, c:c + 1].to_broadcast([128, 128]), ident, i == 0, True, k_sc,
                               b.free, inc=i == 3)
                    b.free = [act(gb[:, 1024 * s + 512 * hf:1024 * s + 512 * hf + 512], b.t, ACT.Copy, k, km,
                                  scale=0.5)]
            k_gb = (A.sem, A.n)
            w0, kw0 = use(f"a{l}o0")
            w1, kw1 = use(f"a{l}o1")
            ws = [(rows_of(w0, 8), kw0), (rows_of(w1, 8), kw1)]
            for t in tiles:
                s = t // 2
                for hf in range(2):
                    b = DP2.take()
                    w, kw = ws[hf]
                    k = token(b, w, 0, 512, mT, 128 * t, [kw, km, b.free])
                    cs_ = slice(512 * hf, 512 * hf + 512)
                    k2 = tt(V, zz[:, cs_], b.t, gb[:, 1024 * s + 512 * hf:1024 * s + 512 * hf + 512], ALU.mult, k, k_gb)
                    b.free = [k2]
                    xr = (XR[t % 2][:, 512 * hf:512 * hf + 512] if l == 0
                          else X[:, 1024 * (t % 2) + 512 * hf:1024 * (t % 2) + 512 * hf + 512])
                    stt(V, zz[:, cs_], xr, ALPHA, zz[:, cs_], ALU.mult, ALU.add, k_xr[t] if l == 0 else None)
                    V.put(lambda e, o=st6[:, 6 * hf:6 * hf + 6], i=zz[:, cs_]: e.bn_stats(o, i), [])
                if l == 0 and t < 2:
                    k_xr.append(dma(XR[t], xin[:, 1024 * t + 2048:1024 * t + 3072], (V.sem, V.n)))
                k = V.put(lambda e: e.bn_aggr(st6[:, 12:14], r3(st6[:, 0:12], 2)), [])
                kr = rstd_small(st6[:, 14:15], st6[:, 13:14], k)
                o = X[:, 1024 * (t % 2):1024 * (t % 2) + 1024] if t >= 2 else CX[:, 1024 * t:1024 * t + 1024]
                stt(V, zz, zz, st6[:, 12:13], rp[:, 0:1024], ALU.subtract, ALU.mult, k_rp)
                k_tiles[t] = stt(V, o, zz, st6[:, 14:15], rp[:, 1024:2048], ALU.mult, ALU.add, k_rp, kr)
                lastp = (P.sem, P.n)
            release(f"a{l}o0", lastp)
            release(f"a{l}o1", lastp)
            return [(V.sem, V.n), (G.sem, G.n), (P.sem, P.n), (A.sem, A.n)], k_out, [k_tiles[t] for t in tiles]

        CX = arena[:, 53200 - 2048:53200]

        def layer_b(l, k_x, k_pre, k_tile):
            top[0] = base
            hT = r3(al(2048), 8)
            par = al(PB_W)
            QPf = al(12 * 260)
            QP = r3(QPf, 12)
            CV = r3(al(3072), 12)
            ZA = r3(al(1024), 4)
            CU = r3(al(4 * 286), 4)
            CA = r3(al(1024), 4)
            ZB = r3(al(1024), 4)
            TH = al(512)
            gh = al(16)
            SG0 = r3(al(1024), 4)
            s0 = top[0]
            k_par = k_next[0]
            SIG = {}
            for c in range(4):
                SIG[(0, 0, c)], SIG[(0, 1, c)], SIG[(1, 0, c)] = SG0[:, c, :], CV[:, 4 + c, :], CV[:, 8 + c, :]
                SIG[(1, 1, c)] = CU[:, c, 0:256]
            DP = Pool(PS[0:2])
            SP_ = Pool(PS[2:5])
            HP = Pool(PS[5:8])
            XS = CX
            nw = par[:, PB_NW:PB_NW + 8]
            k_hk = []
            for t in range(2):
                xs, x = XS[:, 1024 * t:1024 * t + 1024], X[:, 1024 * t:1024 * t + 1024]
                k = act(xs, x, ACT.Square, k_tile[t], k_pre, acc=st2[:, t:t + 1])
                k = ts(G, st2[:, 2 + t:3 + t], st2[:, t:t + 1], 1.0 / 1024, EPS, ALU.mult, ALU.add, k, k_pre)
                kr = tt(G, st2[:, 2 + t:3 + t], st2[:, 2 + t:3 + t], mhalf, ALU.pow, k)
                ka = act(xs[:, 0:512], x[:, 0:512], ACT.Copy, kr, scale=st2[:, 2 + t:3 + t])
                if t == 0:
                    kb = act(xs[:, 512:1024], x[:, 512:1024], ACT.Copy, kr, scale=st2[:, 2 + t:3 + t])
                else:
                    kb = ts(V, xs[:, 512:1024], x[:, 512:1024], st2[:, 3:4], None, ALU.mult, None, kr, ka)
                for q in range(2):
                    b = SP_.take()
                    for i in range(4):
                        k2 = tr(b.t[:, 128 * i:128 * i + 128], xs[:, 512 * q + 128 * i:512 * q + 128 * i + 128], ident,
                                kb if q else ka, b.free, inc=i == 3)
                    if t == 0:
                        for i in range(4):
                            c = 4 * q + i
                            k3 = act(hT[:, c, 0:128], b.t[:, 128 * i:128 * i + 128], ACT.Copy, k2, k_par, k_pre,
                                     scale=nw[:, c:c + 1])
                    else:
                        k3 = tt(V, hT[:, 4 * q:4 * q + 4, 128:256], r3(b.t, 4),
                                nw[:, 4 * q:4 * q + 4].unsqueeze(2).to_broadcast([128, 4, 128]), ALU.mult, k2, k_par)
                    b.free = [k3]
                    if t == 0:
                        k_h0 = k3
                    else:
                        k_hk += [[k_h0, k3]] * 4
            kgh = ts(G, gh, par[:, PB_GB:PB_GB + 16], 0.5, None, ALU.mult, None, k_par, k_x)
            ms(G, QP[:, :, 0:2], 0.0, k_x)
            ms(G, QP[:, :, 258:260], 0.0)
            ms(G, CU[:, :, 0:15], 0.0)
            k_pad = ms(G, CU[:, :, 271:286], 0.0)
            top[0] = s0
            done = {}

            def dense():
                w, kw = use(f"b{l}ab")
                w = rows_of(w, 8)
                b = DP.take()
                k = feat(b, w, 8, 0, 100, hT, 0, 256, 8, [kw, b.free], m=100, kh=k_hk)
                b.free = [act(TH[0:100, 0:256], b.t[0:100, 0:256], ACT.Copy, k)]
                done["ab"] = b.free
                release(f"b{l}ab", k)
                yield
                for j in range(3):
                    w, kw = use(f"b{l}q{j}")
                    w = rows_of(w, 8)
                    for c in range(4):
                        b = DP.take()
                        k = feat(b, w, 8, 128 * c, 128, hT, 0, 256, 8, [kw, b.free], kh=k_hk)
                        b.free = [act(QP[:, 4 * j + c, 2:258], b.t[:, 0:256], ACT.Copy, k)]
                        done[f"q{4 * j + c}"] = b.free
                        yield
                    release(f"b{l}q{j}", k)
                for name in ("za", "cv", "cg", "zb"):
                    w, kw = use(f"b{l}{name}")
                    w = rows_of(w, 8)
                    for c in range(4):
                        b = DP.take()
                        k = feat(b, w, 8, 128 * c, 128, hT, 0, 256, 8, [kw, b.free])
                        ps = b.t[:, 0:256]
                        if name == "cv":
                            b.free = [act(CU[:, c, 15:271], ps, ACT.Copy, k, (G.sem, G.n))]
                        else:
                            dst = {"za": ZA, "zb": ZB, "cg": CA}[name][:, c, :]
                            k1 = act(TH[:, 256:512], ps, ACT.Tanh, k, done.get("th"), scale=0.5)
                            if name == "cg":
                                k2 = stt(V, CU[:, c, 15:271], TH[:, 256:512], 1.0, CU[:, c, 15:271], ALU.add,
                                         ALU.mult, k1)
                                b.free = [k1]
                                done[f"cu{c}"] = k2
                            else:
                                k2 = stt(V, dst, TH[:, 256:512], 1.0, ps, ALU.add, ALU.mult, k1)
                                b.free = [k2]
                            done["th"] = k2
                            done[f"{name}{c}"] = k2
                        yield
                    release(f"b{l}{name}", k)
                for j in range(2):
                    for bi in range(2):
                        while (j, bi) != (0, 0) and "cv" not in done:
                            yield "blocked"
                        while (j, bi) == (1, 1) and "yb" not in done:
                            yield "blocked"
                        w, kw = use(f"b{l}m{bi}{j}")
                        w = rows_of(w, 8)
                        for c in range(4):
                            b = DP.take()
                            k = feat(b, w, 8, 128 * c, 128, hT, 0, 256, 8, [kw, b.free])
                            q = 8 * bi + 4 * j + c
                            done[f"sig{q}"] = act(SIG[(j, bi, c)], b.t[:, 0:256], ACT.Tanh, k, kgh, done["cv"] if (j, bi) != (0, 0) else None,
                                                  done.get("yb") if (j, bi) == (1, 1) else None, scale=0.5,
                                                  bias=gh[:, q:q + 1])
                            b.free = [done[f"sig{q}"]]
                            yield
                        release(f"b{l}m{bi}{j}", k)

            def confconv(scr):
                UM = scr(256)
                UQ = scr(256)
                fw = par[:, PB_FW:PB_FW + 124]
                for pair in ((0, 1), (2, 3)):
                    for c in pair:
                        while f"cu{c}" not in done:
                            yield "blocked"
                    kt_ = {}
                    for c in pair:
                        kt_[c] = ts(V, CA[:, c, :], CU[:, c, 0:256], fw[:, 31 * c:31 * c + 1], None, ALU.mult, None,
                                    done[f"cu{c}"], k_par)
                    for i in range(1, 31):
                        for c in pair:
                            kt_[c] = stt(V, CA[:, c, :], CU[:, c, i:i + 256], fw[:, 31 * c + i:31 * c + i + 1],
                                         CA[:, c, :], ALU.mult, ALU.add, kt_[c], loose=True)
                        if i % 2 == 0:
                            yield
                    for c in pair:
                        ts(V, CA[:, c, :], CA[:, c, :], 0.5, par[:, PB_FB + c:PB_FB + c + 1], ALU.mult, ALU.add)
                    yield
                kca = [(V.sem, V.n), (G.sem, G.n)]
                b = DP.take()
                for c in range(4):
                    k = mm(b.t[:, 0:256], o512, CA[:, c, :], c == 0, c == 3, kca, b.free, inc=c == 3)
                ub = UM.unsqueeze(1).to_broadcast([128, 4, 256])
                k = act(UM, b.t[:, 0:256], ACT.Copy, k)
                b.free = [k]
                k = tt(V, CA[:, :, :], CA[:, :, :], ub, ALU.subtract, k, kca)
                yield
                b = DP.take()
                for c in range(4):
                    k1 = act(UQ, CA[:, c, :], ACT.Square, k, (P.sem, P.n))
                    k2 = mm(b.t[:, 0:256], o512, UQ, c == 0, c == 3, k1, b.free, inc=True)
                b.free = [rstd_big(UM, b.t[:, 0:256], k2)]
                k = tt(V, CA[:, :, :], CA[:, :, :], ub, ALU.mult, b.free)
                for c in range(4):
                    k = ts(V, CA[:, c, :], CA[:, c, :], par[:, PB_LW + c:PB_LW + c + 1],
                           par[:, PB_LB + c:PB_LB + c + 1], ALU.mult, ALU.add)
                k1 = act(CU[:, :, 0:256], CA[:, :, :], ACT.Tanh, k, scale=0.5)
                while "zb3" not in done:
                    yield "blocked"
                stt(V, CA[:, :, :], CU[:, :, 0:256], 1.0, CA[:, :, :], ALU.add, ALU.mult, k1)
                done["yb"] = stt(V, CA[:, :, :], CA[:, :, :], 0.25, ZB[:, :, :], ALU.mult, ALU.mult, done["zb3"])
                yield

            def delta(scr):
                cw = par[:, PB_CW:PB_CW + 60]
                K3 = r3(scr(1024), 2)
                V3 = r3(scr(1024), 2)
                EG = r3(scr(2048), 8)
                DT = r3(scr(2048), 16)
                AT = r3(scr(2048), 16)
                NL = r3(scr(2048), 16)
                XM = r3(scr(2048), 16)
                XT = r3(scr(2048), 16)
                Y = r3(scr(2048), 16)
                QD = r3(QPf[:, 0:2048], 8)
                KG = NL
                KC = Y
                KD = DT
                GB = scr(256)
                GB2 = scr(256)
                GC = r3(scr(200), 2)
                BC = scr(64)
                SS = r3(QPf[:, 2048:3072], 8)
                VW = [scr(512) for _ in range(2)]
                R = scr(512)
                while "ab" not in done:
                    yield "blocked"
                k = ms(V, GB[0:100, :], 0.0)
                act(GB2[0:36, :], TH[0:36, 0:256], ACT.Identity, done["ab"], k_par, k,
                    bias=par[0:36, PB_DT:PB_DT + 1])
                act(TH[0:36, 0:256], GB2[0:36, :], ACT.Abs)
                act(TH[0:36, 0:256], TH[0:36, 0:256], ACT.Exp, scale=-1.0)
                act(TH[0:36, 0:256], TH[0:36, 0:256], ACT.Ln, bias=one[0:36, :])
                k = act(BC[0:36, 0:1], par[0:36, PB_AL:PB_AL + 1], ACT.Exp)
                stt(V, GB2[0:36, :], GB2[0:36, :], 0.0, TH[0:36, 0:256], ALU.max, ALU.add, k)
                ts(V, BC[0:36, 1:2], BC[0:36, 0:1], -1.0, None, ALU.mult, None)
                ts(V, GB2[0:36, :], GB2[0:36, :], BC[0:36, 1:2], None, ALU.mult, None)
                SCN = cst[:, C_SCAN:C_SCAN + 256]
                V.put(lambda e: e.tensor_tensor_scan(GB[0:32, :], SCN[0:32, :], GB2[0:32, :], 0.0, ALU.mult, ALU.add), [])
                V.put(lambda e: e.tensor_tensor_scan(GB[32:36, ::-1], SCN[32:36, :], GB2[32:36, ::-1], 0.0, ALU.mult,
                                                     ALU.add), [])
                k = act(GB[64:100, :], TH[64:100, 0:256], ACT.Tanh, (V.sem, V.n), scale=0.5)
                k = ts(V, GB[64:100, :], GB[64:100, :], 0.5, 0.5, ALU.mult, ALU.add, k)
                yield
                b = SP_.take()
                for t in range(2):
                    k2 = tr(b.t[:, 128 * t:128 * t + 100], GB[0:100, 128 * t:128 * t + 128], ident[0:100, 0:100], k,
                            b.free, inc=t == 1)
                kgc = cp(V, GC, b.t[:, 0:256].rearrange("p (a b) -> p a b", a=2)[:, :, 0:100], k2)
                b.free = [kgc]
                for d in range(2):
                    for t in range(2):
                        o = 8 * d + 4 * t
                        cp(V, BC[:, o:o + 4], GC[:, t, 64 + 32 * d:68 + 32 * d])
                        ts(V, BC[:, 16 + o:20 + o], GC[:, t, 64 + 32 * d:68 + 32 * d], -1.0, None, ALU.mult, None)
                        kbc = act(BC[:, 32 + o:36 + o], GC[:, t, 32 * d:32 * d + 4], ACT.Exp, kgc, (V.sem, V.n))
                yield
                for d in range(2):
                    for hq in range(2):
                        b = SP_.take()
                        for i in range(2):
                            h = 2 * hq + i
                            rr = 32 * d + h
                            k = mm(b.t[:, 256 * i:256 * i + 256], ident[0:36, rr:rr + 1].to_broadcast([36, 128]),
                                   GB[0:36, :], i == 0, True, b.free, k2, inc=i == 1)
                        for i in range(2):
                            h = 2 * hq + i
                            for t in range(2):
                                kv_ = ts(V, DT[:, 8 * d + 4 * t + h, :], b.t[:, 256 * i + 128 * t:256 * i + 128 * t + 128],
                                         GC[:, t, 32 * d + h:32 * d + h + 1], 0.0, ALU.subtract, ALU.min, k,
                                         loose=i + t > 0)
                        b.free = [act(EG[:, 4 * d + 2 * hq:4 * d + 2 * hq + 2, :], r3(b.t, 2), ACT.Exp, kv_)]
                    yield
                for d in range(2):
                    k = act(DT[:, 8 * d:8 * d + 8, :], DT[:, 8 * d:8 * d + 8, :], ACT.Exp)
                    inc_ = cst[:, C_INC + 128 * d:C_INC + 128 * d + 128].unsqueeze(1).to_broadcast([128, 8, 128])
                    tt(G, AT[:, 8 * d:8 * d + 8, :], DT[:, 8 * d:8 * d + 8, :], inc_, ALU.mult, k)
                    for half in range(2):
                        rs = slice(64 * half, 64 * half + 64)
                        col = 64 * half + (0 if d else 63)
                        cp(V, BC[rs, 48 + 8 * d:56 + 8 * d].unsqueeze(2), DT[rs, 8 * d:8 * d + 8, col:col + 1], k)
                    yield
                kdt = (V.sem, V.n)
                kat = (G.sem, G.n)
                for pair in range(6):
                    cs2 = (2 * pair, 2 * pair + 1)
                    for c in cs2:
                        while f"q{c}" not in done:
                            yield "blocked"
                    kt_ = {}
                    for i in range(5):
                        for c in cs2:
                            s = cw[:, 5 * c + i:5 * c + i + 1]
                            if i == 0:
                                kt_[c] = ts(V, CV[:, c, :], QP[:, c, 0:256], s, None, ALU.mult, None, done[f"q{c}"],
                                            k_par, k_pad, loose=c % 2 == 1)
                            else:
                                kt_[c] = stt(V, CV[:, c, :], QP[:, c, i:i + 256], s, CV[:, c, :], ALU.mult, ALU.add,
                                             kt_[c], loose=True)
                    k1 = [act(QP[:, c, 0:256], CV[:, c, :], ACT.Tanh, kt_[c], scale=0.5) for c in cs2]
                    for n, c in enumerate(cs2):
                        stt(V, CV[:, c, :], QP[:, c, 0:256], 1.0, CV[:, c, :], ALU.add, ALU.mult, k1[n],
                            loose=n == 1)
                    yield "ahead" if pair < 5 else None
                kcv = [(V.sem, V.n), (G.sem, G.n)]

                def token_major(src, dst, pool, kw):
                    for t in range(2):
                        b = pool.take()
                        for h in range(4):
                            k = tr(b.t[:, 128 * h:128 * h + 128], CV[:, src + h, 128 * t:128 * t + 128], ident, kw,
                                   b.free, inc=h == 3)
                        b.free = [act(dst[:, t, :], b.t, ACT.Copy, k)]
                        yield

                NB = SP_.banks + HP.banks[0:1]
                RN = XM.rearrange("p a b -> p (a b)")
                SQ = XT.rearrange("p a b -> p (a b)")
                kvh = ts(V, CV[:, 8:12, :], CV[:, 8:12, :], 0.5, None, ALU.mult, None)
                ks = [act(SQ[:, 1024 * c:1024 * c + 1024], CV[:, 4 * c:4 * c + 4, :], ACT.Square, kcv)
                      for c in range(2)]
                yield
                for c in range(8):
                    k = ks[c // 4]
                    b = NB[c // 2]
                    k = mm(b.t[:, 256 * (c % 2):256 * (c % 2) + 256], o128, SQ[:, 256 * c:256 * c + 256], c % 2 == 0,
                           True, k, b.free, inc=True)
                yield
                for c in range(4):
                    NB[c].free = [act(RN[:, 512 * c:512 * c + 512], NB[c].t, ACT.Ln, k, bias=eps, scale=32.0)]
                for c in (1, 0):
                    k = act(RN[:, 1024 * c:1024 * c + 1024], RN[:, 1024 * c:1024 * c + 1024], ACT.Exp, scale=-0.5)
                    f = 128.0 ** -0.5 / 2 if c == 0 else 0.5
                    k = stt(V, CV[:, 4 * c:4 * c + 4, :], CV[:, 4 * c:4 * c + 4, :], f,
                            RN[:, 1024 * c:1024 * c + 1024].rearrange("p (a b) -> p a b", a=4), ALU.mult, ALU.mult, k)
                    if c == 1:
                        kcv = k
                    else:
                        kqn = k
                for _ in token_major(8, V3, Pool(HP.banks[1:3]), kvh):
                    yield
                drain(token_major(4, K3, SP_, kcv))
                kkv = (A.sem, A.n)
                for t in range(2):
                    b = SP_.take()
                    for h in range(4):
                        kt = CV[:, 4 + h, 128 * t:128 * t + 128]
                        k = mm(b.t[:, 128 * h:128 * h + 128], kt, kt, h == 0, True, kcv, b.free, inc=h == 3)
                    for d in range(2):
                        for h in range(4):
                            o = 8 * d + 4 * t + h
                            k3 = stt(V, NL[:, o, :], b.t[:, 128 * h:128 * h + 128], BC[:, 16 + o:17 + o], DT[:, o, :],
                                     ALU.mult, ALU.mult, k, kdt, loose=d + h > 0)
                    b.free = [k3]
                    b = SP_.take()
                    for h in range(4):
                        k = mm(b.t[:, 128 * h:128 * h + 128], CV[:, 4 + h, 128 * t:128 * t + 128],
                               CV[:, h, 128 * t:128 * t + 128], h == 0, True, kqn, b.free, inc=h == 3)
                    for d in range(2):
                        o = 8 * d + 4 * t
                        b.free = [tt(V, AT[:, o:o + 4, :], r3(b.t, 4), AT[:, o:o + 4, :], ALU.mult, k, kat)]
                    yield
                for d in range(2):
                    kqd = tt(V, QD[:, 4 * d:4 * d + 4, :], CV[:, 0:4, :], EG[:, 4 * d:4 * d + 4, :], ALU.mult,
                             (A.sem, A.n))
                done["cv"] = [kqd, k]
                knl = (V.sem, V.n)
                for d in range(2):
                    for t in range(2):
                        for h in range(4):
                            o = 8 * d + 4 * t + h
                            kkd = ts(G, KD[:, o, :], K3[:, t, 128 * h:128 * h + 128], BC[:, 48 + o:49 + o], None,
                                     ALU.mult, None, knl, kdt, kkv, loose=t + h > 0)
                WP = Pool(SP_.banks + HP.banks)
                idb = ident.unsqueeze(1).to_broadcast([128, 16, 128])
                kx = [act(XM[:, :, :], idb, ACT.Copy, kcv), cp(V, XT[:, :, :], idb)]
                kxx = [kx] * 4
                ky = [None] * 4
                for m in MS:
                    for q in range(4):
                        yield [kxx[q]]
                        d = q // 2
                        g = slice(4 * q, 4 * q + 4)
                        mx = mask(m, 1 - d).unsqueeze(1).to_broadcast([128, 4, 128])
                        mt = mask(m, d).unsqueeze(1).to_broadcast([128, 4, 128])
                        b = WP.take()
                        for i in range(4):
                            o = 4 * q + i
                            k = mm(b.t[:, 128 * i:128 * i + 128], NL[:, o, :], XM[:, o, :], i == 0, True, kxx[q],
                                   b.free, inc=i == 3)
                        if m == 32:
                            for i in range(4):
                                o = 4 * q + i
                                t, h = (o // 4) % 2, o % 4
                                kg = ts(V, KG[:, o, :], K3[:, t, 128 * h:128 * h + 128], BC[:, 32 + o:33 + o], None,
                                        ALU.mult, None, k, kbc, kkv, loose=i > 0)
                        if m == 1:
                            pred(XM[:, g, :], mx, r3(b.t, 4), k)
                            b.free = [(V.sem, V.n)]
                            kxx[q] = pred(XT[:, g, :], mt, NL[:, g, :])
                            continue
                        ky[q] = act(Y[:, g, :], r3(b.t, 4), ACT.Copy, k)
                        b.free = [ky[q]]
                    for q in range(4):
                        if m == 1:
                            break
                        yield [ky[q]]
                        d = q // 2
                        g = slice(4 * q, 4 * q + 4)
                        mx = mask(m, 1 - d).unsqueeze(1).to_broadcast([128, 4, 128])
                        mt = mask(m, d).unsqueeze(1).to_broadcast([128, 4, 128])
                        if m < 32:
                            b = WP.take()
                            for i in range(4):
                                o = 4 * q + i
                                k2 = mm(b.t[:, 128 * i:128 * i + 128], XT[:, o, :], Y[:, o, :], i == 0, True, ky[q],
                                        b.free, inc=i == 3)
                            kb1 = (b, k2)
                        b = WP.take()
                        for i in range(4):
                            o = 4 * q + i
                            k2 = mm(b.t[:, 128 * i:128 * i + 128], Y[:, o, :], XT[:, o, :], i == 0, True, ky[q], b.free,
                                    inc=i == 3)
                        if m < 32:
                            kb1[0].free = [pred(XM[:, g, :], mx, r3(kb1[0].t, 4), k2)]
                        b.free = [pred(XT[:, g, :], mt, r3(b.t, 4), k2)]
                        kxx[q] = b.free
                kp = [(P.sem, P.n)]
                kxt = [(V.sem, V.n)]
                kkg = [kkd, kqd]
                for q in range(4):
                    yield [kg, kxx[q]]
                    b = WP.take()
                    for i in range(4):
                        o = 4 * q + i
                        k = mm(b.t[:, 128 * i:128 * i + 128], KG[:, o, :], XT[:, o, :], i == 0, True, kg, kxx[q],
                               b.free, inc=i == 3)
                    b.free = [act(KC[:, 4 * q:4 * q + 4, :], r3(b.t, 4), ACT.Copy, k, kp, scale=-1.0)]
                kkc = b.free
                OB = [HP.banks[0], HP.banks[1]]
                ofirst = [True, True]
                kss = [None, None]
                kvw = [None, None]
                UB = [SP_.banks[0], SP_.banks[1]]
                VB = [SP_.banks[2], HP.banks[2]]
                for i in range(4):
                    kv2 = [None, None]
                    for d in range(2):
                        yield [kss[d], kkc, kxt]
                        n = 3 - i if d else i
                        t, r0 = n // 2, 64 * (n % 2)
                        b = VB[d]
                        for h in range(4):
                            o = 8 * d + 4 * t + h
                            k = mm(b.t[r0:r0 + 64, 128 * h:128 * h + 128], XT[r0:r0 + 64, o, r0:r0 + 64],
                                   V3[r0:r0 + 64, t, 128 * h:128 * h + 128], h == 0, i == 0, kxt, kkv, b.free, kkc,
                                   inc=True)
                            if i:
                                k = mm(b.t[r0:r0 + 64, 128 * h:128 * h + 128], KC[:, o, r0:r0 + 64],
                                       SS[:, 4 * d + h, :], False, True, kss[d], kkc, inc=True)
                        o = 8 * d + 4 * t
                        vw = r3(VW[d], 4)
                        kv2[d] = tt(V, vw[r0:r0 + 64], r3(b.t, 4)[r0:r0 + 64],
                                    BC[r0:r0 + 64, o:o + 4].unsqueeze(2).to_broadcast([64, 4, 128]), ALU.mult, k,
                                    kvw[d])
                        b.free = [kv2[d]]
                    for d in range(2):
                        yield [kv2[d]]
                        n = 3 - i if d else i
                        t, r0 = n // 2, 64 * (n % 2)
                        vw = r3(VW[d], 4)
                        if i < 3:
                            b = UB[d]
                            for h in range(4):
                                o = 8 * d + 4 * t + h
                                k = mm(b.t[:, 128 * h:128 * h + 128], KD[r0:r0 + 64, o, :], vw[r0:r0 + 64, h, :],
                                       h == 0, True, kv2[d], b.free, kkg, inc=h == 3)
                        for h in range(4):
                            o = 8 * d + 4 * t + h
                            dst = OB[t].t[:, 128 * h + r0:128 * h + r0 + 64]
                            if i:
                                k1 = mm(dst, SS[:, 4 * d + h, :], QD[:, 4 * d + h, 64 * n:64 * n + 64], ofirst[t], True,
                                        kss[d], kkg, OB[t].free, inc=True)
                                ofirst[t] = False
                            k1 = mm(dst, vw[r0:r0 + 64, h, :], AT[r0:r0 + 64, o, r0:r0 + 64], ofirst[t], True,
                                    kv2[d], OB[t].free, inc=True)
                            ofirst[t] = False
                        kvw[d] = k1
                        if i < 3:
                            e = 64 * n + (0 if d else 63)
                            for h in range(4):
                                s = SS[:, 4 * d + h, :]
                                u = b.t[:, 128 * h:128 * h + 128]
                                if i == 0:
                                    k2 = cp(V, s, u, k)
                                else:
                                    k2 = stt(V, s, s, EG[:, 4 * d + h, e:e + 1], u, ALU.mult, ALU.add, k, k1,
                                             loose=h > 0)
                            b.free = [k2]
                            kss[d] = k2
                done["states"] = (OB, k1, VW, [R, XM.rearrange("p a b -> p (a b)")[:, 0:512]])

            def heads():
                OB, k1, VW, R = done["states"]
                rr = []
                for t in range(2):
                    k = act(R[t], OB[t].t, ACT.Copy, k1, (V.sem, V.n))
                    OB[t].free = [k]
                    rr.append(tt(V, VW[t], R[t], R[t], ALU.mult, k, k1))
                yield
                for t in range(2):
                    b = SP_.take()
                    k = mm(b.t, o128, VW[t], True, True, rr[t], b.free, inc=True)
                    b.free = [rstd_big(VW[t], b.t, k)]
                    stt(V, R[t], R[t], par[:, PB_DN:PB_DN + 1], VW[t], ALU.mult, ALU.mult, b.free)
                    z = ZA[:, :, 128 * t:128 * t + 128]
                    done["yd"] = stt(V, z, r3(R[t], 4), 0.5, z, ALU.mult, ALU.mult, done["za3"])
                yield

            TM, mT = arena[:, s0:s0 + 256], r3(arena[:, s0 + 256:s0 + 2304], 8)
            ktm = [None]

            def merge(bi, Yt, name, pool, kfree):
                for j in range(2):
                    wb, kwb = use(f"b{l}b{bi}{j}")
                    wb = rows_of(wb, 4)
                    for c in range(4):
                        sg = SIG[(j, bi, c)]
                        yield [done[name]]
                        b = pool.take()
                        k2 = feat(b, wb, 4, 128 * c, 128, Yt, 0, 256, 4, [kwb, done[name], b.free])
                        m = mT[:, 4 * j + c, :]
                        k = done[f"sig{8 * bi + 4 * j + c}"]
                        if bi == 0:
                            k3 = stt(V, m, sg, 1.0, b.t[:, 0:256], ALU.add, ALU.mult, k, k2, kfree)
                        else:
                            k3 = stt(V, TM, sg, 1.0, b.t[:, 0:256], ALU.add, ALU.mult, k, k2, ktm[0], kfree)
                            ktm[0] = tt(G, m, m, TM, ALU.add, k3)
                        b.free = [k3]
                        yield
                    release(f"b{l}b{bi}{j}", k2)

            def first_branch(scr):
                yield from delta(scr)
                yield from heads()
                while "sig7" not in done:
                    yield "blocked"
                yield from merge(0, ZA, "yd", SP_, [(V.sem, V.n), (A.sem, A.n), (P.sem, P.n), (G.sem, G.n)])

            def scr(n):
                return al(n)

            weave(plan, P, SLACK[2], first_branch(scr), confconv(scr), dense(), idle=(1, V))
            top[0] = s0
            allk = [(V.sem, V.n), (A.sem, A.n), (P.sem, P.n), (G.sem, G.n)]
            top[0] = s0 + 2304
            fr = al(1024)
            zz = al(1024)
            f2 = al(4)
            DP2 = Pool(PS)
            drain(merge(1, CA, "yb", DP2, allk))
            km = [(V.sem, V.n), (G.sem, G.n)]
            k_out = [(V.sem, V.n), (G.sem, G.n), (P.sem, P.n), (A.sem, A.n)]
            k_tiles = []
            if l == 0:
                k_next[0] = dma(par, pb[1], k_out)
            else:
                k_fr = dma(fr, rfin.partition_broadcast(128), km)
            w0, kw0 = use(f"b{l}o0")
            w1, kw1 = use(f"b{l}o1")
            ws = [(rows_of(w0, 8), kw0), (rows_of(w1, 8), kw1)]
            stores = []
            for t in range(2):
                for hf in range(2):
                    b = DP2.take()
                    w, kw = ws[hf]
                    k = token(b, w, 0, 512, mT, 128 * t, [kw, km, b.free])
                    x = X[:, 1024 * t + 512 * hf:1024 * t + 512 * hf + 512]
                    b.free = [stt(V, x, b.t, 0.5, x, ALU.mult, ALU.add, k)]
                k_tiles.append(b.free)
                if l == 1:
                    x = X[:, 1024 * t:1024 * t + 1024]
                    k = act(zz, x, ACT.Square, b.free, (V.sem, V.n), acc=f2[:, 0:1])
                    k = ts(V, f2[:, 1:2], f2[:, 0:1], 1.0 / 1024, None, ALU.mult, None, k)
                    kr = rstd_small(f2[:, 2:3], f2[:, 1:2], k)
                    k = stt(V, x, x, f2[:, 2:3], fr, ALU.mult, ALU.mult, k_fr, kr)
                    stores.append(dma(out[128 * t:128 * t + 128, :], x, k))
            lastp = (P.sem, P.n)
            release(f"b{l}o0", lastp)
            release(f"b{l}o1", lastp)
            if stores:
                S.todo.append((stores, None, False))
            return [(V.sem, V.n), (G.sem, G.n), (P.sem, P.n), (A.sem, A.n)], k_out, k_tiles

        k = layer_a(0, None, None, None)
        k = layer_a(1, *k)
        k = layer_b(0, *k)
        layer_b(1, *k)

        def play(E, eng):
            for need, fn, inc in E.todo:
                for s, v in need:
                    eng.wait_ge(s, v)
                if fn is None:
                    continue
                ins = fn(eng)
                if inc:
                    ins.then_inc(E.sem, 1)

        block = ctx.enter_context(nc.Block())

        @block.sync
        def _(e):
            play(S, e)

        @block.gpsimd
        def _(e):
            play(G, e)

        @block.scalar
        def _(e):
            play(A, e)

        @block.tensor
        def _(e):
            play(P, e)

        @block.vector
        def _(e):
            play(V, e)


def make_consts():
    c = np.zeros((128, C_W), np.float32)
    i = np.arange(128)
    c[:, C_ID:C_ID + 128] = np.eye(128)
    for n, m in enumerate(MS):
        a = i[:, None]
        b = i[None, :]
        mk = (a // (2 * m) == b // (2 * m)) & ((a // m) % 2 == 0) & ((b // m) % 2 == 1)
        c[:, C_MASK + 256 * n:C_MASK + 256 * n + 128] = mk
        c[:, C_MASK + 256 * n + 128:C_MASK + 256 * n + 256] = mk.T
    fr = (np.float32(10000.0) ** (-np.arange(0, 32, 2, dtype=np.float32) / np.float32(32))).astype(np.float32)
    tok = np.arange(256)
    for t in range(2):
        p = tok[128 * t:128 * t + 128]
        ar = ((p // 64).astype(np.float32)[:, None] * fr).astype(np.float32)
        ac = ((p % 64).astype(np.float32)[:, None] * fr).astype(np.float32)
        c[:, C_COS + 64 * t:C_COS + 64 * t + 64] = np.concatenate([np.cos(ar)] * 2 + [np.cos(ac)] * 2, 1)
        c[:, C_SIN + 64 * t:C_SIN + 64 * t + 64] = np.concatenate([-np.sin(ar), np.sin(ar), -np.sin(ac), np.sin(ac)], 1)
    c[:, C_SCAN:C_SCAN + 512] = (np.arange(512) % 64 != 0)
    c[:, C_O128:C_O128 + 128] = 1.0 / 128
    c[:, C_O512:C_O512 + 128] = 1.0 / 512
    same = (i[:, None] // 64) == (i[None, :] // 64)
    c[:, C_INC:C_INC + 128] = same & (i[:, None] <= i[None, :])
    c[:, C_INC + 128:C_INC + 256] = same & (i[:, None] >= i[None, :])
    c[:, C_COL:C_COL + 4] = [EPS, 1.0, 0.0, -0.5]
    for g in range(4):
        c[32 * g:32 * g + 2, C_STK:C_STK + 2] = np.eye(2)
    return c


def lay(w):
    return w.reshape(-1, 128, w.shape[1]).transpose(1, 0, 2).reshape(128, -1)


def cols(v):
    return v.reshape(-1, 128).T


def kernel(**inputs):
    import concourse.bacc as bacc
    from concourse.bass_utils import run_bass_kernel_spmd as run

    I = {k: np.asarray(v) for k, v in inputs.items()}
    perm = np.concatenate([np.arange(64 * h, 64 * h + 64) for h in HEADS])
    pieces = {}
    for l in range(2):
        wi = I["w_in"][l]
        for j in range(6):
            pieces[f"a{l}ada{j}"] = lay(I["w_ada"][l][:, 512 * j:512 * j + 512])
        pieces[f"a{l}qa"] = lay(wi[:, 0:512][:, perm])
        pieces[f"a{l}kv"] = lay(np.concatenate([wi[:, 512:768], wi[:, 2304:2336]], 1))
        for n, o in (("gqk", 1280), ("gv", 1792), ("gg", 2336), ("su", 2848), ("sv", 3360), ("sg", 3872)):
            pieces[f"a{l}{n}"] = lay(wi[:, o:o + 512])
        pieces[f"a{l}ag"] = lay(wi[:, 768:1280][:, perm])
        for j in range(2):
            for n, b, wb in ((0, "a", I["w_br_attn"][l][perm]), (1, "g", I["w_br_gla"][l]), (2, "s", I["w_br_sgu"][l])):
                o = 4384 + 1024 * n + 512 * j
                pieces[f"a{l}m{b}{j}"] = lay(wi[:, o:o + 512])
                pieces[f"a{l}b{b}{j}"] = lay(wb[:, 512 * j:512 * j + 512])
            pieces[f"a{l}o{j}"] = lay(I["w_out"][l][:, 512 * j:512 * j + 512])
        wi = I["w_in_2"][l]
        for j in range(3):
            pieces[f"b{l}q{j}"] = lay(wi[:, 512 * j:512 * j + 512])
        ab = np.zeros((1024, 100), np.float32)
        for n in range(4):
            ab[:, 32 * n:32 * n + 4] = wi[:, 2048 + 4 * n:2052 + 4 * n]
        pieces[f"b{l}ab"] = lay(ab)
        for n, o in (("za", 1536), ("cv", 2064), ("cg", 2576), ("zb", 3088)):
            pieces[f"b{l}{n}"] = lay(wi[:, o:o + 512])
        for j in range(2):
            for b, wb in ((0, I["w_dn_out_2"][l]), (1, I["w_cf_out_2"][l])):
                o = 3600 + 1024 * b + 512 * j
                pieces[f"b{l}m{b}{j}"] = lay(wi[:, o:o + 512])
                pieces[f"b{l}b{b}{j}"] = lay(wb[:, 512 * j:512 * j + 512])
            pieces[f"b{l}o{j}"] = lay(I["w_out_2"][l][:, 512 * j:512 * j + 512])
    wf = np.concatenate([pieces[n].reshape(-1) for n, _ in PLAN])
    assert wf.size == 128 * sum(w for _, w in PLAN)

    pa = np.zeros((2, 128, PA_W), np.float32)
    ra = np.zeros((2, RA_W), np.float32)
    rp = np.zeros((2, 2048), np.float32)
    pb = np.zeros((2, 128, PB_W), np.float32)
    for l in range(2):
        pa[l][:, 0:24] = cols(I["b_ada"][l])
        pa[l][:, PA_AB:PA_AB + 2] = cols(I["gla_ab_f"][l])
        pa[l][:, PA_AB + 2:PA_AB + 4] = cols(I["gla_ab_b"][l])
        pa[l][:, PA_ON] = I["gla_o_norm"][l]
        pa[l][0:16, PA_PM:PA_PM + 256] = I["gla_a2_f"][l]
        pa[l][16:32, PA_PM + 256:PA_PM + 512] = I["gla_a2_b"][l]
        pa[l][96, PA_PM:PA_PM + 512] = I["sgu_b"][l].reshape(-1)
        pa[l][:, PA_SW:PA_SW + 512] = I["sgu_w"][l].transpose(2, 0, 1).reshape(128, 512)
        ra[l][0:512] = np.tile(I["attn_q_norm"][l], 8)
        ra[l][512:640] = np.tile(I["attn_k_norm"][l], 2)
        pa[l][:, PA_LG:PA_LG + 4] = cols(I["sgu_ln_g"][l])
        pa[l][64, PA_PM:PA_PM + 512] = I["sgu_ln_b"][l]
        pa[l][65, PA_PM:PA_PM + 512] = 1.0
        rp[l][0:1024] = I["post_ln_g"][l]
        rp[l][1024:2048] = I["post_ln_b"][l]
        q = pb[l]
        q[:, PB_NW:PB_NW + 8] = cols(I["norm_w_2"][l])
        q[:, PB_CW:PB_CW + 60] = I["qkv_conv_w_2"][l].T.reshape(12, 128, 5).transpose(1, 0, 2).reshape(128, 60)
        q[:, PB_FW:PB_FW + 124] = I["cf_conv_w_2"][l].T.reshape(4, 128, 31).transpose(1, 0, 2).reshape(128, 124)
        q[:, PB_FB:PB_FB + 4] = cols(I["cf_conv_b_2"][l])
        q[:, PB_LW:PB_LW + 4] = cols(I["cf_ln_w_2"][l])
        q[:, PB_LB:PB_LB + 4] = cols(I["cf_ln_b_2"][l])
        q[:, PB_GB:PB_GB + 16] = cols(I["gate_b_2"][l])
        q[:, PB_DN] = I["dn_norm_w_2"][l]
        for d in range(2):
            q[32 * d:32 * d + 4, PB_AL] = I["a_log_2"][l][d]
            q[32 * d:32 * d + 4, PB_DT] = I["dt_bias_2"][l][d]

    both = np.concatenate([I["ctx"][0], I["x"][0]], 0)
    data = {
        "wf": wf, "consts": make_consts(),
        "cT": np.stack([cols(I["c"][0]), cols(I["c_ctx"])], 2).reshape(128, 16),
        "xin": both.reshape(4, 128, 1024).transpose(1, 0, 2).reshape(128, 4096),
        "xinT": both.T.reshape(8, 128, 512).transpose(1, 0, 2).reshape(128, 4096),
        "pa": pa, "ra": ra, "rp": rp, "pb": pb, "rfin": I["final_norm_w_2"],
    }
    nc = bacc.Bacc("TRN2", target_bir_lowering=False, num_devices=1)
    arrays, args = {}, []
    for name, a in data.items():
        a = np.ascontiguousarray(a)
        arrays[f"in_{name}"] = a
        args.append(nc.dram_tensor(f"in_{name}", a.shape, mybir.dt.from_np(a.dtype), kind="ExternalInput").ap())
    o = nc.dram_tensor("out_0", (256, 1024), F, kind="ExternalOutput").ap()
    build_program(nc, *args, o)
    r = run(nc, [arrays], core_ids=[0])
    return r.results[0]["out_0"].reshape(1, 256, 1024)
```
